# Optimizing a Trainium2 kernel written in Bass

```python
import jax, jax.numpy as jnp
from jax import lax
import numpy as np

D_MODEL = 1024
BATCH = 1
SEQ = 512
DEPTH = 1

D_MIX = D_MODEL
D_MLSTM = D_MIX // 2
D_POOL = D_MIX - D_MLSTM
N_MLSTM_HEADS = 4
HEAD_DIM = D_MLSTM // N_MLSTM_HEADS
POOL_WINDOWS = (2, 4, 8, 16)
N_POOL_GROUPS = len(POOL_WINDOWS)
POOL_GROUP_DIM = D_POOL // N_POOL_GROUPS
N_DIRS = 2
N_GATE_COLS = N_DIRS * 2 * N_MLSTM_HEADS
D_IN_PROJ = 4 * D_MLSTM + N_GATE_COLS + D_POOL
D_FF = 4 * D_MODEL
CHUNK = 128
EPS = 1e-6


def _rmsnorm(x, g):
    xf = x.astype(jnp.float32)
    y = xf * lax.rsqrt(jnp.mean(xf * xf, axis=-1, keepdims=True) + EPS)
    return (y * g.astype(jnp.float32)).astype(x.dtype)

def _modulate(h, shift, scale):
    return h * (1 + scale[:, None, :]) + shift[:, None, :]

def _mlstm_scan(q, k, v, log_i, log_f):
    B, H, S, Dh = q.shape
    nc = S // CHUNK

    def to_chunks(a):
        a = a.reshape((B, H, nc, CHUNK) + a.shape[3:])
        return jnp.moveaxis(a, 2, 0)

    xs = (to_chunks(q), to_chunks(k), to_chunks(v), to_chunks(log_f), to_chunks(log_i))
    tril = jnp.tril(jnp.ones((CHUNK, CHUNK), dtype=bool))

    def step(carry, inp):
        C, n, m = carry
        q_c, k_c, v_c, lf, li = inp
        b = jnp.cumsum(lf, axis=-1)
        d = b[..., :, None] - b[..., None, :] + li[..., None, :]
        d = jnp.where(tril, d, -jnp.inf)
        inter = b + m[..., None]
        m_t = jnp.maximum(inter, jnp.max(d, axis=-1))
        w = jnp.exp(d - m_t[..., None])
        a = jnp.exp(inter - m_t)
        s = jnp.einsum('bhtd,bhsd->bhts', q_c, k_c) * w
        num = (jnp.einsum('bhts,bhse->bhte', s, v_c)
               + a[..., None] * jnp.einsum('bhtd,bhde->bhte', q_c, C))
        den = jnp.sum(s, axis=-1) + a * jnp.einsum('bhtd,bhd->bht', q_c, n)
        h = num / jnp.maximum(jnp.abs(den), jnp.exp(-m_t))[..., None]
        b_last = b[..., -1]
        g = b_last[..., None] - b + li
        m_new = jnp.maximum(b_last + m, jnp.max(g, axis=-1))
        decay = jnp.exp(b_last + m - m_new)
        wk = jnp.exp(g - m_new[..., None])
        C_new = decay[..., None, None] * C + jnp.einsum('bhs,bhsd,bhse->bhde', wk, k_c, v_c)
        n_new = decay[..., None] * n + jnp.einsum('bhs,bhsd->bhd', wk, k_c)
        return (C_new, n_new, m_new), h

    init = (jnp.zeros((B, H, Dh, Dh), jnp.float32),
            jnp.zeros((B, H, Dh), jnp.float32),
            jnp.zeros((B, H), jnp.float32))
    _, hs = lax.scan(step, init, xs)
    return jnp.moveaxis(hs, 0, 2).reshape(B, H, S, Dh)

def _multiscale_pool(u, w_pool, pool_scale):
    B, S, _ = u.shape
    uf = u.astype(jnp.float32).reshape(B, S, N_POOL_GROUPS, POOL_GROUP_DIM)
    prefix = jnp.concatenate([jnp.zeros_like(uf[:, :1]), jnp.cumsum(uf, axis=1)], axis=1)
    t = jnp.arange(S)
    means = []
    for gi, win in enumerate(POOL_WINDOWS):
        lo = jnp.clip(t - win // 2, 0, S)
        hi = jnp.clip(t + win // 2, 0, S)
        p = prefix[:, :, gi]
        cnt = (hi - lo).astype(jnp.float32)
        means.append((p[:, hi] - p[:, lo]) / cnt[None, :, None])
    pooled = jnp.stack(means, axis=2)
    mixed = (pooled - uf).astype(u.dtype)
    y = jnp.einsum('bsgc,gce->bsge', mixed, w_pool).reshape(B, S, D_POOL)
    return y * pool_scale

def _mixer(h, w_in, b_igate, b_fgate, g_head, w_pool, pool_scale, w_out):
    B, S, _ = h.shape
    H = N_MLSTM_HEADS
    proj = jnp.einsum('bsd,dp->bsp', h, w_in)
    cuts = [D_MLSTM, 2 * D_MLSTM, 3 * D_MLSTM, 4 * D_MLSTM, 4 * D_MLSTM + N_GATE_COLS]
    q, k, v, o, gates, u = jnp.split(proj, cuts, axis=-1)

    def heads(a):
        return a.reshape(B, S, H, HEAD_DIM).transpose(0, 2, 1, 3).astype(jnp.float32)

    qh = heads(q) * (HEAD_DIM ** -0.5)
    kh = heads(k)
    vh = heads(v)
    gates = gates.astype(jnp.float32).reshape(B, S, N_DIRS, 2, H).transpose(2, 3, 0, 4, 1)
    log_i = gates[:, 0] + b_igate.astype(jnp.float32)[:, None, :, None]
    log_f = jax.nn.log_sigmoid(gates[:, 1] + b_fgate.astype(jnp.float32)[:, None, :, None])

    def flip(a):
        return jnp.flip(a, axis=2)

    h_fwd = _mlstm_scan(qh, kh, vh, log_i[0], log_f[0])
    h_bwd = flip(_mlstm_scan(flip(qh), flip(kh), flip(vh), flip(log_i[1]), flip(log_f[1])))
    hm = h_fwd + h_bwd
    hm = hm * lax.rsqrt(jnp.mean(hm * hm, axis=-1, keepdims=True) + EPS)
    hm = hm * g_head.astype(jnp.float32).reshape(H, 1, HEAD_DIM)
    hm = hm.transpose(0, 2, 1, 3).reshape(B, S, D_MLSTM)
    y_a = (jax.nn.sigmoid(o.astype(jnp.float32)) * hm).astype(h.dtype)

    y_b = _multiscale_pool(u, w_pool, pool_scale)
    y = jnp.concatenate([y_a, y_b], axis=-1)
    return jnp.einsum('bsm,md->bsd', y, w_out)

def first_inputs(seed: int = 0) -> dict:
    key = jax.random.key(seed)
    ks = jax.random.split(key, 17)
    f32 = jnp.float32
    H = N_MLSTM_HEADS

    def nrm(k, shape, scale):
        return jax.random.normal(k, shape, f32) * scale

    x = nrm(ks[0], (BATCH, SEQ, D_MODEL), 1.0)
    c = nrm(ks[1], (BATCH, D_MODEL), 1.0)
    w_ada = nrm(ks[2], (DEPTH, D_MODEL, 6 * D_MODEL), D_MODEL ** -0.5)
    b_ada = nrm(ks[3], (DEPTH, 6 * D_MODEL), 0.02)
    g_mix = 1.0 + nrm(ks[4], (DEPTH, D_MODEL), 0.05)
    w_in = nrm(ks[5], (DEPTH, D_MODEL, D_IN_PROJ), D_MODEL ** -0.5)
    b_igate = nrm(ks[6], (DEPTH, N_DIRS, H), 0.1)
    b_fgate = (jnp.broadcast_to(jnp.linspace(3.0, 6.0, H, dtype=f32), (DEPTH, N_DIRS, H))
               + nrm(ks[7], (DEPTH, N_DIRS, H), 0.1))
    g_head = 1.0 + nrm(ks[8], (DEPTH, D_MLSTM), 0.05)
    w_pool = nrm(ks[9], (DEPTH, N_POOL_GROUPS, POOL_GROUP_DIM, POOL_GROUP_DIM), POOL_GROUP_DIM ** -0.5)
    pool_scale = 1.0 + nrm(ks[10], (DEPTH, D_POOL), 0.1)
    w_out = nrm(ks[11], (DEPTH, D_MIX, D_MODEL), D_MIX ** -0.5)
    g_ffn = 1.0 + nrm(ks[12], (DEPTH, D_MODEL), 0.05)
    w_ff1 = nrm(ks[13], (DEPTH, D_MODEL, D_FF), D_MODEL ** -0.5)
    w_ff2 = nrm(ks[14], (DEPTH, D_FF, D_MODEL), D_FF ** -0.5)
    g_final = 1.0 + nrm(ks[15], (D_MODEL,), 0.05)
    return {"x": x, "c": c, "w_ada": w_ada, "b_ada": b_ada, "g_mix": g_mix, "w_in": w_in,
            "b_igate": b_igate, "b_fgate": b_fgate, "g_head": g_head, "w_pool": w_pool,
            "pool_scale": pool_scale, "w_out": w_out, "g_ffn": g_ffn, "w_ff1": w_ff1,
            "w_ff2": w_ff2, "g_final": g_final}

def first_block(x, c, w_ada, b_ada, g_mix, w_in, b_igate, b_fgate, g_head, w_pool,
              pool_scale, w_out, g_ffn, w_ff1, w_ff2, g_final):
    c_act = jax.nn.silu(c)
    for l in range(DEPTH):
        mod = c_act @ w_ada[l] + b_ada[l]
        sh1, sc1, gt1, sh2, sc2, gt2 = jnp.split(mod, 6, axis=-1)
        h = _modulate(_rmsnorm(x, g_mix[l]), sh1, sc1)
        x = x + gt1[:, None, :] * _mixer(h, w_in[l], b_igate[l], b_fgate[l], g_head[l],
                                         w_pool[l], pool_scale[l], w_out[l])
        h = _modulate(_rmsnorm(x, g_ffn[l]), sh2, sc2)
        a = jnp.square(jax.nn.relu(jnp.einsum('bsd,df->bsf', h, w_ff1[l])))
        x = x + gt2[:, None, :] * jnp.einsum('bsf,fd->bsd', a, w_ff2[l])
    return _rmsnorm(x, g_final)


SSD_EXPAND = 2
D_INNER = SSD_EXPAND * D_MODEL
SSD_HEAD_DIM = 64
SSD_HEADS = D_INNER // SSD_HEAD_DIM
SSD_GROUPS = 4
SSD_HEADS_PER_GROUP = SSD_HEADS // SSD_GROUPS
SSD_STATE = 128
SSD_CONV = 4
SSD_CHUNK = 128
SSD_CONV_DIM = D_INNER + 2 * SSD_GROUPS * SSD_STATE
MLA_HEADS = 16
MLA_Q_LORA = 256
MLA_KV_LORA = 128
MLA_NOPE = 64
MLA_ROPE = 32
MLA_QK_DIM = MLA_NOPE + MLA_ROPE
MLA_V_DIM = 64
MLA_WIDTH = MLA_HEADS * MLA_V_DIM
ROPE_THETA = 10000.0
ATTN_Q_BLOCK = 128
D_FF_2 = 2816
FFN_CONV = 3
NORM_EPS = 1e-6

OFF_Z = D_INNER
OFF_XBC = OFF_Z + SSD_CONV_DIM
OFF_DT = OFF_XBC + SSD_HEADS
OFF_QA = OFF_DT + MLA_Q_LORA
OFF_KVA = OFF_QA + MLA_KV_LORA
OFF_KR = OFF_KVA + MLA_ROPE
IN_COLS = OFF_KR + 2 * D_MODEL


def rms_norm(x, g):
    xf = x.astype(jnp.float32)
    xf = xf * lax.rsqrt(jnp.mean(xf * xf, axis=-1, keepdims=True) + NORM_EPS)
    return (xf * g.astype(jnp.float32)).astype(x.dtype)

def causal_depthwise_conv(x, w, b):
    k, c = w.shape
    y = lax.conv_general_dilated(x, w[:, None, :].astype(x.dtype), window_strides=(1,),
                                 padding=[(k - 1, 0)], dimension_numbers=('NWC', 'WIO', 'NWC'),
                                 feature_group_count=c)
    return y + b

def rope_tables(seq, dim):
    inv = 1.0 / (ROPE_THETA ** (jnp.arange(0, dim, 2, dtype=jnp.float32) / dim))
    ang = jnp.arange(seq, dtype=jnp.float32)[:, None] * inv[None, :]
    return jnp.cos(ang)[None, :, None, :], jnp.sin(ang)[None, :, None, :]

def apply_rope(x, cos, sin):
    x1, x2 = jnp.split(x.astype(jnp.float32), 2, axis=-1)
    return jnp.concatenate([x1 * cos - x2 * sin, x1 * sin + x2 * cos], axis=-1).astype(x.dtype)

def ssd_chunked_scan(xdt, a, bm, cm):
    b, l, h, p = xdt.shape
    nc = l // SSD_CHUNK
    f32 = jnp.float32
    xc = xdt.astype(f32).reshape(b, nc, SSD_CHUNK, SSD_GROUPS, SSD_HEADS_PER_GROUP, p)
    bc = bm.astype(f32).reshape(b, nc, SSD_CHUNK, SSD_GROUPS, SSD_STATE)
    cc = cm.astype(f32).reshape(b, nc, SSD_CHUNK, SSD_GROUPS, SSD_STATE)
    ac = a.astype(f32).reshape(b, nc, SSD_CHUNK, SSD_GROUPS, SSD_HEADS_PER_GROUP).transpose(0, 1, 3, 4, 2)
    a_cum = jnp.cumsum(ac, axis=-1)
    causal = jnp.tril(jnp.ones((SSD_CHUNK, SSD_CHUNK), dtype=bool))
    seg = a_cum[..., :, None] - a_cum[..., None, :]
    decay_in = jnp.exp(jnp.where(causal, seg, -jnp.inf))
    scores = jnp.einsum('bclgn,bcsgn->bcgls', cc, bc)
    y_diag = jnp.einsum('bcgls,bcgels,bcsgep->bclgep', scores, decay_in, xc)
    decay_to_end = jnp.exp(a_cum[..., -1:] - a_cum)
    chunk_states = jnp.einsum('bclgn,bcgel,bclgep->bcgepn', bc, decay_to_end, xc)
    chunk_decay = jnp.exp(a_cum[..., -1])

    def carry_state(state, inp):
        new_states, decay = inp
        return state * decay[..., None, None] + new_states, state

    init = jnp.zeros_like(chunk_states[:, 0])
    _, prev = lax.scan(carry_state, init,
                       (jnp.moveaxis(chunk_states, 1, 0), jnp.moveaxis(chunk_decay, 1, 0)))
    y_off = jnp.einsum('bclgn,cbgepn,bcgel->bclgep', cc, prev, jnp.exp(a_cum))
    return (y_diag + y_off).reshape(b, l, h, p).astype(xdt.dtype)

def ssd_mixer(z, xbc, dt_raw, conv_w, conv_b, dt_bias, a_log, d_skip, norm_g):
    b, l, _ = z.shape
    xbc = jax.nn.silu(causal_depthwise_conv(xbc, conv_w, conv_b))
    xs, bm, cm = jnp.split(xbc, [D_INNER, D_INNER + SSD_GROUPS * SSD_STATE], axis=-1)
    xs = xs.reshape(b, l, SSD_HEADS, SSD_HEAD_DIM)
    bm = bm.reshape(b, l, SSD_GROUPS, SSD_STATE)
    cm = cm.reshape(b, l, SSD_GROUPS, SSD_STATE)
    dt = jax.nn.softplus(dt_raw.astype(jnp.float32) + dt_bias.astype(jnp.float32))
    a = -jnp.exp(a_log.astype(jnp.float32))
    y = ssd_chunked_scan(xs * dt[..., None].astype(xs.dtype), dt * a, bm, cm)
    y = y + xs * d_skip[:, None]
    y = y.reshape(b, l, D_INNER) * jax.nn.silu(z)
    y = rms_norm(y.reshape(b, l, SSD_GROUPS, D_INNER // SSD_GROUPS),
                 norm_g.reshape(SSD_GROUPS, D_INNER // SSD_GROUPS))
    return y.reshape(b, l, D_INNER)

def blocked_causal_attention(q, k, v):
    b, l, h, dk = q.shape
    scale = dk ** -0.5
    key_pos = jnp.arange(l)

    def one_block(i):
        start = i * ATTN_Q_BLOCK
        qb = lax.dynamic_slice_in_dim(q, start, ATTN_Q_BLOCK, axis=1)
        s = jnp.einsum('bqhd,bkhd->bhqk', qb, k).astype(jnp.float32) * scale
        qpos = start + jnp.arange(ATTN_Q_BLOCK)
        s = jnp.where(qpos[:, None] >= key_pos[None, :], s, -jnp.inf)
        p = jax.nn.softmax(s, axis=-1).astype(v.dtype)
        return jnp.einsum('bhqk,bkhd->bqhd', p, v)

    out = lax.map(one_block, jnp.arange(l // ATTN_Q_BLOCK))
    return jnp.moveaxis(out, 0, 1).reshape(b, l, h * v.shape[-1])

def mla_mixer(q_a, kv_a, k_rope_raw, q_a_norm_g, w_uq, kv_a_norm_g, w_ukv, q_norm_g, k_norm_g, cos, sin):
    b, l, _ = q_a.shape
    q = (rms_norm(q_a, q_a_norm_g) @ w_uq).reshape(b, l, MLA_HEADS, MLA_QK_DIM)
    kv = (rms_norm(kv_a, kv_a_norm_g) @ w_ukv).reshape(b, l, MLA_HEADS, MLA_NOPE + MLA_V_DIM)
    k_nope, v = jnp.split(kv, [MLA_NOPE], axis=-1)
    k_rope = jnp.broadcast_to(k_rope_raw[:, :, None, :], (b, l, MLA_HEADS, MLA_ROPE))
    k = jnp.concatenate([k_nope, k_rope], axis=-1)
    q = rms_norm(q, q_norm_g)
    k = rms_norm(k, k_norm_g)
    q = jnp.concatenate([q[..., :MLA_NOPE], apply_rope(q[..., MLA_NOPE:], cos, sin)], axis=-1)
    k = jnp.concatenate([k[..., :MLA_NOPE], apply_rope(k[..., MLA_NOPE:], cos, sin)], axis=-1)
    return blocked_causal_attention(q, k, v)

def second_inputs(seed: int = 0) -> dict:
    key = jax.random.key(seed)
    ks = jax.random.split(key, 24)
    f32 = jnp.float32

    def dense(k, shape, fan_in):
        return jax.random.normal(k, (DEPTH,) + shape, f32) * fan_in ** -0.5

    def gain(k, n):
        return 1.0 + 0.02 * jax.random.normal(k, (DEPTH, n), f32)

    def bias(k, n):
        return 0.02 * jax.random.normal(k, (DEPTH, n), f32)

    dt0 = jnp.exp(jax.random.uniform(ks[5], (DEPTH, SSD_HEADS), f32, np.log(1e-3), np.log(1e-1)))
    return {
        "x": jax.random.normal(ks[0], (BATCH, SEQ, D_MODEL), f32),
        "norm_mix_g": gain(ks[1], D_MODEL),
        "w_in": dense(ks[2], (D_MODEL, IN_COLS), D_MODEL),
        "conv_ssd_w": dense(ks[3], (SSD_CONV, SSD_CONV_DIM), SSD_CONV),
        "conv_ssd_b": bias(ks[4], SSD_CONV_DIM),
        "dt_bias": dt0 + jnp.log(-jnp.expm1(-dt0)),
        "a_log": jnp.log(jax.random.uniform(ks[6], (DEPTH, SSD_HEADS), f32, 1.0, 16.0)),
        "d_skip": 1.0 + 0.1 * jax.random.normal(ks[7], (DEPTH, SSD_HEADS), f32),
        "ssd_norm_g": gain(ks[8], D_INNER),
        "w_ssd_proj": dense(ks[9], (D_INNER, D_MODEL), D_INNER),
        "q_a_norm_g": gain(ks[10], MLA_Q_LORA),
        "w_uq": dense(ks[11], (MLA_Q_LORA, MLA_HEADS * MLA_QK_DIM), MLA_Q_LORA),
        "kv_a_norm_g": gain(ks[12], MLA_KV_LORA),
        "w_ukv": dense(ks[13], (MLA_KV_LORA, MLA_HEADS * (MLA_NOPE + MLA_V_DIM)), MLA_KV_LORA),
        "q_norm_g": gain(ks[14], MLA_QK_DIM),
        "k_norm_g": gain(ks[15], MLA_QK_DIM),
        "w_mla_proj": dense(ks[16], (MLA_WIDTH, D_MODEL), MLA_WIDTH),
        "gate_b": bias(ks[17], 2 * D_MODEL),
        "w_o": dense(ks[18], (D_MODEL, D_MODEL), D_MODEL),
        "norm_ffn_g": gain(ks[19], D_MODEL),
        "w_up": dense(ks[20], (D_MODEL, 2 * D_FF_2), D_MODEL),
        "conv_ffn_w": dense(ks[21], (FFN_CONV, 2 * D_FF_2), FFN_CONV),
        "conv_ffn_b": bias(ks[22], 2 * D_FF_2),
        "w_down": dense(ks[23], (D_FF_2, D_MODEL), D_FF_2),
    }

def second_block(x, norm_mix_g, w_in, conv_ssd_w, conv_ssd_b, dt_bias, a_log, d_skip, ssd_norm_g,
              w_ssd_proj, q_a_norm_g, w_uq, kv_a_norm_g, w_ukv, q_norm_g, k_norm_g, w_mla_proj,
              gate_b, w_o, norm_ffn_g, w_up, conv_ffn_w, conv_ffn_b, w_down):
    cos, sin = rope_tables(x.shape[1], MLA_ROPE)
    for i in range(DEPTH):
        h = rms_norm(x, norm_mix_g[i])
        proj = h @ w_in[i]
        z, xbc, dt_raw, q_a, kv_a, k_rope_raw, gates = jnp.split(
            proj, [OFF_Z, OFF_XBC, OFF_DT, OFF_QA, OFF_KVA, OFF_KR], axis=-1)
        y_ssd = ssd_mixer(z, xbc, dt_raw, conv_ssd_w[i], conv_ssd_b[i], dt_bias[i], a_log[i],
                          d_skip[i], ssd_norm_g[i]) @ w_ssd_proj[i]
        y_mla = mla_mixer(q_a, kv_a, k_rope_raw, q_a_norm_g[i], w_uq[i], kv_a_norm_g[i], w_ukv[i],
                          q_norm_g[i], k_norm_g[i], cos, sin) @ w_mla_proj[i]
        g_ssd, g_mla = jnp.split(jax.nn.sigmoid(gates + gate_b[i]), 2, axis=-1)
        x = x + (g_ssd * y_ssd + g_mla * y_mla) @ w_o[i]
        h = rms_norm(x, norm_ffn_g[i])
        u = causal_depthwise_conv(h @ w_up[i], conv_ffn_w[i], conv_ffn_b[i])
        u_gate, u_val = jnp.split(u, 2, axis=-1)
        x = x + (jax.nn.silu(u_gate) * u_val) @ w_down[i]
    return x


def setup_inputs(seed=0):
    out = dict(first_inputs(seed))
    for name, value in second_inputs(seed + 1).items():
        if name != "x":
            out[name + "_2"] = value
    return out


def reference(
    x, c, w_ada, b_ada, g_mix, w_in, b_igate, b_fgate, g_head, w_pool, pool_scale, w_out, g_ffn,
    w_ff1, w_ff2, g_final, norm_mix_g_2, w_in_2, conv_ssd_w_2, conv_ssd_b_2, dt_bias_2, a_log_2,
    d_skip_2, ssd_norm_g_2, w_ssd_proj_2, q_a_norm_g_2, w_uq_2, kv_a_norm_g_2, w_ukv_2,
    q_norm_g_2, k_norm_g_2, w_mla_proj_2, gate_b_2, w_o_2, norm_ffn_g_2, w_up_2, conv_ffn_w_2,
    conv_ffn_b_2, w_down_2,
):
    x = first_block(
        x, c, w_ada, b_ada, g_mix, w_in, b_igate, b_fgate, g_head, w_pool, pool_scale, w_out,
        g_ffn, w_ff1, w_ff2, g_final,
    )
    return second_block(
        x, norm_mix_g_2, w_in_2, conv_ssd_w_2, conv_ssd_b_2, dt_bias_2, a_log_2, d_skip_2,
        ssd_norm_g_2, w_ssd_proj_2, q_a_norm_g_2, w_uq_2, kv_a_norm_g_2, w_ukv_2, q_norm_g_2,
        k_norm_g_2, w_mla_proj_2, gate_b_2, w_o_2, norm_ffn_g_2, w_up_2, conv_ffn_w_2,
        conv_ffn_b_2, w_down_2,
    )


_drawn_inputs = setup_inputs


def setup_inputs(seed=0):
    import zlib

    import numpy as np

    out = dict(_drawn_inputs(seed))
    spreads = {}
    factors = {'b_igate': 8.0,
     'g_head': 4.433,
     'norm_mix_g_2': 3.298,
     'conv_ssd_b_2': 4.123,
     'ssd_norm_g_2': 19.63,
     'q_a_norm_g_2': 8.0,
     'kv_a_norm_g_2': 8.0,
     'q_norm_g_2': 8.0,
     'k_norm_g_2': 8.0,
     'gate_b_2': 8.0,
     'norm_ffn_g_2': 11.54,
     'conv_ffn_b_2': 12.9,
     'd_skip_2': 42.096}
    for name, (base, spread) in spreads.items():
        noise = np.random.default_rng([zlib.crc32(name.encode()), seed]).standard_normal(out[name].shape)
        drawn = base * np.exp(spread * noise) if base else spread * noise
        out[name] = __import__('jax').numpy.asarray(drawn.astype(out[name].dtype))
    for name, factor in factors.items():
        out[name] = (out[name] * factor).astype(out[name].dtype)
    return out
```

```python
import numpy as np
import concourse.bass as bass
import concourse.mybir as mybir

P = 128
S = 512
D = 1024
KT = D // P
TOK = S // P
EPS = 1e-6
H1, DH = 4, 128
G1 = 36
WINDOWS = (2, 4, 8, 16)
SSD_H, SSD_P, SSD_G, XS_T, BC_T, TAPS = 32, 64, 4, 16, 8, 4
QH, QK, NOPE, ROPE, VD = 16, 96, 64, 32, 64
HU = 8
UP_T, TAPS_F = 22, 3
PAD = 8
SLAB = 16 * P

PHASES = [("q", 2), ("k", 2), ("v", 2), ("o", 2), ("u", 2), ("out", 4), ("ff1a", 8), ("ff2a", 8), ("ff1b", 8),
          ("ff2b", 8), ("misc", 2), ("xbc", 12), ("z", 8), ("gates", 8), ("ssd", 8), ("uq", 2), ("ukv", 2),
          ("mla", 4), ("wo", 4), ("upa", 16), ("downa", 8), ("upb", 6), ("downb", 4)]
WIDE = ("ff2a", "ff2b", "ssd", "downa")
OWN_BANKS = ("uq", "ukv")
SLAB0, SLABS, FREED, N_SLABS, _freed, _freed_wide = {}, {}, {}, 0, 0, 2
for _name, _n in PHASES:
    SLAB0[_name], SLABS[_name] = N_SLABS, _n
    N_SLABS += _n
    if _name in WIDE:
        FREED[_name], _freed_wide = _freed_wide, _freed_wide + _n
    elif _name not in OWN_BANKS:
        FREED[_name], _freed = _freed, _freed + 2 * _n

COLS, N_COLS = {}, 0
for _name, _n in [("c", 8), ("b_ada", 48), ("g_mix", 8), ("gate_bias", 1), ("g_head", 4), ("pool_scale", 4),
                  ("g_ffn", 8), ("g_final", 8), ("g_mix2", 8), ("conv_w", 96), ("conv_b", 24), ("dt_bias", 1),
                  ("a_log", 1), ("d_skip", 16), ("ssd_g", 16), ("qa_g", 2), ("kva_g", 1),
                  ("gate_b", 16), ("g_ffn2", 8), ("convf_w", 132), ("convf_b", 44)]:
    COLS[_name] = N_COLS
    N_COLS += _n
SH1, SC1, GT1, SH2, SC2, GT2 = (8 * n for n in range(6))


def build(nc, x_d, slabs_d, ada_d, cols_d, gate_w_d, pool_w_d, consts_d, inv_d, rope_d, qkg_d, out_d):
    f32, f32r, bf16 = mybir.dt.float32, mybir.dt.float32r, mybir.dt.bfloat16
    ALU, ACT, AX = mybir.AluOpType, mybir.ActivationFunctionType, mybir.AxisListType
    base = (nc.sbuf_base + 31) // 32 * 32
    K = 1024

    def at(name, shape, dt, offset):
        return nc.alloc_sbuf_tensor_at(name, [P] + shape, dt, offset=base + offset)

    x = at("x", [KT, S], f32, 0)
    raw = at("raw", [2, SLAB], f32, 16 * K)
    w_hi = at("w_hi", [2, SLAB], f32r, 32 * K)
    w_lo = at("w_lo", [2, SLAB], f32r, 48 * K)
    h = at("h", [2 * KT, S], f32r, 64 * K)
    h_hi, h_lo = h[:, 0:KT, :], h[:, KT:, :]
    A = 96 * K
    Z = A + 106 * K
    cols = at("cols", [N_COLS], f32, Z)
    consts = at("consts", [4, P], f32, Z + 1920)
    ident, keep_up, keep_low, causal = (consts[:, n, :] for n in range(4))
    mod = at("mod", [48], f32, Z + 3968)
    gain = at("gain", [16], f32, Z + 4160)
    small = at("small", [16], f32, Z + 4224)
    eps, c_act = small[:, 0:1], small[:, 8:16]
    mean = at("mean", [P], f32, Z + 4288)
    ones = at("ones", [P], f32, Z + 4800)
    kr_col = at("kr_col", [TOK, ROPE], f32, Z + 5312)
    sq = at("sq", [2, S], f32, A + 93 * K)
    rs = at("rs", [S], f32, A + 97 * K)
    t0 = at("t0", [S], f32, A + 99 * K)
    t1 = at("t1", [S], f32, A + 101 * K)
    ada_w = at("ada_w", [6, 2048], f32, A)
    ada_acc = at("ada_acc", [48 * P], f32, A + 53 * K)
    UW = S + 2 * PAD
    qk = at("qk", [8, S], f32, A)
    v1 = at("v1", [TOK, S], f32, A + 16 * K)
    og = at("og", [4, S], f32, A + 24 * K)
    u = at("u", [4, UW], f32, A + 32 * K)
    gw = at("gw", [KT, P], f32, A + 77 * K)
    gw_hi = at("gw_hi", [KT, P], f32r, A + 81 * K)
    gw_lo = at("gw_lo", [KT, P], f32r, A + 85 * K)
    win = at("win", [2, UW], f32, A + 41 * K)
    mixed1 = at("mixed1", [S], f32, A + 46 * K)
    e1 = at("e1", [1280], f32, A + 41 * K)
    p1 = at("p1", [1280], f32, A + 46 * K)
    y_hi = at("y_hi", [8, S], f32r, A + 53 * K)
    y_lo = at("y_lo", [8, S], f32r, A + 69 * K)
    rows = at("rows", [4, S], f32, A + 85 * K)
    hm = at("hm", [S], f32, A + 85 * K)
    den1 = at("den1", [S], f32, A + 87 * K)
    floor1 = at("floor1", [S], f32, A + 89 * K)
    hb = at("hb", [S], f32, A + 91 * K)
    inv = at("inv", [4, S], f32, A + 85 * K)
    neg_max = at("neg_max", [S], f32, A + 103 * K)
    neg_m = at("neg_m", [S], f32, A + 99 * K)
    a_col = at("a_col", [TOK, G1], f32, A + 40 * K + 256)
    pool_w = at("pool_w", [4, P], f32, A + 51 * K)
    a_hi = at("a_hi", [16, S], f32r, A)
    a_lo = at("a_lo", [16, S], f32r, A + 32 * K)
    relu = at("relu", [2, S], f32, A + 64 * K)
    asq = at("asq", [S], f32, A + 68 * K)
    xbc = at("xbc", [XS_T + BC_T, S], f32, A)
    qa = at("qa", [3, S], f32, A + 48 * K)
    mz = at("mz", [S], f32, A + 54 * K)
    xdt = at("xdt", [TOK, SSD_H * SSD_P], f32, A + 56 * K)
    cpad = at("cpad", [2, S + 4], f32, A + 56 * K)
    cacc = at("cacc", [2, S], f32, A + 62 * K)
    sm = at("sm", [1280], f32, A + 88 * K)
    p2 = at("p2", [2, 1280], f32, A + 93 * K)
    drow = at("drow", [4, S], f32, A + 88 * K)
    acum = at("acum", [S], f32, A + 103 * K)
    nac_col = at("nac_col", [TOK, SSD_H], f32, A + 105 * K)
    dt_col = at("dt_col", [TOK, SSD_H], f32, A + 105 * K + 512)
    rope = at("rope", [2, TOK, ROPE // 2], f32, A + 87 * K)
    qk_g = at("qk_g", [2, QK], f32, A + 104 * K)
    zt = at("zt", [2, S], f32, A + 88 * K)
    ys_hi = at("ys_hi", [XS_T, S], f32r, A + 56 * K)
    ys_lo = at("ys_lo", [XS_T, S], f32r, A)
    mix = at("mix", [8, S], f32, A + 32 * K)
    gm = at("gm", [8, S], f32, A + 88 * K)
    q2 = at("q2", [QH, S], f32, 64 * K)
    k2 = at("k2", [QH, S], f32, A)
    v2 = at("v2", [TOK, QH * VD], f32, A + 56 * K)
    qn_hi = at("qn_hi", [3, S], f32r, A + 72 * K)
    qn_lo = at("qn_lo", [3, S], f32r, A + 78 * K)
    tt = at("tt", [2, HU, QK], f32, A + 48 * K)
    tsq = at("tsq", [HU, QK], f32, A + 84 * K)
    trope = at("trope", [4, HU, ROPE // 2], f32, A + 54 * K)
    stat = at("stat", [3, HU], f32, A + 87 * K + 512)
    p3 = [at(f"p3_{n}", [1280], f32, A + (72, 48)[n] * K) for n in range(2)]
    pt = [at(f"pt_{n}", [1280], f32, A + (77, 82)[n] * K) for n in range(2)]
    mx = at("mx", [2, 3, TOK], f32, A + 87 * K + 640)
    mask16 = at("mask16", [2, P], bf16, A + 55 * K)
    att = at("att", [QH, S], f32r, 64 * K)
    ao = at("ao", [S], f32, A + 53 * K)
    mt = at("mt", [S], f32, A + 84 * K)
    mm_hi = at("mm_hi", [8, S], f32r, A)
    mm_lo = at("mm_lo", [8, S], f32r, A + 16 * K)
    sq_l = at("sq_l", [2, S], f32, A + 56 * K)
    rs_l = at("rs_l", [S], f32, A + 60 * K)
    t0_l = at("t0_l", [S], f32, A + 62 * K)
    t1_l = at("t1_l", [S], f32, A + 64 * K)
    fpad = at("fpad", [2, S + 4], f32, A + 64 * K)
    facc = at("facc", [2, S], f32, A + 70 * K)
    fgate = at("fgate", [S], f32, A + 74 * K)
    fa = at("fa", [S], f32, A + 76 * K)

    banks = [nc.alloc_psum_tensor(f"bank{n}", [P, S], f32) for n in range(8)]
    sems = {}

    def sem(name):
        if name not in sems:
            sems[name] = nc.alloc_semaphore(name)
        return sems[name]

    def col(name, n=0, first=0, rows=P):
        return cols[first:first + rows, bass.ds(COLS[name] + n, 1)]

    class Steps:

        def __init__(self, eng, name):
            self.eng, self.sem, self.n, self.turn, self.per = eng, sem(name), 0, 0, 0

        def __call__(self, ins):
            self.n += 1
            ins.then_inc(self.sem, 1)
            self.eng.wait_ge(self.sem, self.per * self.turn + self.n)

        def tell(self, ins, name, value):
            ins.then_inc(sem(name), 1)
            self.eng.wait_ge(sem(name), value)

        def loop(self, turn, per):
            self.turn, self.per, self.start = turn, per, self.n

        def end(self, turns):
            assert self.n - self.start == self.per, (self.n - self.start, self.per)
            self.n, self.turn, self.per = self.start + self.per * turns, 0, 0

    def spans(back):
        out, used = [], 0
        for j in range(TOK):
            lo, hi = (0, P * (j + 1)) if back else (P * j, S)
            out.append((j, lo, hi, used))
            used += hi - lo
        return out

    def beside():
        out, used = [], S
        for j in range(TOK - 1):
            lo = P * (j + 1)
            out.append((j, lo, S, used))
            used += S - lo
        return out

    block = nc.Block()
    with block:
        @block.sync
        def _(sp):
            sp.dma_start(cols[:], cols_d).then_inc(sem("cols_in"), 16)
            for k in range(0, KT, 4):
                sp.dma_start(x[:, k:k + 4, :], x_d[:, k:k + 4, :]).then_inc(sem("x_in"), 16)
            sp.dma_start(consts[:], consts_d).then_inc(sem("consts_in"), 16)
            sp.dma_start(gw[:], gate_w_d).then_inc(sem("gate_w_in"), 16)
            sp.dma_start(pool_w[:], pool_w_d).then_inc(sem("pool_w_in"), 16)
            for slot in range(2):
                sp.dma_start(raw[:, slot, :], slabs_d[slot, :, :]).then_inc(sem(f"raw_in{slot}"), 16)
            with sp.Fori(1, N_SLABS // 2) as i:
                for slot in range(2):
                    sp.wait_ge(sem("w_split"), 2 * i + slot - 1)
                    sp.dma_start(raw[:, slot, :], slabs_d[2 * i + slot, :, :]).then_inc(sem(f"raw_in{slot}"), 16)
            for m in range(KT):
                sp.wait_ge(sem("x_final"), m + 1)
                sp.dma_start(out_d[:, m, :], x[:, m, :]).then_inc(sem("out_sent"), 16)
            sp.wait_ge(sem("out_sent"), 16 * KT)

        @block.gpsimd
        def _(pool):
            def split(slot, nth):
                pool.tensor_tensor(w_hi[:, slot, :], raw[:, slot, :], ones[:, 0:1].to_broadcast([P, SLAB]),
                                   ALU.mult).then_inc(sem("w_head"), 1)
                pool.wait_ge(sem("w_head"), nth)
                pool.tensor_tensor(w_lo[:, slot, :], raw[:, slot, :], w_hi[:, slot, :].bitcast(f32),
                                   ALU.subtract).then_inc(sem("w_split"), 1)

            pool.wait_ge(sem("set"), 1)
            for slot in range(2):
                pool.wait_ge(sem(f"raw_in{slot}"), 16)
                split(slot, slot + 1)
            with pool.Fori(1, N_SLABS // 2) as i:
                for slot in range(2):
                    pool.wait_ge(sem(f"raw_in{slot}"), 16 * i + 16)
                    pool.wait_ge(sem("tile_done"), 4 * i + 2 * slot - 2)
                    pool.wait_ge(sem("w_split"), 2 * i + slot - 1)
                    split(slot, 2 * i + slot + 1)

        @block.scalar
        def _(act):
            do = Steps(act, "act_step")
            n_sq, n_root = 0, 0

            def fn(out, in_, f, **kw):
                return act.activation(out, in_, f, **kw)

            def tile_ready(name, t):
                act.wait_ge(sem("tile_done"), 2 * SLAB0[name] + t + 1)

            def free(ins, name, t):
                do.tell(ins, "bank_free", FREED[name] + t + 1)

            def squares(tiles, buf):
                nonlocal n_sq
                for tile in tiles:
                    if n_sq >= 2:
                        act.wait_ge(sem("sq_used"), n_sq - 1)
                    n_sq += 1
                    do.tell(fn(buf[:, (n_sq - 1) % 2, :], tile, ACT.Square), "sq_ready", n_sq)

            def root(buf, bank=7):
                nonlocal n_root
                act.wait_ge(sem("sq_used"), n_sq)
                if n_root:
                    act.wait_ge(sem("root_used"), n_root)
                n_root += 1
                do.tell(fn(buf[:], banks[bank][:], ACT.Sqrt, bias=eps), "root_ready", n_root)

            def norm():
                squares([x[:, k, :] for k in range(KT)], sq)
                root(rs)

            def heads(stage, shift=None):
                for k in range(KT):
                    n = KT * (stage - 1) + k + 1
                    act.wait_ge(sem("h_scaled"), n)
                    src = (t0, t1)[k % 2]
                    if shift is None:
                        do.tell(fn(h_hi[:, k, :], src[:], ACT.Copy), "h_head", n)
                    else:
                        do.tell(fn(h_hi[:, k, :], src[:], ACT.Identity, bias=mod[:, shift + k:shift + k + 1]), "h_head", n)

            for n in range(3 * KT):
                if n >= 6:
                    act.wait_ge(sem("ada_used"), n - 5)
                act.dma_start(ada_w[:, n % 6, :], ada_d[n, :, :]).then_inc(sem(f"ada_in{n % 6}"), 16)
                if n == 5:
                    act.wait_ge(sem("cols_in"), 16)
                    act.wait_ge(sem("set"), 1)
                    do.tell(fn(c_act, cols[:, COLS["c"]:COLS["c"] + KT], ACT.Silu), "c_ready", 1)
            act.wait_ge(sem("x_in"), 32)
            norm()
            heads(1, SH1)
            for name, first, scale in (("q", 0, DH ** -0.5), ("k", 4, 1.0)):
                for t in range(4):
                    tile_ready(name, t)
                    free(fn(qk[:, first + t, :], banks[t % 2][:], ACT.Copy, scale=scale), name, t)
            for c in range(2):
                for m in range(2):
                    tile_ready("v", 2 * c + m)
                    free(fn(v1[:, 2 * m:2 * m + 2, 256 * c:256 * c + 256],
                            banks[m][:].rearrange("p (t e) -> p t e", t=2), ACT.Copy), "v", 2 * c + m)
            for t in range(4):
                tile_ready("o", t)
                free(fn(og[:, t, :], banks[t % 2][:], ACT.Sigmoid), "o", t)
            act.wait_ge(sem("u_zeroed"), 1)
            for t in range(4):
                tile_ready("u", t)
                free(fn(u[:, t, PAD:PAD + S], banks[t % 2][:], ACT.Copy), "u", t)
            act.wait_ge(sem("gates_done"), 1)
            do(fn(rows[0:G1, 0, :], banks[4][0:G1, :], ACT.Identity, bias=col("gate_bias", 0, 0, G1)))
            do.tell(fn(rows[0:G1, 1, :], banks[4][64:64 + G1, :], ACT.Identity, bias=col("gate_bias", 0, 64, G1)),
                    "gates_biased", 1)
            act.wait_ge(sem("gate_negabs"), 1)
            do.tell(fn(rows[0:G1, 2, :], rows[0:G1, 2, :], ACT.Exp), "gate_exp", 1)
            act.wait_ge(sem("gate_onep"), 1)
            do.tell(fn(neg_m[0:G1, :], rows[0:G1, 3, :], ACT.Ln), "gate_ln", 1)
            act.wait_ge(sem("a_turned"), 1)
            do.tell(fn(a_col[:], banks[4][:, 0:TOK * G1].rearrange("p (t g) -> p t g", t=TOK), ACT.Copy), "a_col_ready", 1)
            for n in range(2 * H1):
                head, back = n // 2, n % 2
                r = 32 * back + head
                act.wait_ge(sem("bc1_done"), n + 1)
                if n:
                    act.wait_ge(sem("h1_made"), n)
                for j, lo, hi, used in spans(back):
                    do(fn(e1[:, used:used + hi - lo], banks[4][:, lo:hi], ACT.Exp, bias=a_col[:, j, r:r + 1]))
                do.tell(fn(floor1[:], banks[7][:], ACT.Exp), "e1_made", n + 1)
                if back:
                    act.wait_ge(sem("h1_made"), n + 1)
                    squares([hm[:]], sq)
                    root(rs, bank=5)
            act.wait_ge(sem("pool_place"), 1)
            act.dma_start(inv[:], inv_d).then_inc(sem("inv_in"), 16)
            act.wait_ge(sem("x_ready"), 1)
            norm()
            heads(2, SH2)
            for half, name in enumerate(("ff1a", "ff1b")):
                with act.Fori(0, SLABS[name] // 2) as i:
                    for t in range(4):
                        act.wait_ge(sem("tile_done"), 4 * i + 2 * SLAB0[name] + t + 1)
                        if half or t >= 2:
                            act.wait_ge(sem("relu_used"), 4 * i + 16 * half + t - 1)
                        else:
                            act.wait_ge(sem("relu_used"), 4 * i + t)
                        do.tell(fn(relu[:, t % 2, :], banks[t % 2][:], ACT.Relu), "bank_free", 4 * i + FREED[name] + t + 1)
            for after in (2, 3):
                act.wait_ge(sem("x_ready"), after)
                norm()
            heads(3)
            for t in range(4):
                tile_ready("misc", t)
                free(fn(qa[:, t, :] if t < 3 else mz[:], banks[t % 2][:], ACT.Copy), "misc", t)
            act.wait_ge(sem("dt_negabs"), 1)
            do.tell(fn(drow[0:32, 1, :], drow[0:32, 1, :], ACT.Exp), "dt_exp", 1)
            act.wait_ge(sem("dt_onep"), 1)
            do(fn(small[0:32, 1:2], col("a_log", 0, 0, 32), ACT.Exp))
            do.tell(fn(drow[0:32, 3, :], drow[0:32, 2, :], ACT.Ln), "dt_ln", 1)
            act.wait_ge(sem("cpad_zeroed"), 1)
            name = "xbc"
            with act.Fori(0, SLABS[name] // 2) as i:
                for t in range(4):
                    act.wait_ge(sem("tile_done"), 4 * i + 2 * SLAB0[name] + t + 1)
                    if t >= 2:
                        act.wait_ge(sem("conv_done"), 4 * i + t - 1)
                    else:
                        act.wait_ge(sem("conv_done"), 4 * i)
                    do.tell(fn(cpad[:, t % 2, TAPS - 1:TAPS - 1 + S], banks[t % 2][:], ACT.Copy), "bank_free",
                            4 * i + FREED[name] + t + 1)
                    act.wait_ge(sem("conv_done"), 4 * i + t + 1)
                    do.tell(fn(xbc[:, 4 * i + t, :], cacc[:, t % 2, :], ACT.Silu), "xbc_ready", 4 * i + t + 1)
            act.wait_ge(sem("dt_turned"), 1)
            for b, place in ((4, nac_col), (5, dt_col)):
                do(fn(place[:], banks[b][:, 0:P].rearrange("p (t g) -> p t g", t=TOK), ACT.Copy))
            do.tell(fn(kr_col[:], banks[6][:].rearrange("p (t g) -> p t g", t=TOK)[:, :, 64:64 + ROPE], ACT.Copy),
                    "dt_col_ready", 1)
            for hd in range(SSD_H):
                act.wait_ge(sem("diagonal_made"), hd + 1)
                e2 = p2[:, hd % 2, :]
                for j, lo, hi, used in beside():
                    do(fn(e2[:, used:used + hi - lo], banks[4 + hd % 2][:, lo:hi], ACT.Exp, bias=nac_col[:, j, hd:hd + 1]))
                do.tell(fn(e2[:, 0:S], e2[:, 0:S], ACT.Exp), "e2_made", hd + 1)
            act.wait_ge(sem("ys_made"), XS_T)
            name = "z"
            with act.Fori(0, SLABS[name] // 2) as i:
                for t in range(4):
                    act.wait_ge(sem("tile_done"), 4 * i + 2 * SLAB0[name] + t + 1)
                    if t >= 2:
                        act.wait_ge(sem("z_used"), 4 * i + t - 1)
                    else:
                        act.wait_ge(sem("z_used"), 4 * i)
                    do.tell(fn(zt[:, t % 2, :], banks[t % 2][:], ACT.Silu), "bank_free", 4 * i + FREED[name] + t + 1)
            act.wait_ge(sem("z_used"), XS_T)
            for g in range(SSD_G):
                squares([xbc[:, 4 * g + k, :] for k in range(4)], sq)
                root(rs)
            act.wait_ge(sem("root_used"), 8 + SSD_G)
            for t in range(16):
                tile_ready("gates", t)
                free(fn(mix[:, t, :] if t < 8 else gm[:, t - 8, :], banks[t % 2][:], ACT.Sigmoid, bias=col("gate_b", t)),
                     "gates", t)
            act.wait_ge(sem("mix_made"), 8)
            act.dma_start(rope[:], rope_d).then_inc(sem("rope_in"), 16)
            act.dma_start(qk_g[:], qkg_d).then_inc(sem("rope_in"), 16)
            squares([qa[:, k, :] for k in range(2)], sq_l)
            root(rs_l)
            squares([qa[:, 2, :]], sq_l)
            root(rs_l)
            def unit_in(n):
                keys, c, tok = n // 8, n // 4 % 2, n % 4
                if n % 2:
                    act.wait_ge(sem("tile_done"), 2 * (SLAB0["uq"] + n // 4) + n % 4 // 2 + 1)
                else:
                    act.wait_ge(sem("unit_done"), n // 2 + 1)
                if n >= 2:
                    act.wait_ge(sem("heads_turned"), n - 1)
                for half in range(2):
                    bank = banks[2 * (n % 2) + half]
                    part = slice(4 * half, 4 * half + 4)
                    if keys:
                        src = bank[:].rearrange("p (h e) -> p h e", h=4)
                        do(fn(tt[:, n % 2, part, 0:NOPE], src[:, :, 0:NOPE], ACT.Copy))
                        h0 = VD * (8 * c + 4 * half)
                        do(fn(v2[:, tok, h0:h0 + 4 * VD].rearrange("p (h e) -> p h e", h=4), src[:, :, NOPE:], ACT.Copy))
                        do(fn(tt[:, n % 2, part, NOPE:QK],
                              kr_col[:, tok, :].unsqueeze(1).to_broadcast([P, 4, ROPE]), ACT.Copy))
                    else:
                        do(fn(tt[:, n % 2, part, :], bank[:, 0:4 * QK].rearrange("p (h e) -> p h e", h=4), ACT.Copy))
                do.tell(fn(tsq[:], tt[:, n % 2, :, :], ACT.Square), "unit_squared", n + 1)

            def unit_out(n):
                keys, c, tok = n // 8, n // 4 % 2, n % 4
                act.wait_ge(sem("heads_turned"), n + 1)
                for half in range(2):
                    h0 = 8 * c + 4 * half
                    ins = fn((k2 if keys else q2)[0:QK, h0:h0 + 4, P * tok:P * tok + P],
                             banks[4 + 2 * (n % 2) + half][0:QK, :].rearrange("p (h t) -> p h t", h=4), ACT.Copy)
                    if half:
                        do.tell(ins, "heads_ready", n + 1)
                    else:
                        do(ins)

            act.wait_ge(sem("qn_made"), 3)
            for n in range(16):
                unit_in(n)
                if n:
                    unit_out(n - 1)
                act.wait_ge(sem("unit_summed"), n + 1)
                do.tell(fn(stat[:, 1, :], stat[:, 0, :], ACT.Sqrt, scale=1.0 / QK, bias=eps), "unit_root", n + 1)
            unit_out(15)
            for step in range(QH + 1):
                if step < QH:
                    hd = step
                    if hd >= 2:
                        act.wait_ge(sem("p3_turned"), hd - 1)
                    for i, lo, hi, used in spans(1):
                        act.wait_ge(sem("max_made"), TOK * hd + i + 1)
                        do.tell(fn(p3[hd % 2][:, used:used + hi], banks[i][:, 0:hi], ACT.Exp, scale=QK ** -0.5,
                                   bias=mx[:, hd % 2, 1, i:i + 1], accum_out=mx[:, hd % 2, 2, i:i + 1]),
                                "p3_made", TOK * hd + i + 1)
                if step:
                    hd = step - 1
                    place = pt[hd % 2]
                    act.wait_ge(sem("p3_turned"), hd + 1)
                    if hd >= 2:
                        act.wait_ge(sem("pv3_done"), hd - 1)
                    do(fn(place[:, 0:S], banks[4][:], ACT.Copy))
                    do(fn(place[:, S:S + 384], banks[5][:, 0:384], ACT.Copy))
                    do(fn(place[:, S + 384:S + 640], banks[6][:, 0:256], ACT.Copy))
                    do.tell(fn(place[:, S + 640:], banks[5][:, 384:S], ACT.Copy), "pt_made", hd + 1)
            act.wait_ge(sem("x_ready"), 4)
            norm()
            heads(4)
            act.wait_ge(sem("fpad_zeroed"), 1)
            for name, done in (("upa", 0), ("upb", 16)):
                with act.Fori(0, SLABS[name] // 2) as i:
                    for slot in range(2):
                        for m in range(2):
                            t = 2 * slot + m
                            act.wait_ge(sem("tile_done"), 4 * i + 2 * SLAB0[name] + t + 1)
                            act.wait_ge(sem("fa_made"), 2 * i + done + slot)
                            do.tell(fn(fpad[:, m, TAPS_F - 1:TAPS_F - 1 + S], banks[m][:], ACT.Copy), "bank_free",
                                    4 * i + FREED[name] + t + 1)
                        act.wait_ge(sem("fconv_done"), 2 * i + done + slot + 1)
                        do.tell(fn(fgate[:], facc[:, 0, :], ACT.Silu), "fgate_made", 2 * i + done + slot + 1)

        @block.vector
        def _(dve):
            do = Steps(dve, "dve_step")
            n_root = 0
            n_x = 0

            def free(ins, name, t, which="bank_free"):
                do.tell(ins, which, FREED[name] + t + 1)

            def split(hi, lo, src):
                do(dve.tensor_copy(hi, src))
                return dve.tensor_tensor(lo, src, hi.bitcast(f32), ALU.subtract)

            def inverse_root(buf):
                nonlocal n_root
                n_root += 1
                dve.wait_ge(sem("root_ready"), n_root)
                do(dve.reciprocal(buf[:], buf[:]))

            def add_to_x(name, gate=None, wide=False):
                for m in range(KT):
                    s = SLAB0[name] + (m if wide else m // 2)
                    dve.wait_ge(sem("tile_done"), 2 * s + (2 if wide else m % 2 + 1))
                    bank = banks[(2 if wide else 0) + m % 2]
                    if gate is None:
                        ins = dve.tensor_tensor(x[:, m, :], bank[:], x[:, m, :], ALU.add)
                    else:
                        ins = dve.scalar_tensor_tensor(x[:, m, :], bank[:], mod[:, gate + m:gate + m + 1], x[:, m, :],
                                                       ALU.mult, ALU.add)
                    free(ins, name, m, "bank_free_wide" if wide else "bank_free")

            def told_x():
                nonlocal n_x
                n_x += 1
                do.tell(dve.tensor_copy(small[:, 2:3], small[:, 0:1]), "x_ready", n_x)

            def modulated(stage, scale, shift=None):
                inverse_root(rs)
                first = KT * (stage - 1)

                def scaled(k):
                    do.tell(dve.scalar_tensor_tensor((t0, t1)[k % 2][:], x[:, k, :], scale(k), rs[:], ALU.mult, ALU.mult),
                            "h_scaled", first + k + 1)

                scaled(0)
                for k in range(KT):
                    if k + 1 < KT:
                        scaled(k + 1)
                    dve.wait_ge(sem("h_head"), first + k + 1)
                    src, head = (t0, t1)[k % 2][:], h_hi[:, k, :].bitcast(f32)
                    if shift is None:
                        ins = dve.tensor_tensor(h_lo[:, k, :], src, head, ALU.subtract)
                    else:
                        ins = dve.scalar_tensor_tensor(h_lo[:, k, :], src, mod[:, shift + k:shift + k + 1], head,
                                                       ALU.add, ALU.subtract)
                    do.tell(ins, "h_ready", first + k + 1)
                do.tell(dve.tensor_copy(small[:, 2:3], small[:, 0:1]), "root_used", n_root)

            do(dve.memset(small[:], EPS))
            do(dve.memset(ones[:], 1.0))
            do.tell(dve.memset(mean[:], 1.0 / D), "set", 1)
            for n in range(2):
                do.tell(dve.memset(small[:, 3:4], 0.0), "bank_free_wide", n + 1)
            dve.wait_ge(sem("c_ready"), 1)
            for n in range(3 * KT):
                third, k = n // KT, n % KT
                dve.wait_ge(sem(f"ada_in{n % 6}"), 16 * (n // 6) + 16)
                acc = ada_acc[:, 2048 * third:2048 * third + 2048]
                if k == 0:
                    ins = dve.tensor_scalar(acc, ada_w[:, n % 6, :], c_act[:, 0:1], None, ALU.mult)
                else:
                    ins = dve.scalar_tensor_tensor(acc, ada_w[:, n % 6, :], c_act[:, k:k + 1], acc, ALU.mult, ALU.add)
                do.tell(ins, "ada_used", n + 1)
            dve.wait_ge(sem("mod_done"), 1)
            do(dve.scalar_tensor_tensor(mod[:], banks[4][:, 0:48], float(D), cols[:, COLS["b_ada"]:COLS["b_ada"] + 48],
                                        ALU.mult, ALU.add))
            for first, sc, g in ((0, SC1, "g_mix"), (8, SC2, "g_ffn")):
                do(dve.scalar_tensor_tensor(gain[:, first:first + 8], mod[:, sc:sc + 8], 1.0,
                                            cols[:, COLS[g]:COLS[g] + 8], ALU.add, ALU.mult))
            dve.wait_ge(sem("gate_w_in"), 16)
            do.tell(split(gw_hi[:], gw_lo[:], gw[:]), "gate_w_split", 1)
            modulated(1, lambda k: gain[:, k:k + 1], SH1)
            do.tell(dve.memset(u[:], 0.0), "u_zeroed", 1)
            dve.wait_ge(sem("gates_biased"), 1)
            li, lf, r2, r3 = (rows[0:G1, n, :] for n in range(4))
            ge, gs = neg_max[0:G1, :], neg_m[0:G1, :]
            do.tell(dve.scalar_tensor_tensor(r2, lf, -1.0, lf, ALU.mult, ALU.min), "gate_negabs", 1)
            dve.wait_ge(sem("gate_exp"), 1)
            do.tell(dve.tensor_scalar(r3, r2, 1.0, None, ALU.add), "gate_onep", 1)
            do(dve.scalar_tensor_tensor(r2, r3, -1.0, r2, ALU.add, ALU.subtract))
            dve.wait_ge(sem("gate_ln"), 1)
            do(dve.reciprocal(r3, r3))
            do(dve.tensor_tensor(r2, r2, r3, ALU.mult))
            do(dve.tensor_tensor(r2, gs, r2, ALU.subtract))
            do(dve.scalar_tensor_tensor(lf, lf, 0.0, r2, ALU.min, ALU.subtract))
            do(dve.memset(r3, 1.0))

            def scan(out, data0, data1, first, op0, op1, initial):
                rows_ = slice(first, first + H1)
                turn = slice(None, None, -1) if first else slice(None)
                do(dve.tensor_tensor_scan(out[rows_, turn], data0[rows_, turn], data1[rows_, turn], initial, op0, op1))

            total, a, top = r2, li, ge
            do(dve.memset(total, 0.0))
            do(dve.memset(top, 0.0))
            for first in (0, 32):
                scan(rows[:, 2, :], rows[:, 3, :], rows[:, 1, :], first, ALU.mult, ALU.add, 0.0)
            do(dve.tensor_tensor(a, li, total, ALU.subtract))
            for first in (0, 32):
                scan(neg_max[:], rows[:, 0, :], rows[:, 0, :], first, ALU.max, ALU.max, 0.0)
            do(dve.scalar_tensor_tensor(gs, total, -1.0, top, ALU.mult, ALU.subtract))
            do.tell(dve.tensor_scalar(ge, top, -1.0, None, ALU.mult), "gate_rows", 1)
            dve.wait_ge(sem("a_col_ready"), 1)
            do.tell(dve.memset(mean[:], 1.0 / DH), "mean_set", 1)
            dve.wait_ge(sem("consts_in"), 16)
            for n in range(2 * H1):
                head, back = n // 2, n % 2
                dve.wait_ge(sem("e1_made"), n + 1)
                dve.wait_ge(sem("s1_done"), head + 1)
                if n:
                    dve.wait_ge(sem("pv1_done"), n)
                keep = keep_low if back else keep_up
                for j, lo, hi, used in spans(back):
                    do(dve.scalar_tensor_tensor(p1[:, used:used + hi - lo], e1[:, used:used + hi - lo], 1.0,
                                                banks[j][:, lo:hi], ALU.min, ALU.mult))
                    d0 = used + P * j - lo
                    ins = dve.tensor_tensor(p1[:, d0:d0 + P], p1[:, d0:d0 + P], keep, ALU.mult)
                    if j < TOK - 1:
                        do(ins)
                    else:
                        do.tell(ins, "p1_made", n + 1)
                dve.wait_ge(sem("pv1_done"), n + 1)
                do(dve.scalar_tensor_tensor(den1[:], banks[6][:], -1.0, floor1[:], ALU.mult, ALU.max))
                do(dve.tensor_tensor(den1[:], den1[:], banks[6][:], ALU.max))
                do(dve.reciprocal(den1[:], den1[:]))
                if back:
                    do(dve.tensor_tensor(hb[:], banks[5][:], den1[:], ALU.mult))
                    do.tell(dve.tensor_tensor(hm[:], hm[:], hb[:], ALU.add), "h1_made", n + 1)
                    inverse_root(rs)
                    do(dve.tensor_tensor(hb[:], hm[:], rs[:], ALU.mult))
                    do(dve.scalar_tensor_tensor(t1[:], hb[:], col("g_head", head), og[:, head, :], ALU.mult, ALU.mult))
                    do.tell(split(y_hi[:, head, :], y_lo[:, head, :], t1[:]), "root_used", n_root)
                else:
                    do.tell(dve.tensor_tensor(hm[:], banks[5][:], den1[:], ALU.mult), "h1_made", n + 1)
            do.tell(dve.memset(win[:], 0.0), "pool_place", 1)
            dve.wait_ge(sem("inv_in"), 16)
            for g, size in enumerate(WINDOWS):
                if g:
                    dve.wait_ge(sem("pool_done"), g)
                src, edge = u[:, g, :], 1
                do(dve.tensor_tensor(win[:, 0, 1:UW], u[:, g, 0:UW - 1], u[:, g, 1:UW], ALU.add))
                w, reach, margin = 0, 1, 1
                while 2 * reach < size:
                    a0, a1 = margin + reach, UW - margin - reach
                    do(dve.tensor_tensor(win[:, 1 - w, a0:a1], win[:, w, a0 - reach:a1 - reach],
                                         win[:, w, a0 + reach:a1 + reach], ALU.add))
                    margin, w, reach = margin + reach, 1 - w, 2 * reach
                do(dve.tensor_tensor(mixed1[:], win[:, w, PAD:PAD + S], inv[:, g, :], ALU.mult))
                do.tell(dve.tensor_tensor(mixed1[:], mixed1[:], u[:, g, PAD:PAD + S], ALU.subtract), "pooled", g + 1)
                dve.wait_ge(sem("pool_done"), g + 1)
                do(dve.tensor_scalar(t1[:], banks[4 + g % 2][:], col("pool_scale", g), None, ALU.mult))
                do.tell(split(y_hi[:, 4 + g, :], y_lo[:, 4 + g, :], t1[:]), "y_ready", g + 1)
            do.tell(dve.memset(mean[:], 1.0 / D), "mean_set", 2)
            add_to_x("out", GT1)
            told_x()
            modulated(2, lambda k: gain[:, 8 + k:9 + k], SH2)
            for half, (up, down) in enumerate((("ff1a", "ff2a"), ("ff1b", "ff2b"))):
                with dve.Fori(0, SLABS[up] // 2) as i:
                    do.loop(i, 4)
                    for t in range(4):
                        dve.wait_ge(sem("bank_free"), 4 * i + FREED[up] + t + 1)
                        do.tell(dve.tensor_tensor(asq[:], relu[:, t % 2, :], relu[:, t % 2, :], ALU.mult), "relu_used",
                                4 * i + 16 * half + t + 1)
                        place = 4 * i + t
                        do(dve.tensor_copy(a_hi[:, place, :], asq[:]))
                        do.tell(dve.tensor_tensor(a_lo[:, place, :], asq[:], a_hi[:, place, :].bitcast(f32), ALU.subtract),
                                "a_ready", 4 * i + 16 * half + t + 1)
                do.end(SLABS[up] // 2)
                add_to_x(down, GT2, wide=True)
            told_x()
            inverse_root(rs)
            for k in range(KT):
                do(dve.scalar_tensor_tensor(x[:, k, :], x[:, k, :], col("g_final", k), rs[:], ALU.mult, ALU.mult))
            do.tell(dve.tensor_copy(small[:, 2:3], small[:, 0:1]), "root_used", n_root)
            told_x()
            modulated(3, lambda k: col("g_mix2", k))
            dve.wait_ge(sem("bank_free"), FREED["misc"] + 4)
            d0, d1, d2, d3 = (drow[0:32, n, :] for n in range(4))
            do(dve.tensor_scalar(d0, mz[0:32, :], col("dt_bias", 0, 0, 32), None, ALU.add))
            do.tell(dve.scalar_tensor_tensor(d1, d0, -1.0, d0, ALU.mult, ALU.min), "dt_negabs", 1)
            dve.wait_ge(sem("dt_exp"), 1)
            do.tell(dve.tensor_scalar(d2, d1, 1.0, None, ALU.add), "dt_onep", 1)
            do(dve.scalar_tensor_tensor(d1, d2, -1.0, d1, ALU.add, ALU.subtract))
            dve.wait_ge(sem("dt_ln"), 1)
            do(dve.reciprocal(d2, d2))
            do(dve.tensor_tensor(d1, d1, d2, ALU.mult))
            do(dve.tensor_tensor(d3, d3, d1, ALU.subtract))
            do(dve.scalar_tensor_tensor(d0, d0, 0.0, d3, ALU.max, ALU.add))
            do(dve.tensor_scalar(d1, d0, small[0:32, 1:2], -1.0, ALU.mult, ALU.mult))
            do(dve.memset(d2, 1.0))
            do(dve.tensor_tensor_scan(acum[0:32, :], d2, d1, 0.0, ALU.mult, ALU.add))
            do.tell(dve.tensor_scalar(d3, acum[0:32, :], -1.0, None, ALU.mult), "dt_rows", 1)
            do.tell(dve.memset(cpad[:], 0.0), "cpad_zeroed", 1)
            with dve.Fori(0, SLABS["xbc"] // 2) as i:
                do.loop(i, 4 * (TAPS - 1))
                for t in range(4):
                    n = 4 * i + t
                    dve.wait_ge(sem("bank_free"), 4 * i + FREED["xbc"] + t + 1)
                    if t >= 2:
                        dve.wait_ge(sem("xbc_ready"), 4 * i + t - 1)
                    else:
                        dve.wait_ge(sem("xbc_ready"), 4 * i)
                    acc, pad = cacc[:, t % 2, :], cpad[:, t % 2, :]
                    do(dve.tensor_scalar(acc, pad[:, 0:S], col("conv_w", TAPS * n), col("conv_b", n), ALU.mult, ALU.add))
                    for tap in range(1, TAPS):
                        ins = dve.scalar_tensor_tensor(acc, pad[:, tap:tap + S], col("conv_w", TAPS * n + tap), acc,
                                                       ALU.mult, ALU.add)
                        if tap < TAPS - 1:
                            do(ins)
                        else:
                            do.tell(ins, "conv_done", 4 * i + t + 1)
            do.end(SLABS["xbc"] // 2)
            dve.wait_ge(sem("dt_col_ready"), 1)
            for n in range(TOK * 4):
                tok, quad = n // 4, n % 4
                dve.wait_ge(sem("xs_turned"), n + 1)
                scale = dt_col[:, tok, 8 * quad:8 * quad + 8].unsqueeze(2).to_broadcast([P, 8, SSD_P])
                do.tell(dve.tensor_tensor(xdt[:, tok, S * quad:S * quad + S].rearrange("p (h e) -> p h e", h=8),
                                          banks[n % 4][:].rearrange("p (h e) -> p h e", h=8), scale, ALU.mult),
                        "xdt_made", n + 1)
            def diagonal_exponents(hd):
                dve.wait_ge(sem("bc2_done"), hd + 1)
                if hd >= 2:
                    dve.wait_ge(sem("pv2_done"), hd - 1)
                for j in range(TOK):
                    part = slice(P * j, P * j + P)
                    ins = dve.tensor_scalar(p2[:, hd % 2, part], banks[4 + hd % 2][:, part], nac_col[:, j, hd:hd + 1], 0.0,
                                            ALU.add, ALU.min)
                    if j < TOK - 1:
                        do(ins)
                    else:
                        do.tell(ins, "diagonal_made", hd + 1)

            diagonal_exponents(0)
            for hd in range(SSD_H):
                g = hd // 8
                if hd % 8 == 0:
                    dve.wait_ge(sem("s2_done"), g + 1)
                    for j, lo, hi, used in beside():
                        do(dve.tensor_copy(sm[:, used:used + hi - lo], banks[j][:, lo:hi]))
                    for j in range(TOK):
                        part = slice(P * j, P * j + P)
                        ins = dve.tensor_tensor(sm[:, part], banks[j][:, part], keep_up, ALU.mult)
                        if j < TOK - 1:
                            do(ins)
                        else:
                            do.tell(ins, "sm_made", g + 1)
                if hd + 1 < SSD_H:
                    diagonal_exponents(hd + 1)
                dve.wait_ge(sem("e2_made"), hd + 1)
                do.tell(dve.tensor_tensor(p2[:, hd % 2, :], p2[:, hd % 2, :], sm[:], ALU.mult), "p2_made", hd + 1)
                if hd % 2:
                    pair = hd // 2
                    dve.wait_ge(sem("pv2_done"), hd + 1)
                    do.tell(dve.scalar_tensor_tensor(xbc[:, pair, :], xbc[:, pair, :], col("d_skip", pair),
                                                     banks[6 + pair % 2][:], ALU.mult, ALU.add), "ys_made", pair + 1)
            with dve.Fori(0, SLABS["z"] // 2) as i:
                for t in range(4):
                    dve.wait_ge(sem("bank_free"), 4 * i + FREED["z"] + t + 1)
                    place = xbc[:, 4 * i + t, :]
                    do.tell(dve.tensor_tensor(place, place, zt[:, t % 2, :], ALU.mult), "z_used", 4 * i + t + 1)
            do.tell(dve.memset(mean[:], 1.0 / (4 * P)), "mean_set", 3)
            for g in range(SSD_G):
                inverse_root(rs)
                for k in range(4 * g, 4 * g + 4):
                    do(dve.scalar_tensor_tensor(t1[:], xbc[:, k, :], col("ssd_g", k), rs[:], ALU.mult, ALU.mult))
                    ins = split(ys_hi[:, k, :], ys_lo[:, k, :], t1[:])
                    if k % 4 < 3:
                        do(ins)
                    else:
                        do.tell(ins, "root_used", n_root)
            dve.wait_ge(sem("bank_free"), FREED["gates"] + 16)
            for m in range(8):
                dve.wait_ge(sem("tile_done"), 2 * (SLAB0["ssd"] + m) + 2)
                do.tell(dve.tensor_tensor(mix[:, m, :], mix[:, m, :], banks[2 + m % 2][:], ALU.mult), "bank_free_wide",
                        FREED["ssd"] + m + 1)
                do.tell(dve.tensor_copy(small[:, 2:3], small[:, 0:1]), "mix_made", m + 1)
            do.tell(dve.memset(mean[:], 1.0 / (2 * P)), "mean_set", 4)
            for first, n in ((0, 2), (2, 1)):
                inverse_root(rs_l)
                for k in range(first, first + n):
                    do(dve.scalar_tensor_tensor(t1_l[:], qa[:, k, :], col("qa_g", k), rs_l[:], ALU.mult, ALU.mult))
                    do.tell(split(qn_hi[:, k, :], qn_lo[:, k, :], t1_l[:]), "qn_made", k + 1)
                if first == 0:
                    do.tell(dve.memset(mean[:], 1.0 / P), "mean_set", 5)
                do.tell(dve.tensor_copy(small[:, 2:3], small[:, 0:1]), "root_used", n_root)
            dve.wait_ge(sem("rope_in"), 32)
            for n in range(16):
                keys, tok = n // 8, n % 4
                tile = tt[:, n % 2, :, :]
                dve.wait_ge(sem("unit_squared"), n + 1)
                do.tell(dve.tensor_reduce(stat[:, 0, :], tsq[:], AX.X, ALU.add), "unit_summed", n + 1)
                dve.wait_ge(sem("unit_root"), n + 1)
                do(dve.reciprocal(stat[:, 2, :], stat[:, 1, :]))
                do(dve.tensor_tensor(tile, tile, stat[:, 2, :].unsqueeze(2).to_broadcast([P, HU, QK]), ALU.mult))
                do(dve.tensor_tensor(tile, tile, qk_g[:, keys, :].unsqueeze(1).to_broadcast([P, HU, QK]), ALU.mult))
                cos, sin = (rope[:, s, tok, :].unsqueeze(1).to_broadcast([P, HU, ROPE // 2]) for s in range(2))
                first, second = tile[:, :, NOPE:NOPE + ROPE // 2], tile[:, :, NOPE + ROPE // 2:QK]
                for part, src, f in ((0, first, cos), (1, second, sin), (2, first, sin), (3, second, cos)):
                    do(dve.tensor_tensor(trope[:, part, :, :], src, f, ALU.mult))
                do(dve.tensor_tensor(first, trope[:, 0, :, :], trope[:, 1, :, :], ALU.subtract))
                do.tell(dve.tensor_tensor(second, trope[:, 2, :, :], trope[:, 3, :, :], ALU.add), "heads_scaled", n + 1)
            do(dve.tensor_copy(mask16[:, 0, :], ident))
            do.tell(dve.tensor_copy(mask16[:, 1, :], causal), "mask_made", 1)

            def maxima(hd):
                for i, lo, hi, used in spans(1):
                    dve.wait_ge(sem("s3_done"), TOK * hd + i + 1)
                    top, bias = (mx[:, hd % 2, n, i:i + 1] for n in range(2))
                    do(dve.tensor_reduce(top, banks[i][:, 0:hi], AX.X, ALU.max))
                    do.tell(dve.tensor_scalar(bias, top, -QK ** -0.5, None, ALU.mult), "max_made", TOK * hd + i + 1)

            maxima(0)
            for step in range(QH + 2):
                if step < QH:
                    hd = step
                    for i, lo, hi, used in spans(1):
                        part, total = p3[hd % 2][:, used:used + hi], mx[:, hd % 2, 2, i:i + 1]
                        dve.wait_ge(sem("p3_made"), TOK * hd + i + 1)
                        do(dve.reciprocal(total, total))
                        do.tell(dve.tensor_scalar(part, part, total, None, ALU.mult), "p3_scaled", TOK * hd + i + 1)
                if step + 1 < QH:
                    maxima(step + 1)
                if step >= 2 and step % 2:
                    pair = step // 2 - 1
                    dve.wait_ge(sem("pv3_done"), 2 * pair + 2)
                    do(dve.tensor_copy(ao[:], banks[7][:]))
                    do.tell(split(att[:, 2 * pair, :], att[:, 2 * pair + 1, :], ao[:]), "att_made", pair + 1)
            for m in range(8):
                dve.wait_ge(sem("tile_done"), 2 * SLAB0["mla"] + m + 1)
                free(dve.tensor_tensor(mt[:], gm[:, m, :], banks[m % 2][:], ALU.mult), "mla", m)
                do(dve.tensor_tensor(mix[:, m, :], mix[:, m, :], mt[:], ALU.add))
                do.tell(split(mm_hi[:, m, :], mm_lo[:, m, :], mix[:, m, :]), "mm_made", m + 1)
            do.tell(dve.memset(mean[:], 1.0 / D), "mean_set", 6)
            add_to_x("wo")
            told_x()
            modulated(4, lambda k: col("g_ffn2", k))
            do.tell(dve.memset(fpad[:], 0.0), "fpad_zeroed", 1)
            for up, done in (("upa", 0), ("upb", 16)):
                with dve.Fori(0, SLABS[up] // 2) as i:
                    do.loop(i, 2 * (2 * TAPS_F - 1 + 2))
                    for slot in range(2):
                        for m in range(2):
                            dve.wait_ge(sem("bank_free"), 4 * i + FREED[up] + 2 * slot + m + 1)
                            tile = 2 * (2 * i + done + slot) + m
                            acc, pad = facc[:, m, :], fpad[:, m, :]
                            do(dve.tensor_scalar(acc, pad[:, 0:S], col("convf_w", TAPS_F * tile), col("convf_b", tile),
                                                 ALU.mult, ALU.add))
                            for tap in range(1, TAPS_F):
                                ins = dve.scalar_tensor_tensor(acc, pad[:, tap:tap + S], col("convf_w", TAPS_F * tile + tap),
                                                               acc, ALU.mult, ALU.add)
                                if m == 0 and tap == TAPS_F - 1:
                                    do.tell(ins, "fconv_done", 2 * i + done + slot + 1)
                                else:
                                    do(ins)
                        dve.wait_ge(sem("fgate_made"), 2 * i + done + slot + 1)
                        do(dve.tensor_tensor(fa[:], fgate[:], facc[:, 1, :], ALU.mult))
                        place = 2 * i + slot
                        do(dve.tensor_copy(a_hi[:, place, :], fa[:]))
                        do.tell(dve.tensor_tensor(a_lo[:, place, :], fa[:], a_hi[:, place, :].bitcast(f32), ALU.subtract),
                                "fa_made", 2 * i + done + slot + 1)
                do.end(SLABS[up] // 2)
                if up == "upa":
                    add_to_x("downa", wide=True)
            for m in range(KT):
                dve.wait_ge(sem("tile_done"), 2 * SLAB0["downb"] + m + 1)
                free(dve.tensor_tensor(x[:, m, :], banks[m % 2][:], x[:, m, :], ALU.add), "downb", m)
                do.tell(dve.tensor_copy(small[:, 2:3], small[:, 0:1]), "x_final", m + 1)

        @block.tensor
        def _(pe):
            n_sq = 0

            def three(out, w, a, start, stop):
                pe.matmul(out, w[0], a[0], start=start, stop=False)
                pe.matmul(out, w[0], a[1], start=False, stop=False)
                return pe.matmul(out, w[1], a[0], start=False, stop=stop)

            def weights(slot, tile, n=1):
                part = slice(P * tile, P * (tile + n))
                return w_hi[:, slot, part], w_lo[:, slot, part]

            def product(name, hi, lo, kt=KT, gate=None):
                wide = name in WIDE
                bank0, which = (2, "bank_free_wide") if wide else (0, "bank_free")

                def turn(i):
                    for slot in range(2):
                        pe.wait_ge(sem("w_split"), 2 * i + SLAB0[name] + slot + 1)
                        for m in range(1 if wide else 2):
                            t = slot if wide else 2 * slot + m
                            per = 2 if wide else 4
                            before = FREED[name] + t - 1
                            if not isinstance(i, int) or before > 0:
                                pe.wait_ge(sem(which), per * i + before)
                            for k in range(kt):
                                last = three(banks[bank0 + t % 2][:], weights(slot, (16 if wide else KT) * m + k),
                                             (hi[:, k, :], lo[:, k, :]), k == 0, k == kt - 1)
                            last.then_inc(sem("tile_done"), 2 if wide else 1)

                if SLABS[name] == 2:
                    turn(0)
                else:
                    with pe.Fori(0, SLABS[name] // 2) as i:
                        turn(i)

            def sum_squares(n, buf, bank=7):
                nonlocal n_sq
                for k in range(n):
                    pe.wait_ge(sem("sq_ready"), n_sq + 1)
                    pe.matmul(banks[bank][:], mean[:], buf[:, n_sq % 2, :], start=k == 0, stop=k == n - 1)\
                      .then_inc(sem("sq_used"), 1)
                    n_sq += 1

            def norm(stage):
                sum_squares(KT, sq)
                pe.wait_ge(sem("h_ready"), KT * stage)

            def row(n, count):
                return ident[0:count, n:n + 1].to_broadcast([count, P])

            pe.wait_ge(sem("set"), 1)
            sum_squares(KT, sq)
            pe.wait_ge(sem("ada_used"), 3 * KT)
            for m in range(48):
                last = pe.matmul(banks[4][:, m:m + 1], ada_acc[:, P * m:P * m + P], mean[:, 0:1], start=True, stop=True)
            last.then_inc(sem("mod_done"), 1)
            pe.wait_ge(sem("h_ready"), KT)
            pe.wait_ge(sem("gate_w_split"), 1)
            for k in range(KT):
                last = three(banks[4][:], (gw_hi[:, k, :], gw_lo[:, k, :]), (h_hi[:, k, :], h_lo[:, k, :]), k == 0, k == KT - 1)
            last.then_inc(sem("gates_done"), 1)
            product("q", h_hi, h_lo)
            product("k", h_hi, h_lo)
            for c in range(2):
                pe.wait_ge(sem("w_split"), SLAB0["v"] + c + 1)
                for m in range(2):
                    pe.wait_ge(sem("bank_free"), FREED["v"] + 2 * c + m - 1)
                    for half in range(2):
                        tok = slice(P * (2 * m + half), P * (2 * m + half + 1))
                        for k in range(KT):
                            last = three(banks[m][:, 256 * half:256 * half + 256], (h_hi[:, k, tok], h_lo[:, k, tok]),
                                         weights(c, 2 * k, 2), k == 0, k == KT - 1)
                    last.then_inc(sem("tile_done"), 1)
            product("o", h_hi, h_lo)
            product("u", h_hi, h_lo)
            pe.wait_ge(sem("consts_in"), 16)
            pe.wait_ge(sem("gate_rows"), 1)
            for t in range(TOK):
                last = pe.transpose(banks[4][:, G1 * t:G1 * t + G1], rows[0:G1, 0, P * t:P * t + P], ident[0:G1, 0:G1])
            last.then_inc(sem("a_turned"), 1)
            pe.wait_ge(sem("bank_free"), FREED["u"] + 4)
            pe.wait_ge(sem("a_col_ready"), 1)
            pe.wait_ge(sem("mean_set"), 1)
            for n in range(2 * H1):
                head, back = n // 2, n % 2
                r = 32 * back + head
                if n:
                    pe.wait_ge(sem("e1_made"), n)
                pe.matmul(banks[4][:], row(r, G1), neg_max[0:G1, :], start=True, stop=True)
                pe.matmul(banks[7][:], row(r, G1), neg_m[0:G1, :], start=True, stop=True).then_inc(sem("bc1_done"), 1)
                if not back:
                    if n:
                        pe.wait_ge(sem("p1_made"), n)
                    for j in range(TOK):
                        last = pe.matmul(banks[j][:], qk[:, 4 + head, P * j:P * j + P], qk[:, head, :], start=True, stop=True)
                    last.then_inc(sem("s1_done"), 1)
                pe.wait_ge(sem("p1_made"), n + 1)
                if n:
                    pe.wait_ge(sem("h1_made"), n)
                    pe.wait_ge(sem("root_ready"), 1 + n // 2)
                order = spans(back)[::-1] if back else spans(back)
                for bank, left in ((5, None), (6, ones)):
                    for nth, (j, lo, hi, used) in enumerate(order):
                        w = v1[:, j, DH * head:DH * head + DH] if left is None else left[:]
                        last = pe.matmul(banks[bank][:, lo:hi], w, p1[:, used:used + hi - lo], start=nth == 0, stop=nth == TOK - 1)
                last.then_inc(sem("pv1_done"), 1)
                if back:
                    sum_squares(1, sq, 5)
            pe.wait_ge(sem("pool_w_in"), 16)
            for g in range(4):
                pe.wait_ge(sem("pooled"), g + 1)
                if g >= 2:
                    pe.wait_ge(sem("y_ready"), g - 1)
                pe.matmul(banks[4 + g % 2][:], pool_w[:, g, :], mixed1[:], start=True, stop=True).then_inc(sem("pool_done"), 1)
            pe.wait_ge(sem("y_ready"), 4)
            product("out", y_hi, y_lo)
            pe.wait_ge(sem("mean_set"), 2)
            norm(2)
            for half in "ab":
                product("ff1" + half, h_hi, h_lo)
                pe.wait_ge(sem("a_ready"), 16 if half == "a" else 32)
                product("ff2" + half, a_hi, a_lo, 16)
            sum_squares(KT, sq)
            norm(3)
            product("misc", h_hi, h_lo)
            product("xbc", h_hi, h_lo)
            pe.wait_ge(sem("dt_rows"), 1)
            for t in range(TOK):
                tok = slice(P * t, P * t + P)
                pe.transpose(banks[4][:, 32 * t:32 * t + 32], drow[0:32, 3, tok], ident[0:32, 0:32])
                pe.transpose(banks[5][:, 32 * t:32 * t + 32], drow[0:32, 0, tok], ident[0:32, 0:32])
                last = pe.transpose(banks[6][:, P * t:P * t + P], mz[:, tok], ident)
            last.then_inc(sem("dt_turned"), 1)
            pe.wait_ge(sem("xbc_ready"), XS_T + BC_T)
            for n in range(TOK * 4):
                tok, quad = n // 4, n % 4
                if n >= 4:
                    pe.wait_ge(sem("xdt_made"), n - 3)
                for m in range(4):
                    last = pe.transpose(banks[n % 4][:, P * m:P * m + P], xbc[:, 4 * quad + m, P * tok:P * tok + P], ident)
                last.then_inc(sem("xs_turned"), 1)
            pe.wait_ge(sem("xdt_made"), TOK * 4)

            def running_sums(hd):
                if hd >= 2:
                    pe.wait_ge(sem("e2_made"), hd - 1)
                pe.matmul(banks[4 + hd % 2][:], row(hd, 32), acum[0:32, :], start=True, stop=True).then_inc(sem("bc2_done"), 1)

            running_sums(0)
            for hd in range(SSD_H):
                g, pair = hd // 8, hd // 2
                if hd % 8 == 0:
                    if g:
                        pe.wait_ge(sem("sm_made"), g)
                    for j, lo, hi, used in spans(0):
                        last = pe.matmul(banks[j][:, lo:hi], xbc[:, XS_T + g, P * j:P * j + P], xbc[:, XS_T + SSD_G + g, lo:hi],
                                         start=True, stop=True)
                    last.then_inc(sem("s2_done"), 1)
                if hd + 1 < SSD_H:
                    running_sums(hd + 1)
                pe.wait_ge(sem("p2_made"), hd + 1)
                if hd % 2 == 0 and pair >= 2:
                    pe.wait_ge(sem("ys_made"), pair - 1)
                out = banks[6 + pair % 2][64 * (hd % 2):64 * (hd % 2) + 64, :]
                blocks = [(j, P * j, P * j + P, P * j) for j in range(TOK)] + beside()
                for nth, (j, lo, hi, used) in enumerate(blocks):
                    last = pe.matmul(out[:, lo:hi], xdt[:, j, SSD_P * hd:SSD_P * hd + SSD_P], p2[:, hd % 2, used:used + hi - lo],
                                     start=nth == 0, stop=nth == len(blocks) - 1)
                last.then_inc(sem("pv2_done"), 1)
            product("z", h_hi, h_lo)
            pe.wait_ge(sem("mean_set"), 3)
            for g in range(SSD_G):
                sum_squares(4, sq)
            product("gates", h_hi, h_lo)
            pe.wait_ge(sem("root_used"), 8 + SSD_G)
            product("ssd", ys_hi, ys_lo, 16)
            pe.wait_ge(sem("mean_set"), 4)
            sum_squares(2, sq_l)
            pe.wait_ge(sem("mean_set"), 5)
            sum_squares(1, sq_l)
            pe.wait_ge(sem("qn_made"), 3)
            pe.wait_ge(sem("bank_free"), FREED["gates"] + 16)

            def unit(n):
                keys, tok, slot = n // 8, slice(P * (n % 4), P * (n % 4) + P), n // 4 % 2
                pe.wait_ge(sem("w_split"), SLAB0["uq"] + n // 4 + 1)
                if n >= 2:
                    pe.wait_ge(sem("unit_squared"), n - 1)
                width = S if keys else 4 * QK
                for half in range(2):
                    for k in range(1 if keys else 2):
                        first = (0 if keys else 2 * width * k) + width * half
                        kk = 2 if keys else k
                        last = three(banks[2 * (n % 2) + half][:, 0:width], (qn_hi[:, kk, tok], qn_lo[:, kk, tok]),
                                     (w_hi[:, slot, first:first + width], w_lo[:, slot, first:first + width]),
                                     k == 0, bool(keys) or k == 1)
                last.then_inc(sem("tile_done" if n % 2 else "unit_done"), 1)

            def turn_heads(n):
                pe.wait_ge(sem("heads_scaled"), n + 1)
                if n >= 2:
                    pe.wait_ge(sem("heads_ready"), n - 1)
                for hh in range(HU):
                    last = pe.transpose(banks[4 + 2 * (n % 2) + hh // 4][0:QK, P * (hh % 4):P * (hh % 4) + P],
                                        tt[:, n % 2, hh, :], ident)
                last.then_inc(sem("heads_turned"), 1)

            for n in range(16):
                unit(n)
                if n:
                    turn_heads(n - 1)
            turn_heads(15)
            pe.wait_ge(sem("heads_ready"), 16)

            def scores(hd):
                for i, lo, hi, used in spans(1):
                    if hd:
                        pe.wait_ge(sem("p3_made"), TOK * (hd - 1) + i + 1)
                    pe.matmul(banks[i][:, 0:hi], q2[0:QK, hd, P * i:P * i + P], k2[0:QK, hd, 0:hi], start=True, stop=False)
                    pe.matmul(banks[i][:, P * i:hi], mask16[:, 0, :], mask16[:, 1, :], start=False, stop=True)\
                      .then_inc(sem("s3_done"), 1)

            def turn_probabilities(hd):
                if hd:
                    pe.wait_ge(sem("pt_made"), hd)
                for i, lo, hi, used in spans(1):
                    pe.wait_ge(sem("p3_scaled"), TOK * hd + i + 1)
                    for j in range(i + 1):
                        bank, first = ((4, 0), (5, 0), (6, 0), (5, 384))[j]
                        last = pe.transpose(banks[bank][:, first + P * (i - j):first + P * (i - j) + P],
                                            p3[hd % 2][:, used + P * j:used + P * j + P], ident)
                last.then_inc(sem("p3_turned"), 1)

            def weighted_values(hd):
                pair = hd // 2
                pe.wait_ge(sem("pt_made"), hd + 1)
                if hd % 2 == 0 and pair:
                    pe.wait_ge(sem("att_made"), pair)
                out = banks[7][64 * (hd % 2):64 * (hd % 2) + 64, :]
                for j, lo, hi, used in spans(0):
                    last = pe.matmul(out[:, lo:hi], v2[:, j, VD * hd:VD * hd + VD], pt[hd % 2][:, used:used + hi - lo],
                                     start=j == 0, stop=j == TOK - 1)
                last.then_inc(sem("pv3_done"), 1)

            pe.wait_ge(sem("mask_made"), 1)
            for step in range(QH + 2):
                if step < QH:
                    scores(step)
                if 1 <= step <= QH:
                    turn_probabilities(step - 1)
                if step >= 2:
                    weighted_values(step - 2)
            pe.wait_ge(sem("att_made"), 8)
            product("mla", att[:, 0:16:2, :], att[:, 1:16:2, :])
            pe.wait_ge(sem("mm_made"), 8)
            product("wo", mm_hi, mm_lo)
            pe.wait_ge(sem("mean_set"), 6)
            norm(4)
            product("upa", h_hi, h_lo)
            pe.wait_ge(sem("fa_made"), 16)
            product("downa", a_hi, a_lo, 16)
            product("upb", h_hi, h_lo)
            pe.wait_ge(sem("fa_made"), UP_T)
            product("downb", a_hi, a_lo, UP_T - 16)


def kernel(**inputs):
    import concourse.bacc as bacc
    from concourse.bass_utils import run_bass_kernel_spmd

    f = {name: np.asarray(a) for name, a in inputs.items()}
    one = {name: (a[0] if name not in ("x", "c", "g_final") else a) for name, a in f.items()}

    def pairs(w):
        n = w.shape[1] // 256
        kt = w.shape[0] // P
        out = np.zeros((n, P, 2, KT, P), w.dtype)
        out[:, :, :, :kt] = w.reshape(kt, P, n, 2, P).transpose(2, 1, 3, 0, 4)
        return out.reshape(n, P, SLAB)

    def wides(w):
        return w.reshape(16, P, KT, P).transpose(2, 1, 0, 3).reshape(KT, P, SLAB)

    def tiles(a):
        return a.reshape(-1, P).T

    w_in, w_in2 = one["w_in"], one["w_in_2"]
    dm = H1 * DH
    gate0 = 4 * dm
    u0 = gate0 + 16
    by_token = w_in[:, 2 * dm:3 * dm].reshape(KT, P, 2, 256).transpose(2, 1, 0, 3).reshape(2, P, SLAB)
    xbc0, dt0 = 2048, 5120
    qa0, kr0 = dt0 + 32, dt0 + 32 + 384
    misc = np.zeros((D, 4 * P), w_in2.dtype)
    misc[:, 0:384] = w_in2[:, qa0:qa0 + 384]
    misc[:, 384:416] = w_in2[:, dt0:dt0 + 32]
    misc[:, 448:480] = w_in2[:, kr0:kr0 + 32]
    up = one["w_up_2"].reshape(D, 2, UP_T, P).transpose(0, 2, 1, 3).reshape(D, 2 * UP_T * P)
    down, ff1, ff2 = one["w_down_2"], one["w_ff1"], one["w_ff2"]
    uq = np.zeros((2, P, SLAB), w_in.dtype)
    uq[:, :, 0:1536] = one["w_uq_2"].reshape(2, P, 2, 768).transpose(2, 1, 0, 3).reshape(2, P, 1536)
    ukv = np.zeros((2, P, SLAB), w_in.dtype)
    ukv[:, :, 0:1024] = one["w_ukv_2"].reshape(P, 2, 1024).transpose(1, 0, 2)
    parts = {"q": pairs(w_in[:, 0:dm]), "k": pairs(w_in[:, dm:2 * dm]), "v": by_token, "o": pairs(w_in[:, 3 * dm:4 * dm]),
             "u": pairs(w_in[:, u0:]), "out": pairs(one["w_out"]),
             "ff1a": pairs(ff1[:, 0:2048]), "ff1b": pairs(ff1[:, 2048:]), "ff2a": wides(ff2[0:2048]), "ff2b": wides(ff2[2048:]),
             "misc": pairs(misc), "xbc": pairs(w_in2[:, xbc0:dt0]), "z": pairs(w_in2[:, 0:2048]), "gates": pairs(w_in2[:, kr0 + 32:]),
             "ssd": wides(one["w_ssd_proj_2"]), "uq": uq, "ukv": ukv, "mla": pairs(one["w_mla_proj_2"]), "wo": pairs(one["w_o_2"]),
             "upa": pairs(up[:, 0:16 * 256]), "upb": pairs(up[:, 16 * 256:]), "downa": wides(down[0:2048]), "downb": pairs(down[2048:])}
    slabs = np.concatenate([parts[name] for name, _ in PHASES])
    gate_w = np.zeros((P, KT, P), w_in.dtype)
    gate_bias = np.zeros((P, 1), w_in.dtype)
    for d in range(2):
        for g, name in enumerate(("b_igate", "b_fgate")):
            first = 64 * g + 32 * d
            c0 = gate0 + 8 * d + 4 * g
            gate_w[:, :, first:first + H1] = w_in[:, c0:c0 + H1].reshape(KT, P, H1).transpose(1, 0, 2)
            gate_bias[first:first + H1, 0] = one[name][d]

    def rows32(a):
        out = np.zeros((P, 1), a.dtype)
        out[0:32, 0] = a
        return out

    convf_w = one["conv_ffn_w_2"].reshape(TAPS_F, 2, UP_T, P).transpose(3, 2, 1, 0).reshape(P, 2 * UP_T * TAPS_F)
    convf_b = one["conv_ffn_b_2"].reshape(2, UP_T, P).transpose(2, 1, 0).reshape(P, 2 * UP_T)
    by_name = {"c": tiles(f["c"][0]), "b_ada": tiles(one["b_ada"]), "g_mix": tiles(one["g_mix"]), "gate_bias": gate_bias,
               "g_head": tiles(one["g_head"]), "pool_scale": tiles(one["pool_scale"]), "g_ffn": tiles(one["g_ffn"]),
               "g_final": tiles(f["g_final"]), "g_mix2": tiles(one["norm_mix_g_2"]),
               "conv_w": one["conv_ssd_w_2"].reshape(TAPS, 24, P).transpose(2, 1, 0).reshape(P, 96),
               "conv_b": tiles(one["conv_ssd_b_2"]), "dt_bias": rows32(one["dt_bias_2"]), "a_log": rows32(one["a_log_2"]),
               "d_skip": tiles(np.repeat(one["d_skip_2"], SSD_P)), "ssd_g": tiles(one["ssd_norm_g_2"]),
               "qa_g": tiles(one["q_a_norm_g_2"]), "kva_g": tiles(one["kv_a_norm_g_2"]), "gate_b": tiles(one["gate_b_2"]),
               "g_ffn2": tiles(one["norm_ffn_g_2"]), "convf_w": convf_w, "convf_b": convf_b}
    cols = np.concatenate([by_name[name] for name in COLS], axis=1)
    ada = one["w_ada"].reshape(KT, P, 3, 2048).transpose(2, 0, 1, 3).reshape(3 * KT, P, 2048)
    x_t = f["x"][0].T.reshape(KT, P, S).transpose(1, 0, 2)
    at = np.arange(P)
    consts = np.stack([np.eye(P), at[None, :] >= at[:, None], at[None, :] <= at[:, None],
                       np.where(at[None, :] <= at[:, None], 0.0, -1e30)], 1).astype(np.float32)
    t = np.arange(S)
    sizes = [np.clip(t + n // 2, 0, S) - np.clip(t - n // 2, 0, S) for n in WINDOWS]
    inv = np.broadcast_to(1.0 / np.array(sizes, np.float32), (P, 4, S))
    freq = (1.0 / (10000.0 ** (np.arange(0, ROPE, 2, dtype=np.float32) / np.float32(ROPE)))).astype(np.float32)
    angle = t.astype(np.float32)[:, None] * freq[None, :]
    rope = np.stack([np.cos(angle), np.sin(angle)]).reshape(2, TOK, P, ROPE // 2).transpose(2, 0, 1, 3)
    qk_g = np.broadcast_to(np.stack([one["q_norm_g_2"], one["k_norm_g_2"]]), (P, 2, QK))
    pool_w = one["w_pool"].transpose(1, 0, 2)
    arrays = {"x_in": x_t, "slabs": slabs, "ada": ada, "cols": cols, "gate_w": gate_w, "pool_w": pool_w, "consts": consts,
              "inv": inv, "rope": rope, "qk_g": qk_g}
    arrays = {name: np.ascontiguousarray(a) for name, a in arrays.items()}
    nc = bacc.Bacc("TRN2", target_bir_lowering=False, num_devices=1)
    drams = [nc.dram_tensor(name, a.shape, mybir.dt.from_np(a.dtype), kind="ExternalInput").ap() for name, a in arrays.items()]
    out = nc.dram_tensor("out", (P, KT, S), mybir.dt.float32, kind="ExternalOutput").ap()
    build(nc, *drams, out)
    got = run_bass_kernel_spmd(nc, [arrays], core_ids=[0]).results[0]["out"]
    return np.ascontiguousarray(np.asarray(got).transpose(2, 1, 0).reshape(1, S, D))
```

```python
import numpy as np
import concourse.bass as bass
import concourse.mybir as mybir

P = 128
S = 512
D = 1024
KT = D // P
TOK = S // P
EPS = 1e-6
H1, DH = 4, 128
G1 = 36
WINDOWS = (2, 4, 8, 16)
SSD_H, SSD_P, SSD_G, XS_T, BC_T, TAPS = 32, 64, 4, 16, 8, 4
QH, QK, NOPE, ROPE, VD = 16, 96, 64, 32, 64
HU = 8
UP_T, TAPS_F = 22, 3
PAD = 8
SLAB = 16 * P

PHASES = [("u", 2), ("q", 2), ("k", 2), ("v", 2), ("o", 2), ("out", 4), ("ff1a", 8), ("ff2a", 8), ("ff1b", 8),
          ("ff2b", 8), ("misc", 2), ("xbc", 12), ("z", 8), ("gates", 8), ("ssd", 8), ("uq", 2), ("ukv", 2),
          ("mla", 4), ("wo", 4), ("upa", 16), ("downa", 8), ("upb", 6), ("downb", 4)]
WIDE = ("ff2a", "ff2b", "ssd", "downa")
OWN_BANKS = ("uq", "ukv")
SLAB0, SLABS, FREED, N_SLABS, _freed, _freed_wide = {}, {}, {}, 0, 0, 2
for _name, _n in PHASES:
    SLAB0[_name], SLABS[_name] = N_SLABS, _n
    N_SLABS += _n
    if _name in WIDE:
        FREED[_name], _freed_wide = _freed_wide, _freed_wide + _n
    elif _name not in OWN_BANKS:
        FREED[_name], _freed = _freed, _freed + 2 * _n

COLS, N_COLS = {}, 0
for _name, _n in [("c", 8), ("b_ada", 48), ("g_mix", 8), ("gate_bias", 1), ("g_head", 4), ("pool_scale", 4),
                  ("g_ffn", 8), ("g_final", 8), ("g_mix2", 8), ("conv_w", 96), ("conv_b", 24), ("dt_bias", 1),
                  ("a_log", 1), ("d_skip", 16), ("ssd_g", 16), ("qa_g", 2), ("kva_g", 1),
                  ("gate_b", 16), ("g_ffn2", 8), ("convf_w", 132), ("convf_b", 44)]:
    COLS[_name] = N_COLS
    N_COLS += _n
SH1, SC1, GT1, SH2, SC2, GT2 = (8 * n for n in range(6))


def build(nc, x_d, slabs_d, ada_d, cols_d, gate_w_d, pool_w_d, consts_d, inv_d, rope_d, qkg_d, out_d):
    f32, f32r, bf16 = mybir.dt.float32, mybir.dt.float32r, mybir.dt.bfloat16
    ALU, ACT, AX = mybir.AluOpType, mybir.ActivationFunctionType, mybir.AxisListType
    base = (nc.sbuf_base + 31) // 32 * 32
    K = 1024

    def at(name, shape, dt, offset):
        return nc.alloc_sbuf_tensor_at(name, [P] + shape, dt, offset=base + offset)

    x = at("x", [KT, S], f32, 0)
    raw = at("raw", [2, SLAB], f32, 16 * K)
    w_hi = at("w_hi", [2, SLAB], f32r, 32 * K)
    w_lo = at("w_lo", [2, SLAB], f32r, 48 * K)
    h = at("h", [2 * KT, S], f32r, 64 * K)
    h_hi, h_lo = h[:, 0:KT, :], h[:, KT:, :]
    A = 96 * K
    Z = A + 106 * K
    cols = at("cols", [N_COLS], f32, Z)
    consts = at("consts", [4, P], f32, Z + 1920)
    ident, keep_up, keep_low, causal = (consts[:, n, :] for n in range(4))
    mask16 = at("mask16", [2, P], bf16, Z + 1920 + 3 * 4 * P)
    mask16_made = at("mask16_made", [2, P], bf16, A + 103 * K)
    ident16, causal16 = mask16[:, 0, :], mask16[:, 1, :]
    mod = at("mod", [48], f32, Z + 3968)
    gain = at("gain", [16], f32, Z + 4160)
    small = at("small", [16], f32, Z + 4224)
    eps, c_act = small[:, 0:1], small[:, 8:16]
    mean = at("mean", [P], f32, Z + 4288)
    ones = at("ones", [P], f32, Z + 4800)
    kr_col = at("kr_col", [TOK, ROPE], f32, Z + 5312)
    sq = at("sq", [2, S], f32, A + 93 * K)
    rs = at("rs", [S], f32, A + 97 * K)
    t0 = at("t0", [S], f32, A + 99 * K)
    t1 = at("t1", [S], f32, A + 101 * K)
    ada_w = at("ada_w", [6, 2048], f32, A)
    ada_acc = at("ada_acc", [48 * P], f32, A + 53 * K)
    UW = S + 2 * PAD
    qk = at("qk", [8, S], f32, A)
    v1 = at("v1", [TOK, S], f32, A + 16 * K)
    og = at("og", [4, S], f32, A + 24 * K)
    u = at("u", [4, UW], f32, A + 32 * K)
    gw = at("gw", [KT, P], f32, A + 77 * K)
    gw_hi = at("gw_hi", [KT, P], f32r, A + 81 * K)
    gw_lo = at("gw_lo", [KT, P], f32r, A + 85 * K)
    win = at("win", [2, UW], f32, A + 41 * K)
    mixed1 = at("mixed1", [4, S], f32, A + 77 * K)
    p1 = at("p1", [2, 1280], f32, A + 41 * K)
    y_hi = at("y_hi", [8, S], f32r, A + 53 * K)
    y_lo = at("y_lo", [8, S], f32r, A + 69 * K)
    rows = at("rows", [4, S], f32, A + 85 * K)
    hm = at("hm", [H1, S], f32, A + 69 * K)
    den1 = at("den1", [S], f32, A + 87 * K)
    floor1 = at("floor1", [2, S], f32, A + 89 * K)
    rs_h = at("rs_h", [H1, S], f32, A + 85 * K)
    inv = at("inv", [4, S], f32, A + 69 * K)
    neg_max = at("neg_max", [S], f32, A + 103 * K)
    neg_m = at("neg_m", [S], f32, A + 99 * K)
    a_col = at("a_col", [TOK, G1], f32, A + 40 * K + 256)
    pool_w = at("pool_w", [4, P], f32, A + 51 * K)
    a_hi = at("a_hi", [16, S], f32r, A)
    a_lo = at("a_lo", [16, S], f32r, A + 32 * K)
    relu = at("relu", [2, S], f32, A + 64 * K)
    asq = at("asq", [S], f32, A + 68 * K)
    xbc = at("xbc", [XS_T + BC_T, S], f32, A)
    qa = at("qa", [3, S], f32, A + 48 * K)
    mz = at("mz", [S], f32, A + 54 * K)
    xdt = at("xdt", [TOK, SSD_H * SSD_P], f32, A + 56 * K)
    cpad = at("cpad", [2, S + 4], f32, A + 56 * K)
    cacc = at("cacc", [2, S], f32, A + 62 * K)
    sm = at("sm", [1280], f32, A + 88 * K)
    p2 = at("p2", [2, 1280], f32, A + 93 * K)
    drow = at("drow", [4, S], f32, A + 88 * K)
    acum = at("acum", [S], f32, A + 103 * K)
    nac_col = at("nac_col", [TOK, SSD_H], f32, A + 105 * K)
    dt_col = at("dt_col", [TOK, SSD_H], f32, A + 105 * K + 512)
    rope = at("rope", [2, TOK, ROPE // 2], f32, A + 87 * K)
    qk_g = at("qk_g", [2, QK], f32, A + 104 * K)
    zt = at("zt", [S], f32, A + 54 * K)
    ys_hi = at("ys_hi", [XS_T, S], f32r, A + 56 * K)
    ys_lo = at("ys_lo", [XS_T, S], f32r, A)
    mix = at("mix", [8, S], f32, A + 32 * K)
    gm = at("gm", [8, S], f32, A + 88 * K)
    q2 = at("q2", [QH, S], f32, 64 * K)
    k2 = at("k2", [QH, S], f32, A)
    v2 = at("v2", [TOK, QH * VD], f32, A + 56 * K)
    qn_hi = at("qn_hi", [3, S], f32r, A + 72 * K)
    qn_lo = at("qn_lo", [3, S], f32r, A + 78 * K)
    tt = at("tt", [2, HU, QK], f32, A + 48 * K)
    tsq = at("tsq", [HU, QK], f32, A + 84 * K)
    trope = at("trope", [4, HU, ROPE // 2], f32, A + 54 * K)
    stat = at("stat", [3, HU], f32, A + 87 * K + 512)
    p3 = [at(f"p3_{n}", [1280], f32, A + (72, 48)[n] * K) for n in range(2)]
    pt = [at(f"pt_{n}", [1280], f32, A + (77, 82)[n] * K) for n in range(2)]
    mx = at("mx", [2, 3, TOK], f32, A + 87 * K + 640)
    att = at("att", [QH, S], f32r, 64 * K)
    ao = at("ao", [S], f32, A + 53 * K)
    mt = at("mt", [S], f32, A + 84 * K)
    mm_hi = at("mm_hi", [8, S], f32r, A)
    mm_lo = at("mm_lo", [8, S], f32r, A + 16 * K)
    sq_l = at("sq_l", [2, S], f32, A + 56 * K)
    rs_l = at("rs_l", [S], f32, A + 60 * K)
    t0_l = at("t0_l", [S], f32, A + 62 * K)
    t1_l = at("t1_l", [S], f32, A + 64 * K)
    fpad = at("fpad", [2, S + 4], f32, A + 64 * K)
    facc = at("facc", [2, S], f32, A + 70 * K)
    fgate = at("fgate", [S], f32, A + 74 * K)
    fa = at("fa", [S], f32, A + 76 * K)

    banks = [nc.alloc_psum_tensor(f"bank{n}", [P, S], f32) for n in range(8)]
    sems = {}

    def sem(name):
        if name not in sems:
            sems[name] = nc.alloc_semaphore(name)
        return sems[name]

    def col(name, n=0, first=0, rows=P):
        return cols[first:first + rows, bass.ds(COLS[name] + n, 1)]

    class Steps:

        def __init__(self, eng, name):
            self.eng, self.sem, self.n, self.turn, self.per = eng, sem(name), 0, 0, 0

        def __call__(self, ins):
            self.n += 1
            ins.then_inc(self.sem, 1)
            self.eng.wait_ge(self.sem, self.per * self.turn + self.n)

        def tell(self, ins, name, value):
            ins.then_inc(sem(name), 1)
            self.eng.wait_ge(sem(name), value)

        def loop(self, turn, per):
            self.turn, self.per, self.start = turn, per, self.n

        def end(self, turns):
            assert self.n - self.start == self.per, (self.n - self.start, self.per)
            self.n, self.turn, self.per = self.start + self.per * turns, 0, 0

    def spans(back):
        out, used = [], 0
        for j in range(TOK):
            lo, hi = (0, P * (j + 1)) if back else (P * j, S)
            out.append((j, lo, hi, used))
            used += hi - lo
        return out

    def paired(back):
        out, used = [], 0
        for j in (1, 0, 2, 3) if back else (0, 1, 3, 2):
            lo, hi = (0, P * (j + 1)) if back else (P * j, S)
            out.append((j, lo, hi, used))
            used += hi - lo
        return out

    def diagonals(a, back):
        first, wide = (P, a[:, 2 * P:]) if back else (7 * P, a[:, 0:8 * P])
        wide = wide.rearrange("p (r c) -> p r c", r=2)
        near = a[:, first:first + 2 * P].rearrange("p (r c) -> p r c", r=2)
        far = wide[:, :, 3 * P:] if back else wide[:, :, 0:P]
        return far, near

    pool_banks, head_banks = [banks[n] for n in (5, 6, 7, 5)], [banks[n] for n in (4, 7, 2, 3)]

    def score_place(j):
        return ((1, 0), (2, 0), (3, 0), (3, 256))[j]

    block = nc.Block()
    with block:
        @block.sync
        def _(sp):
            sp.dma_start(cols[:], cols_d).then_inc(sem("cols_in"), 16)
            for k in range(0, KT, 4):
                sp.dma_start(x[:, k:k + 4, :], x_d[:, k:k + 4, :]).then_inc(sem("x_in"), 16)
            sp.dma_start(consts[:], consts_d).then_inc(sem("consts_in"), 16)
            sp.dma_start(gw[:], gate_w_d).then_inc(sem("gate_w_in"), 16)
            sp.dma_start(pool_w[:], pool_w_d).then_inc(sem("pool_w_in"), 16)
            for slot in range(2):
                sp.dma_start(raw[:, slot, :], slabs_d[slot, :, :]).then_inc(sem(f"raw_in{slot}"), 16)
            with sp.Fori(1, N_SLABS // 2) as i:
                for slot in range(2):
                    sp.wait_ge(sem("w_split"), 2 * i + slot - 1)
                    sp.dma_start(raw[:, slot, :], slabs_d[2 * i + slot, :, :]).then_inc(sem(f"raw_in{slot}"), 16)
            for m in range(KT):
                sp.wait_ge(sem("x_final"), m + 1)
                sp.dma_start(out_d[:, m, :], x[:, m, :]).then_inc(sem("out_sent"), 16)
            sp.wait_ge(sem("out_sent"), 16 * KT)

        @block.gpsimd
        def _(pool):
            def split(slot, nth):
                pool.tensor_tensor(w_hi[:, slot, :], raw[:, slot, :], ones[:, 0:1].to_broadcast([P, SLAB]),
                                   ALU.mult).then_inc(sem("w_head"), 1)
                pool.wait_ge(sem("w_head"), nth)
                pool.tensor_tensor(w_lo[:, slot, :], raw[:, slot, :], w_hi[:, slot, :].bitcast(f32),
                                   ALU.subtract).then_inc(sem("w_split"), 1)

            pool.wait_ge(sem("set"), 1)
            for slot in range(2):
                pool.wait_ge(sem(f"raw_in{slot}"), 16)
                split(slot, slot + 1)
            with pool.Fori(1, N_SLABS // 2) as i:
                for slot in range(2):
                    pool.wait_ge(sem(f"raw_in{slot}"), 16 * i + 16)
                    pool.wait_ge(sem("tile_done"), 4 * i + 2 * slot - 2)
                    pool.wait_ge(sem("w_split"), 2 * i + slot - 1)
                    split(slot, 2 * i + slot + 1)

        @block.scalar
        def _(act):
            do = Steps(act, "act_step")
            n_sq, n_root = 0, 0

            def fn(out, in_, f, **kw):
                return act.activation(out, in_, f, **kw)

            def tile_ready(name, t):
                act.wait_ge(sem("tile_done"), 2 * SLAB0[name] + t + 1)

            def free(ins, name, t):
                do.tell(ins, "bank_free", FREED[name] + t + 1)

            def squares(tiles, buf):
                nonlocal n_sq
                for tile in tiles:
                    if n_sq >= 2:
                        act.wait_ge(sem("sq_used"), n_sq - 1)
                    n_sq += 1
                    do.tell(fn(buf[:, (n_sq - 1) % 2, :], tile, ACT.Square), "sq_ready", n_sq)

            def root(buf):
                nonlocal n_root
                act.wait_ge(sem("sq_used"), n_sq)
                if n_root:
                    act.wait_ge(sem("root_used"), n_root)
                n_root += 1
                do.tell(fn(buf[:], banks[7][:], ACT.Sqrt, bias=eps), "root_ready", n_root)

            def norm():
                squares([x[:, k, :] for k in range(KT)], sq)
                root(rs)

            def heads(stage, shift=None):
                for k in range(KT):
                    n = KT * (stage - 1) + k + 1
                    act.wait_ge(sem("h_scaled"), n)
                    src = (t0, t1)[k % 2]
                    if shift is None:
                        do.tell(fn(h_hi[:, k, :], src[:], ACT.Copy), "h_head", n)
                    else:
                        do.tell(fn(h_hi[:, k, :], src[:], ACT.Identity, bias=mod[:, shift + k:shift + k + 1]), "h_head", n)

            for n in range(3 * KT):
                if n >= 6:
                    act.wait_ge(sem("ada_used"), n - 5)
                act.dma_start(ada_w[:, n % 6, :], ada_d[n, :, :]).then_inc(sem(f"ada_in{n % 6}"), 16)
                if n == 5:
                    act.wait_ge(sem("cols_in"), 16)
                    act.wait_ge(sem("set"), 1)
                    do.tell(fn(c_act, cols[:, COLS["c"]:COLS["c"] + KT], ACT.Silu), "c_ready", 1)
            act.wait_ge(sem("x_in"), 32)
            norm()
            heads(1, SH1)
            act.dma_start(inv[:], inv_d).then_inc(sem("inv_in"), 16)
            act.wait_ge(sem("gates_done"), 1)
            do(fn(rows[0:G1, 0, :], banks[4][0:G1, :], ACT.Identity, bias=col("gate_bias", 0, 0, G1)))
            do.tell(fn(rows[0:G1, 1, :], banks[4][64:64 + G1, :], ACT.Identity, bias=col("gate_bias", 0, 64, G1)),
                    "gates_biased", 1)
            act.wait_ge(sem("gate_negabs"), 1)
            do.tell(fn(rows[0:G1, 2, :], rows[0:G1, 2, :], ACT.Exp), "gate_exp", 1)
            act.wait_ge(sem("gate_onep"), 1)
            do.tell(fn(neg_m[0:G1, :], rows[0:G1, 3, :], ACT.Ln), "gate_ln", 1)
            act.wait_ge(sem("u_zeroed"), 1)
            for t in range(4):
                tile_ready("u", t)
                free(fn(u[:, t, PAD:PAD + S], banks[t % 2][:], ACT.Copy), "u", t)
            for name, first, scale in (("q", 0, DH ** -0.5), ("k", 4, 1.0)):
                for t in range(4):
                    tile_ready(name, t)
                    free(fn(qk[:, first + t, :], banks[t % 2][:], ACT.Copy, scale=scale), name, t)
                if name == "q":
                    act.wait_ge(sem("a_turned"), 1)
                    do.tell(fn(a_col[:], banks[4][:, 0:TOK * G1].rearrange("p (t g) -> p t g", t=TOK), ACT.Copy),
                            "a_col_ready", 1)
            for c in range(2):
                for m in range(2):
                    tile_ready("v", 2 * c + m)
                    free(fn(v1[:, 2 * m:2 * m + 2, 256 * c:256 * c + 256],
                            banks[m][:].rearrange("p (t e) -> p t e", t=2), ACT.Copy), "v", 2 * c + m)
            for n in range(2 * H1):
                head, back = n // 2, n % 2
                r = 32 * back + head
                act.wait_ge(sem("bc1_done"), n + 1)
                if n >= 2:
                    act.wait_ge(sem("h1_made"), n - 1)
                for j, lo, hi, used in paired(back):
                    do(fn(p1[:, back, used:used + hi - lo], banks[4][:, lo:hi], ACT.Exp, bias=a_col[:, j, r:r + 1]))
                do.tell(fn(floor1[:, back, :], banks[7][:], ACT.Exp), "e1_made", n + 1)
            for head in range(H1):
                act.wait_ge(sem("hm_made"), head + 1)
                squares([hm[:, head, :]], sq)
            act.wait_ge(sem("sq_used"), n_sq)
            for head in range(H1):
                do.tell(fn(rs_h[:, head, :], head_banks[head][:], ACT.Sqrt, bias=eps), "head_root", head + 1)
            for t in range(4):
                tile_ready("o", t)
                free(fn(og[:, t, :], banks[t % 2][:], ACT.Sigmoid), "o", t)
            act.wait_ge(sem("x_ready"), 1)
            norm()
            heads(2, SH2)
            for half, name in enumerate(("ff1a", "ff1b")):
                with act.Fori(0, SLABS[name] // 2) as i:
                    for t in range(4):
                        act.wait_ge(sem("tile_done"), 4 * i + 2 * SLAB0[name] + t + 1)
                        if half or t >= 2:
                            act.wait_ge(sem("relu_used"), 4 * i + 16 * half + t - 1)
                        else:
                            act.wait_ge(sem("relu_used"), 4 * i + t)
                        do.tell(fn(relu[:, t % 2, :], banks[t % 2][:], ACT.Relu), "bank_free", 4 * i + FREED[name] + t + 1)
            for after in (2, 3):
                act.wait_ge(sem("x_ready"), after)
                norm()
            heads(3)
            for t in range(4):
                tile_ready("misc", t)
                free(fn(qa[:, t, :] if t < 3 else mz[:], banks[t % 2][:], ACT.Copy), "misc", t)
            act.wait_ge(sem("dt_negabs"), 1)
            do.tell(fn(drow[0:32, 1, :], drow[0:32, 1, :], ACT.Exp), "dt_exp", 1)
            act.wait_ge(sem("dt_onep"), 1)
            do(fn(small[0:32, 1:2], col("a_log", 0, 0, 32), ACT.Exp))
            do.tell(fn(drow[0:32, 3, :], drow[0:32, 2, :], ACT.Ln), "dt_ln", 1)
            act.wait_ge(sem("cpad_zeroed"), 1)
            name = "xbc"
            with act.Fori(0, SLABS[name] // 2) as i:
                for t in range(4):
                    act.wait_ge(sem("tile_done"), 4 * i + 2 * SLAB0[name] + t + 1)
                    if t >= 2:
                        act.wait_ge(sem("conv_done"), 4 * i + t - 1)
                    else:
                        act.wait_ge(sem("conv_done"), 4 * i)
                    do.tell(fn(cpad[:, t % 2, TAPS - 1:TAPS - 1 + S], banks[t % 2][:], ACT.Copy), "bank_free",
                            4 * i + FREED[name] + t + 1)
                    act.wait_ge(sem("conv_done"), 4 * i + t + 1)
                    do.tell(fn(xbc[:, 4 * i + t, :], cacc[:, t % 2, :], ACT.Silu), "xbc_ready", 4 * i + t + 1)
            act.wait_ge(sem("dt_turned"), 1)
            for b, place in ((4, nac_col), (5, dt_col)):
                do(fn(place[:], banks[b][:, 0:P].rearrange("p (t g) -> p t g", t=TOK), ACT.Copy))
            do.tell(fn(kr_col[:], banks[6][:].rearrange("p (t g) -> p t g", t=TOK)[:, :, 64:64 + ROPE], ACT.Copy),
                    "dt_col_ready", 1)
            def half_tanh(pair):
                act.wait_ge(sem("tile_done"), 2 * SLAB0["z"] + pair + 1)
                if pair:
                    act.wait_ge(sem("z_used"), pair)
                do.tell(fn(zt[:], banks[0][:], ACT.Tanh, scale=0.5), "z_tanh", pair + 1)

            for hd in range(SSD_H):
                act.wait_ge(sem("diagonal_made"), hd + 1)
                e2 = p2[:, hd % 2, :]
                for j, lo, hi, used in paired(0):
                    if j < TOK - 1:
                        do(fn(e2[:, used + P:used + hi - lo], banks[4 + hd % 2][:, lo + P:hi], ACT.Exp, bias=nac_col[:, j, hd:hd + 1]))
                two, two_more = diagonals(e2, 0)
                do(fn(two, two, ACT.Exp))
                do.tell(fn(two_more, two_more, ACT.Exp), "e2_made", hd + 1)
                if hd % 2 == 0 and hd:
                    half_tanh(hd // 2 - 1)
            half_tanh(XS_T - 1)
            act.wait_ge(sem("z_used"), XS_T)
            for g in range(SSD_G):
                squares([xbc[:, 4 * g + k, :] for k in range(4)], sq)
                root(rs)
            act.wait_ge(sem("root_used"), 4 + SSD_G)
            for t in range(16):
                tile_ready("gates", t)
                free(fn(mix[:, t, :] if t < 8 else gm[:, t - 8, :], banks[t % 2][:], ACT.Sigmoid, bias=col("gate_b", t)),
                     "gates", t)
            act.wait_ge(sem("mix_made"), 8)
            act.dma_start(rope[:], rope_d).then_inc(sem("rope_in"), 16)
            act.dma_start(qk_g[:], qkg_d).then_inc(sem("rope_in"), 16)
            squares([qa[:, k, :] for k in range(2)], sq_l)
            root(rs_l)
            squares([qa[:, 2, :]], sq_l)
            root(rs_l)
            def unit_in(n):
                keys, c, tok = n // 8, n // 4 % 2, n % 4
                if n % 2:
                    act.wait_ge(sem("tile_done"), 2 * (SLAB0["uq"] + n // 4) + n % 4 // 2 + 1)
                else:
                    act.wait_ge(sem("unit_done"), n // 2 + 1)
                if n >= 2:
                    act.wait_ge(sem("heads_turned"), n - 1)
                for half in range(2):
                    bank = banks[2 * (n % 2) + half]
                    part = slice(4 * half, 4 * half + 4)
                    if keys:
                        src = bank[:].rearrange("p (h e) -> p h e", h=4)
                        do(fn(tt[:, n % 2, part, 0:NOPE], src[:, :, 0:NOPE], ACT.Copy))
                        h0 = VD * (8 * c + 4 * half)
                        do(fn(v2[:, tok, h0:h0 + 4 * VD].rearrange("p (h e) -> p h e", h=4), src[:, :, NOPE:], ACT.Copy))
                        do(fn(tt[:, n % 2, part, NOPE:QK],
                              kr_col[:, tok, :].unsqueeze(1).to_broadcast([P, 4, ROPE]), ACT.Copy))
                    else:
                        do(fn(tt[:, n % 2, part, :], bank[:, 0:4 * QK].rearrange("p (h e) -> p h e", h=4), ACT.Copy))
                do.tell(fn(tsq[:], tt[:, n % 2, :, :], ACT.Square), "unit_squared", n + 1)

            def unit_out(n):
                keys, c, tok = n // 8, n // 4 % 2, n % 4
                act.wait_ge(sem("heads_turned"), n + 1)
                for half in range(2):
                    h0 = 8 * c + 4 * half
                    ins = fn((k2 if keys else q2)[0:QK, h0:h0 + 4, P * tok:P * tok + P],
                             banks[4 + 2 * (n % 2) + half][0:QK, :].rearrange("p (h t) -> p h t", h=4), ACT.Copy)
                    if half:
                        do.tell(ins, "heads_ready", n + 1)
                    else:
                        do(ins)

            act.wait_ge(sem("qn_made"), 3)
            for n in range(16):
                unit_in(n)
                if n:
                    unit_out(n - 1)
                act.wait_ge(sem("unit_summed"), n + 1)
                do.tell(fn(stat[:, 1, :], stat[:, 0, :], ACT.Sqrt, scale=1.0 / QK, bias=eps), "unit_root", n + 1)
            unit_out(15)
            for step in range(QH + 1):
                if step < QH:
                    hd = step
                    if hd >= 2:
                        act.wait_ge(sem("p3_turned"), hd - 1)
                    for i, lo, hi, used in spans(1):
                        act.wait_ge(sem("max_made"), TOK * hd + i + 1)
                        do.tell(fn(p3[hd % 2][:, used:used + hi], banks[i][:, 0:hi], ACT.Exp, scale=QK ** -0.5,
                                   bias=mx[:, hd % 2, 1, i:i + 1], accum_out=mx[:, hd % 2, 2, i:i + 1]),
                                "p3_made", TOK * hd + i + 1)
                if step:
                    hd = step - 1
                    place = pt[hd % 2]
                    act.wait_ge(sem("p3_turned"), hd + 1)
                    if hd >= 2:
                        act.wait_ge(sem("pv3_done"), hd - 1)
                    do(fn(place[:, 0:S], banks[4][:], ACT.Copy))
                    do(fn(place[:, S:S + 384], banks[5][:, 0:384], ACT.Copy))
                    do(fn(place[:, S + 384:S + 640], banks[6][:, 0:256], ACT.Copy))
                    do.tell(fn(place[:, S + 640:], banks[5][:, 384:S], ACT.Copy), "pt_made", hd + 1)
            act.wait_ge(sem("x_ready"), 4)
            norm()
            heads(4)
            act.wait_ge(sem("fpad_zeroed"), 1)
            for name, done in (("upa", 0), ("upb", 16)):
                with act.Fori(0, SLABS[name] // 2) as i:
                    for slot in range(2):
                        for m in range(2):
                            t = 2 * slot + m
                            act.wait_ge(sem("tile_done"), 4 * i + 2 * SLAB0[name] + t + 1)
                            act.wait_ge(sem("fa_made"), 2 * i + done + slot)
                            do.tell(fn(fpad[:, m, TAPS_F - 1:TAPS_F - 1 + S], banks[m][:], ACT.Copy), "bank_free",
                                    4 * i + FREED[name] + t + 1)
                        act.wait_ge(sem("fconv_done"), 2 * i + done + slot + 1)
                        do.tell(fn(fgate[:], facc[:, 0, :], ACT.Silu), "fgate_made", 2 * i + done + slot + 1)

        @block.vector
        def _(dve):
            do = Steps(dve, "dve_step")
            n_root = 0
            n_x = 0

            def free(ins, name, t, which="bank_free"):
                do.tell(ins, which, FREED[name] + t + 1)

            def split(hi, lo, src):
                do(dve.tensor_copy(hi, src))
                return dve.tensor_tensor(lo, src, hi.bitcast(f32), ALU.subtract)

            def inverse_root(buf):
                nonlocal n_root
                n_root += 1
                dve.wait_ge(sem("root_ready"), n_root)
                do(dve.reciprocal(buf[:], buf[:]))

            def add_to_x(name, gate=None, wide=False):
                for m in range(KT):
                    s = SLAB0[name] + (m if wide else m // 2)
                    dve.wait_ge(sem("tile_done"), 2 * s + (2 if wide else m % 2 + 1))
                    bank = banks[(2 if wide else 0) + m % 2]
                    if gate is None:
                        ins = dve.tensor_tensor(x[:, m, :], bank[:], x[:, m, :], ALU.add)
                    else:
                        ins = dve.scalar_tensor_tensor(x[:, m, :], bank[:], mod[:, gate + m:gate + m + 1], x[:, m, :],
                                                       ALU.mult, ALU.add)
                    free(ins, name, m, "bank_free_wide" if wide else "bank_free")

            def told_x():
                nonlocal n_x
                n_x += 1
                do.tell(dve.tensor_copy(small[:, 2:3], small[:, 0:1]), "x_ready", n_x)

            def modulated(stage, scale, shift=None):
                inverse_root(rs)
                first = KT * (stage - 1)

                def scaled(k):
                    do.tell(dve.scalar_tensor_tensor((t0, t1)[k % 2][:], x[:, k, :], scale(k), rs[:], ALU.mult, ALU.mult),
                            "h_scaled", first + k + 1)

                scaled(0)
                for k in range(KT):
                    if k + 1 < KT:
                        scaled(k + 1)
                    dve.wait_ge(sem("h_head"), first + k + 1)
                    src, head = (t0, t1)[k % 2][:], h_hi[:, k, :].bitcast(f32)
                    if shift is None:
                        ins = dve.tensor_tensor(h_lo[:, k, :], src, head, ALU.subtract)
                    else:
                        ins = dve.scalar_tensor_tensor(h_lo[:, k, :], src, mod[:, shift + k:shift + k + 1], head,
                                                       ALU.add, ALU.subtract)
                    do.tell(ins, "h_ready", first + k + 1)
                do.tell(dve.tensor_copy(small[:, 2:3], small[:, 0:1]), "root_used", n_root)

            do(dve.memset(small[:], EPS))
            do(dve.memset(ones[:], 1.0))
            do.tell(dve.memset(mean[:], 1.0 / D), "set", 1)
            dve.wait_ge(sem("consts_in"), 16)
            do(dve.tensor_copy(mask16_made[:, 0, :], ident))
            do(dve.tensor_copy(mask16_made[:, 1, :], causal))
            do.tell(dve.tensor_copy(mask16[:], mask16_made[:]), "mask_made", 1)
            for n in range(2):
                do.tell(dve.memset(small[:, 3:4], 0.0), "bank_free_wide", n + 1)
            dve.wait_ge(sem("c_ready"), 1)
            for n in range(3 * KT):
                third, k = n // KT, n % KT
                dve.wait_ge(sem(f"ada_in{n % 6}"), 16 * (n // 6) + 16)
                acc = ada_acc[:, 2048 * third:2048 * third + 2048]
                if k == 0:
                    ins = dve.tensor_scalar(acc, ada_w[:, n % 6, :], c_act[:, 0:1], None, ALU.mult)
                else:
                    ins = dve.scalar_tensor_tensor(acc, ada_w[:, n % 6, :], c_act[:, k:k + 1], acc, ALU.mult, ALU.add)
                do.tell(ins, "ada_used", n + 1)
            dve.wait_ge(sem("mod_done"), 1)
            do(dve.scalar_tensor_tensor(mod[:], banks[4][:, 0:48], float(D), cols[:, COLS["b_ada"]:COLS["b_ada"] + 48],
                                        ALU.mult, ALU.add))
            for first, sc, g in ((0, SC1, "g_mix"), (8, SC2, "g_ffn")):
                do(dve.scalar_tensor_tensor(gain[:, first:first + 8], mod[:, sc:sc + 8], 1.0,
                                            cols[:, COLS[g]:COLS[g] + 8], ALU.add, ALU.mult))
            dve.wait_ge(sem("gate_w_in"), 16)
            do.tell(split(gw_hi[:], gw_lo[:], gw[:]), "gate_w_split", 1)
            modulated(1, lambda k: gain[:, k:k + 1], SH1)
            do.tell(dve.memset(u[:], 0.0), "u_zeroed", 1)
            dve.wait_ge(sem("gates_biased"), 1)
            li, lf, r2, r3 = (rows[0:G1, n, :] for n in range(4))
            ge, gs = neg_max[0:G1, :], neg_m[0:G1, :]
            do.tell(dve.scalar_tensor_tensor(r2, lf, -1.0, lf, ALU.mult, ALU.min), "gate_negabs", 1)
            dve.wait_ge(sem("gate_exp"), 1)
            do.tell(dve.tensor_scalar(r3, r2, 1.0, None, ALU.add), "gate_onep", 1)
            do(dve.scalar_tensor_tensor(r2, r3, -1.0, r2, ALU.add, ALU.subtract))
            dve.wait_ge(sem("gate_ln"), 1)
            do(dve.reciprocal(r3, r3))
            do(dve.tensor_tensor(r2, r2, r3, ALU.mult))
            do(dve.tensor_tensor(r2, gs, r2, ALU.subtract))
            do(dve.scalar_tensor_tensor(lf, lf, 0.0, r2, ALU.min, ALU.subtract))
            do(dve.memset(r3, 1.0))

            def scan(out, data0, data1, first, op0, op1, initial):
                rows_ = slice(first, first + H1)
                turn = slice(None, None, -1) if first else slice(None)
                do(dve.tensor_tensor_scan(out[rows_, turn], data0[rows_, turn], data1[rows_, turn], initial, op0, op1))

            total, a, top = r2, li, ge
            do(dve.memset(total, 0.0))
            do(dve.memset(top, 0.0))
            for first in (0, 32):
                scan(rows[:, 2, :], rows[:, 3, :], rows[:, 1, :], first, ALU.mult, ALU.add, 0.0)
            do(dve.tensor_tensor(a, li, total, ALU.subtract))
            for first in (0, 32):
                scan(neg_max[:], rows[:, 0, :], rows[:, 0, :], first, ALU.max, ALU.max, 0.0)
            do(dve.scalar_tensor_tensor(gs, total, -1.0, top, ALU.mult, ALU.subtract))
            do.tell(dve.tensor_scalar(ge, top, -1.0, None, ALU.mult), "gate_rows", 1)
            do.tell(dve.memset(mean[:], 1.0 / DH), "mean_set", 1)
            do(dve.memset(win[:], 0.0))
            dve.wait_ge(sem("inv_in"), 16)
            for g, size in enumerate(WINDOWS):
                dve.wait_ge(sem("bank_free"), FREED["u"] + g + 1)
                do(dve.tensor_tensor(win[:, 0, 1:UW], u[:, g, 0:UW - 1], u[:, g, 1:UW], ALU.add))
                w, reach, margin = 0, 1, 1
                while 2 * reach < size:
                    a0, a1 = margin + reach, UW - margin - reach
                    do(dve.tensor_tensor(win[:, 1 - w, a0:a1], win[:, w, a0 - reach:a1 - reach],
                                         win[:, w, a0 + reach:a1 + reach], ALU.add))
                    margin, w, reach = margin + reach, 1 - w, 2 * reach
                do(dve.tensor_tensor(mixed1[:, g, :], win[:, w, PAD:PAD + S], inv[:, g, :], ALU.mult))
                do.tell(dve.tensor_tensor(mixed1[:, g, :], mixed1[:, g, :], u[:, g, PAD:PAD + S], ALU.subtract), "pooled", g + 1)
            for g in range(4):
                dve.wait_ge(sem("pool_done"), g + 1)
                do(dve.tensor_scalar(t1[:], pool_banks[g][:], col("pool_scale", g), None, ALU.mult))
                do.tell(split(y_hi[:, 4 + g, :], y_lo[:, 4 + g, :], t1[:]), "y_ready", g + 1)
            def weighted(n):
                head, back = n // 2, n % 2
                place = p1[:, back, :]
                dve.wait_ge(sem("e1_made"), n + 1)
                dve.wait_ge(sem("s1_done"), head + 1)
                for j, lo, hi, used in paired(back):
                    part = place[:, used:used + hi - lo]
                    do(dve.scalar_tensor_tensor(part, part, 1.0, banks[j][:, lo:hi], ALU.min, ALU.mult))
                keep = (keep_low if back else keep_up).unsqueeze(1).to_broadcast([P, 2, P])
                two, two_more = diagonals(place, back)
                do(dve.tensor_tensor(two, two, keep, ALU.mult))
                do.tell(dve.tensor_tensor(two_more, two_more, keep, ALU.mult), "p1_made", n + 1)

            def normalised(n):
                head, back = n // 2, n % 2
                dve.wait_ge(sem("pv1_done"), n + 1)
                do(dve.scalar_tensor_tensor(den1[:], banks[6][:], -1.0, floor1[:, back, :], ALU.mult, ALU.max))
                do(dve.tensor_tensor(den1[:], den1[:], banks[6][:], ALU.max))
                do(dve.reciprocal(den1[:], den1[:]))
                do.tell(dve.tensor_tensor(t1[:] if back else hm[:, head, :], banks[5][:], den1[:], ALU.mult), "h1_made", n + 1)
                if back:
                    do.tell(dve.tensor_tensor(hm[:, head, :], hm[:, head, :], t1[:], ALU.add), "hm_made", head + 1)

            for n in range(2 * H1):
                weighted(n)
                if n:
                    normalised(n - 1)
            normalised(2 * H1 - 1)
            for head in range(H1):
                dve.wait_ge(sem("head_root"), head + 1)
                do(dve.reciprocal(rs_h[:, head, :], rs_h[:, head, :]))
                do(dve.scalar_tensor_tensor(hm[:, head, :], hm[:, head, :], col("g_head", head), rs_h[:, head, :],
                                            ALU.mult, ALU.mult))
            do.tell(dve.memset(mean[:], 1.0 / D), "mean_set", 2)
            for head in range(H1):
                dve.wait_ge(sem("bank_free"), FREED["o"] + head + 1)
                do(dve.tensor_tensor(t1[:], hm[:, head, :], og[:, head, :], ALU.mult))
                do.tell(split(y_hi[:, head, :], y_lo[:, head, :], t1[:]), "y_ready", 4 + head + 1)
            add_to_x("out", GT1)
            told_x()
            modulated(2, lambda k: gain[:, 8 + k:9 + k], SH2)
            for half, (up, down) in enumerate((("ff1a", "ff2a"), ("ff1b", "ff2b"))):
                with dve.Fori(0, SLABS[up] // 2) as i:
                    do.loop(i, 4)
                    for t in range(4):
                        dve.wait_ge(sem("bank_free"), 4 * i + FREED[up] + t + 1)
                        do.tell(dve.tensor_tensor(asq[:], relu[:, t % 2, :], relu[:, t % 2, :], ALU.mult), "relu_used",
                                4 * i + 16 * half + t + 1)
                        place = 4 * i + t
                        do(dve.tensor_copy(a_hi[:, place, :], asq[:]))
                        do.tell(dve.tensor_tensor(a_lo[:, place, :], asq[:], a_hi[:, place, :].bitcast(f32), ALU.subtract),
                                "a_ready", 4 * i + 16 * half + t + 1)
                do.end(SLABS[up] // 2)
                add_to_x(down, GT2, wide=True)
            told_x()
            inverse_root(rs)
            for k in range(KT):
                do(dve.scalar_tensor_tensor(x[:, k, :], x[:, k, :], col("g_final", k), rs[:], ALU.mult, ALU.mult))
            do.tell(dve.tensor_copy(small[:, 2:3], small[:, 0:1]), "root_used", n_root)
            told_x()
            modulated(3, lambda k: col("g_mix2", k))
            dve.wait_ge(sem("bank_free"), FREED["misc"] + 4)
            d0, d1, d2, d3 = (drow[0:32, n, :] for n in range(4))
            do(dve.tensor_scalar(d0, mz[0:32, :], col("dt_bias", 0, 0, 32), None, ALU.add))
            do.tell(dve.scalar_tensor_tensor(d1, d0, -1.0, d0, ALU.mult, ALU.min), "dt_negabs", 1)
            dve.wait_ge(sem("dt_exp"), 1)
            do.tell(dve.tensor_scalar(d2, d1, 1.0, None, ALU.add), "dt_onep", 1)
            do(dve.scalar_tensor_tensor(d1, d2, -1.0, d1, ALU.add, ALU.subtract))
            dve.wait_ge(sem("dt_ln"), 1)
            do(dve.reciprocal(d2, d2))
            do(dve.tensor_tensor(d1, d1, d2, ALU.mult))
            do(dve.tensor_tensor(d3, d3, d1, ALU.subtract))
            do(dve.scalar_tensor_tensor(d0, d0, 0.0, d3, ALU.max, ALU.add))
            do(dve.tensor_scalar(d1, d0, small[0:32, 1:2], -1.0, ALU.mult, ALU.mult))
            do(dve.memset(d2, 1.0))
            do(dve.tensor_tensor_scan(acum[0:32, :], d2, d1, 0.0, ALU.mult, ALU.add))
            do.tell(dve.tensor_scalar(d3, acum[0:32, :], -1.0, None, ALU.mult), "dt_rows", 1)
            do.tell(dve.memset(cpad[:], 0.0), "cpad_zeroed", 1)
            with dve.Fori(0, SLABS["xbc"] // 2) as i:
                do.loop(i, 4 * (TAPS - 1))
                for t in range(4):
                    n = 4 * i + t
                    dve.wait_ge(sem("bank_free"), 4 * i + FREED["xbc"] + t + 1)
                    if t >= 2:
                        dve.wait_ge(sem("xbc_ready"), 4 * i + t - 1)
                    else:
                        dve.wait_ge(sem("xbc_ready"), 4 * i)
                    acc, pad = cacc[:, t % 2, :], cpad[:, t % 2, :]
                    do(dve.tensor_scalar(acc, pad[:, 0:S], col("conv_w", TAPS * n), col("conv_b", n), ALU.mult, ALU.add))
                    for tap in range(1, TAPS):
                        ins = dve.scalar_tensor_tensor(acc, pad[:, tap:tap + S], col("conv_w", TAPS * n + tap), acc,
                                                       ALU.mult, ALU.add)
                        if tap < TAPS - 1:
                            do(ins)
                        else:
                            do.tell(ins, "conv_done", 4 * i + t + 1)
            do.end(SLABS["xbc"] // 2)
            dve.wait_ge(sem("dt_col_ready"), 1)
            for n in range(TOK * 4):
                tok, quad = n // 4, n % 4
                dve.wait_ge(sem("xs_turned"), n + 1)
                scale = dt_col[:, tok, 8 * quad:8 * quad + 8].unsqueeze(2).to_broadcast([P, 8, SSD_P])
                do.tell(dve.tensor_tensor(xdt[:, tok, S * quad:S * quad + S].rearrange("p (h e) -> p h e", h=8),
                                          banks[n % 4][:].rearrange("p (h e) -> p h e", h=8), scale, ALU.mult),
                        "xdt_made", n + 1)
            def gated_pair(pair):
                y = xbc[:, pair, :]
                dve.wait_ge(sem("pv2_done"), 2 * pair + 2)
                do.tell(dve.scalar_tensor_tensor(y, y, col("d_skip", pair), banks[6 + pair % 2][:], ALU.mult, ALU.add),
                        "ys_made", pair + 1)
                dve.wait_ge(sem("z_tanh"), pair + 1)
                free(dve.scalar_tensor_tensor(zt[:], zt[:], 1.0, banks[0][:], ALU.add, ALU.mult), "z", pair)
                do.tell(dve.scalar_tensor_tensor(y, zt[:], 0.5, y, ALU.mult, ALU.mult), "z_used", pair + 1)

            def diagonal_exponents(hd):
                dve.wait_ge(sem("bc2_done"), hd + 1)
                if hd >= 2:
                    dve.wait_ge(sem("pv2_done"), hd - 1)
                for nth, (j, lo, hi, used) in enumerate(paired(0)):
                    ins = dve.tensor_scalar(p2[:, hd % 2, used:used + P], banks[4 + hd % 2][:, lo:lo + P], nac_col[:, j, hd:hd + 1],
                                            0.0, ALU.add, ALU.min)
                    if nth < TOK - 1:
                        do(ins)
                    else:
                        do.tell(ins, "diagonal_made", hd + 1)

            diagonal_exponents(0)
            for hd in range(SSD_H):
                g = hd // 8
                if hd % 8 == 0:
                    dve.wait_ge(sem("s2_done"), g + 1)
                    for j, lo, hi, used in paired(0):
                        bank, first = score_place(j)
                        do(dve.tensor_copy(sm[:, used:used + hi - lo], banks[bank][:, first:first + hi - lo]))
                    two, two_more = diagonals(sm, 0)
                    keep = keep_up.unsqueeze(1).to_broadcast([P, 2, P])
                    do(dve.tensor_tensor(two, two, keep, ALU.mult))
                    do.tell(dve.tensor_tensor(two_more, two_more, keep, ALU.mult), "sm_made", g + 1)
                dve.wait_ge(sem("e2_made"), hd + 1)
                do.tell(dve.tensor_tensor(p2[:, hd % 2, :], p2[:, hd % 2, :], sm[:], ALU.mult), "p2_made", hd + 1)
                if hd % 2 == 0 and hd:
                    gated_pair(hd // 2 - 1)
                if hd + 1 < SSD_H:
                    diagonal_exponents(hd + 1)
            gated_pair(XS_T - 1)
            do.tell(dve.memset(mean[:], 1.0 / (4 * P)), "mean_set", 3)
            for g in range(SSD_G):
                inverse_root(rs)
                for k in range(4 * g, 4 * g + 4):
                    do(dve.scalar_tensor_tensor(t1[:], xbc[:, k, :], col("ssd_g", k), rs[:], ALU.mult, ALU.mult))
                    ins = split(ys_hi[:, k, :], ys_lo[:, k, :], t1[:])
                    if k % 4 < 3:
                        do(ins)
                    else:
                        do.tell(ins, "root_used", n_root)
            dve.wait_ge(sem("bank_free"), FREED["gates"] + 16)
            for m in range(8):
                dve.wait_ge(sem("tile_done"), 2 * (SLAB0["ssd"] + m) + 2)
                do.tell(dve.tensor_tensor(mix[:, m, :], mix[:, m, :], banks[2 + m % 2][:], ALU.mult), "bank_free_wide",
                        FREED["ssd"] + m + 1)
                do.tell(dve.tensor_copy(small[:, 2:3], small[:, 0:1]), "mix_made", m + 1)
            do.tell(dve.memset(mean[:], 1.0 / (2 * P)), "mean_set", 4)
            for first, n in ((0, 2), (2, 1)):
                inverse_root(rs_l)
                for k in range(first, first + n):
                    do(dve.scalar_tensor_tensor(t1_l[:], qa[:, k, :], col("qa_g", k), rs_l[:], ALU.mult, ALU.mult))
                    do.tell(split(qn_hi[:, k, :], qn_lo[:, k, :], t1_l[:]), "qn_made", k + 1)
                if first == 0:
                    do.tell(dve.memset(mean[:], 1.0 / P), "mean_set", 5)
                do.tell(dve.tensor_copy(small[:, 2:3], small[:, 0:1]), "root_used", n_root)
            dve.wait_ge(sem("rope_in"), 32)
            for n in range(16):
                keys, tok = n // 8, n % 4
                tile = tt[:, n % 2, :, :]
                dve.wait_ge(sem("unit_squared"), n + 1)
                do.tell(dve.tensor_reduce(stat[:, 0, :], tsq[:], AX.X, ALU.add), "unit_summed", n + 1)
                dve.wait_ge(sem("unit_root"), n + 1)
                do(dve.reciprocal(stat[:, 2, :], stat[:, 1, :]))
                do(dve.tensor_tensor(tile, tile, stat[:, 2, :].unsqueeze(2).to_broadcast([P, HU, QK]), ALU.mult))
                do(dve.tensor_tensor(tile, tile, qk_g[:, keys, :].unsqueeze(1).to_broadcast([P, HU, QK]), ALU.mult))
                cos, sin = (rope[:, s, tok, :].unsqueeze(1).to_broadcast([P, HU, ROPE // 2]) for s in range(2))
                first, second = tile[:, :, NOPE:NOPE + ROPE // 2], tile[:, :, NOPE + ROPE // 2:QK]
                for part, src, f in ((0, first, cos), (1, second, sin), (2, first, sin), (3, second, cos)):
                    do(dve.tensor_tensor(trope[:, part, :, :], src, f, ALU.mult))
                do(dve.tensor_tensor(first, trope[:, 0, :, :], trope[:, 1, :, :], ALU.subtract))
                do.tell(dve.tensor_tensor(second, trope[:, 2, :, :], trope[:, 3, :, :], ALU.add), "heads_scaled", n + 1)

            def maxima(hd):
                for i, lo, hi, used in spans(1):
                    dve.wait_ge(sem("s3_done"), TOK * hd + i + 1)
                    top, bias = (mx[:, hd % 2, n, i:i + 1] for n in range(2))
                    do(dve.tensor_reduce(top, banks[i][:, 0:hi], AX.X, ALU.max))
                    do.tell(dve.tensor_scalar(bias, top, -QK ** -0.5, None, ALU.mult), "max_made", TOK * hd + i + 1)

            maxima(0)
            for step in range(QH + 2):
                if step < QH:
                    hd = step
                    for i, lo, hi, used in spans(1):
                        part, total = p3[hd % 2][:, used:used + hi], mx[:, hd % 2, 2, i:i + 1]
                        dve.wait_ge(sem("p3_made"), TOK * hd + i + 1)
                        do(dve.reciprocal(total, total))
                        do.tell(dve.tensor_scalar(part, part, total, None, ALU.mult), "p3_scaled", TOK * hd + i + 1)
                if step + 1 < QH:
                    maxima(step + 1)
                if step >= 2 and step % 2:
                    pair = step // 2 - 1
                    dve.wait_ge(sem("pv3_done"), 2 * pair + 2)
                    do(dve.tensor_copy(ao[:], banks[7][:]))
                    do.tell(split(att[:, 2 * pair, :], att[:, 2 * pair + 1, :], ao[:]), "att_made", pair + 1)
            for m in range(8):
                dve.wait_ge(sem("tile_done"), 2 * SLAB0["mla"] + m + 1)
                free(dve.tensor_tensor(mt[:], gm[:, m, :], banks[m % 2][:], ALU.mult), "mla", m)
                do(dve.tensor_tensor(mix[:, m, :], mix[:, m, :], mt[:], ALU.add))
                do.tell(split(mm_hi[:, m, :], mm_lo[:, m, :], mix[:, m, :]), "mm_made", m + 1)
            do.tell(dve.memset(mean[:], 1.0 / D), "mean_set", 6)
            add_to_x("wo")
            told_x()
            modulated(4, lambda k: col("g_ffn2", k))
            do.tell(dve.memset(fpad[:], 0.0), "fpad_zeroed", 1)
            for up, done in (("upa", 0), ("upb", 16)):
                with dve.Fori(0, SLABS[up] // 2) as i:
                    do.loop(i, 2 * (2 * TAPS_F - 1 + 2))
                    for slot in range(2):
                        for m in range(2):
                            dve.wait_ge(sem("bank_free"), 4 * i + FREED[up] + 2 * slot + m + 1)
                            tile = 2 * (2 * i + done + slot) + m
                            acc, pad = facc[:, m, :], fpad[:, m, :]
                            do(dve.tensor_scalar(acc, pad[:, 0:S], col("convf_w", TAPS_F * tile), col("convf_b", tile),
                                                 ALU.mult, ALU.add))
                            for tap in range(1, TAPS_F):
                                ins = dve.scalar_tensor_tensor(acc, pad[:, tap:tap + S], col("convf_w", TAPS_F * tile + tap),
                                                               acc, ALU.mult, ALU.add)
                                if m == 0 and tap == TAPS_F - 1:
                                    do.tell(ins, "fconv_done", 2 * i + done + slot + 1)
                                else:
                                    do(ins)
                        dve.wait_ge(sem("fgate_made"), 2 * i + done + slot + 1)
                        do(dve.tensor_tensor(fa[:], fgate[:], facc[:, 1, :], ALU.mult))
                        place = 2 * i + slot
                        do(dve.tensor_copy(a_hi[:, place, :], fa[:]))
                        do.tell(dve.tensor_tensor(a_lo[:, place, :], fa[:], a_hi[:, place, :].bitcast(f32), ALU.subtract),
                                "fa_made", 2 * i + done + slot + 1)
                do.end(SLABS[up] // 2)
                if up == "upa":
                    add_to_x("downa", wide=True)
            for m in range(KT):
                dve.wait_ge(sem("tile_done"), 2 * SLAB0["downb"] + m + 1)
                free(dve.tensor_tensor(x[:, m, :], banks[m % 2][:], x[:, m, :], ALU.add), "downb", m)
                do.tell(dve.tensor_copy(small[:, 2:3], small[:, 0:1]), "x_final", m + 1)

        @block.tensor
        def _(pe):
            n_sq = 0

            def three(out, w, a, start, stop):
                pe.matmul(out, w[0], a[0], start=start, stop=False)
                pe.matmul(out, w[0], a[1], start=False, stop=False)
                return pe.matmul(out, w[1], a[0], start=False, stop=stop)

            def weights(slot, tile, n=1):
                part = slice(P * tile, P * (tile + n))
                return w_hi[:, slot, part], w_lo[:, slot, part]

            def product(name, hi, lo, kt=KT, slots=(0, 1)):
                wide = name in WIDE
                bank0, which = (2, "bank_free_wide") if wide else (0, "bank_free")

                def turn(i):
                    for slot in slots:
                        pe.wait_ge(sem("w_split"), 2 * i + SLAB0[name] + slot + 1)
                        for m in range(1 if wide else 2):
                            t = slot if wide else 2 * slot + m
                            per = 2 if wide else 4
                            before = FREED[name] + t - 1
                            if not isinstance(i, int) or before > 0:
                                pe.wait_ge(sem(which), per * i + before)
                            for k in range(kt):
                                last = three(banks[bank0 + t % 2][:], weights(slot, (16 if wide else KT) * m + k),
                                             (hi[:, k, :], lo[:, k, :]), k == 0, k == kt - 1)
                            last.then_inc(sem("tile_done"), 2 if wide else 1)

                if SLABS[name] == 2:
                    turn(0)
                else:
                    with pe.Fori(0, SLABS[name] // 2) as i:
                        turn(i)

            def sum_squares(n, buf, bank=banks[7]):
                nonlocal n_sq
                for k in range(n):
                    pe.wait_ge(sem("sq_ready"), n_sq + 1)
                    pe.matmul(bank[:], mean[:], buf[:, n_sq % 2, :], start=k == 0, stop=k == n - 1)\
                      .then_inc(sem("sq_used"), 1)
                    n_sq += 1

            def norm(stage):
                sum_squares(KT, sq)
                pe.wait_ge(sem("h_ready"), KT * stage)

            def row(n, count):
                return ident[0:count, n:n + 1].to_broadcast([count, P])

            pe.wait_ge(sem("set"), 1)
            sum_squares(KT, sq)
            pe.wait_ge(sem("ada_used"), 3 * KT)
            for m in range(48):
                last = pe.matmul(banks[4][:, m:m + 1], ada_acc[:, P * m:P * m + P], mean[:, 0:1], start=True, stop=True)
            last.then_inc(sem("mod_done"), 1)
            pe.wait_ge(sem("h_ready"), KT)
            pe.wait_ge(sem("gate_w_split"), 1)
            for k in range(KT):
                last = three(banks[4][:], (gw_hi[:, k, :], gw_lo[:, k, :]), (h_hi[:, k, :], h_lo[:, k, :]), k == 0, k == KT - 1)
            last.then_inc(sem("gates_done"), 1)
            product("u", h_hi, h_lo)
            product("q", h_hi, h_lo)
            pe.wait_ge(sem("consts_in"), 16)
            pe.wait_ge(sem("gate_rows"), 1)
            for t in range(TOK):
                last = pe.transpose(banks[4][:, G1 * t:G1 * t + G1], rows[0:G1, 0, P * t:P * t + P], ident[0:G1, 0:G1])
            last.then_inc(sem("a_turned"), 1)
            product("k", h_hi, h_lo)
            for c in range(2):
                pe.wait_ge(sem("w_split"), SLAB0["v"] + c + 1)
                for m in range(2):
                    pe.wait_ge(sem("bank_free"), FREED["v"] + 2 * c + m - 1)
                    for half in range(2):
                        tok = slice(P * (2 * m + half), P * (2 * m + half + 1))
                        for k in range(KT):
                            last = three(banks[m][:, 256 * half:256 * half + 256], (h_hi[:, k, tok], h_lo[:, k, tok]),
                                         weights(c, 2 * k, 2), k == 0, k == KT - 1)
                    last.then_inc(sem("tile_done"), 1)
                if c == 0:
                    pe.wait_ge(sem("pool_w_in"), 16)
                    for g in range(4):
                        pe.wait_ge(sem("pooled"), g + 1)
                        if g == 3:
                            pe.wait_ge(sem("y_ready"), 1)
                        pe.matmul(pool_banks[g][:], pool_w[:, g, :], mixed1[:, g, :], start=True, stop=True)\
                          .then_inc(sem("pool_done"), 1)
            def broadcasts(n):
                r = 32 * (n % 2) + n // 2
                if n:
                    pe.wait_ge(sem("e1_made"), n)
                pe.matmul(banks[4][:], row(r, G1), neg_max[0:G1, :], start=True, stop=True)
                pe.matmul(banks[7][:], row(r, G1), neg_m[0:G1, :], start=True, stop=True).then_inc(sem("bc1_done"), 1)

            def head_scores(head):
                for j in range(TOK):
                    last = pe.matmul(banks[j][:], qk[:, 4 + head, P * j:P * j + P], qk[:, head, :], start=True, stop=True)
                last.then_inc(sem("s1_done"), 1)

            pe.wait_ge(sem("a_col_ready"), 1)
            pe.wait_ge(sem("y_ready"), 4)
            broadcasts(0)
            pe.wait_ge(sem("bank_free"), FREED["v"] + 4)
            head_scores(0)
            for n in range(2 * H1):
                head, back = n // 2, n % 2
                if n + 1 < 2 * H1:
                    broadcasts(n + 1)
                pe.wait_ge(sem("p1_made"), n + 1)
                if back and head + 1 < H1:
                    head_scores(head + 1)
                if n:
                    pe.wait_ge(sem("h1_made"), n)
                order = sorted(paired(back), key=lambda block_row: block_row[1] - block_row[2])
                for bank, left in ((5, None), (6, ones)):
                    for nth, (j, lo, hi, used) in enumerate(order):
                        w = v1[:, j, DH * head:DH * head + DH] if left is None else left[:]
                        last = pe.matmul(banks[bank][:, lo:hi], w, p1[:, back, used:used + hi - lo], start=nth == 0, stop=nth == TOK - 1)
                last.then_inc(sem("pv1_done"), 1)
            pe.wait_ge(sem("mean_set"), 1)
            for head in range(H1 - 1):
                sum_squares(1, sq, head_banks[head])
            product("o", h_hi, h_lo, slots=(0,))
            sum_squares(1, sq, head_banks[H1 - 1])
            product("o", h_hi, h_lo, slots=(1,))
            pe.wait_ge(sem("y_ready"), 8)
            product("out", y_hi, y_lo)
            pe.wait_ge(sem("mean_set"), 2)
            norm(2)
            for half in "ab":
                product("ff1" + half, h_hi, h_lo)
                pe.wait_ge(sem("a_ready"), 16 if half == "a" else 32)
                product("ff2" + half, a_hi, a_lo, 16)
            sum_squares(KT, sq)
            norm(3)
            product("misc", h_hi, h_lo)
            product("xbc", h_hi, h_lo)
            pe.wait_ge(sem("dt_rows"), 1)
            for t in range(TOK):
                tok = slice(P * t, P * t + P)
                pe.transpose(banks[4][:, 32 * t:32 * t + 32], drow[0:32, 3, tok], ident[0:32, 0:32])
                pe.transpose(banks[5][:, 32 * t:32 * t + 32], drow[0:32, 0, tok], ident[0:32, 0:32])
                last = pe.transpose(banks[6][:, P * t:P * t + P], mz[:, tok], ident)
            last.then_inc(sem("dt_turned"), 1)
            pe.wait_ge(sem("xbc_ready"), XS_T + BC_T)
            for n in range(TOK * 4):
                tok, quad = n // 4, n % 4
                if n >= 4:
                    pe.wait_ge(sem("xdt_made"), n - 3)
                for m in range(4):
                    last = pe.transpose(banks[n % 4][:, P * m:P * m + P], xbc[:, 4 * quad + m, P * tok:P * tok + P], ident)
                last.then_inc(sem("xs_turned"), 1)
            pe.wait_ge(sem("xdt_made"), TOK * 4)
            def running_sums(hd):
                bank = banks[4 + hd % 2]
                if hd >= 2:
                    pe.wait_ge(sem("e2_made"), hd - 1)
                pe.matmul(bank[:], row(hd, 32), acum[0:32, :], start=True, stop=True).then_inc(sem("bc2_done"), 1)

            def group_scores(g):
                if g:
                    pe.wait_ge(sem("sm_made"), g)
                for j, lo, hi, used in spans(0):
                    bank, first = score_place(j)
                    last = pe.matmul(banks[bank][:, first:first + hi - lo], xbc[:, XS_T + g, P * j:P * j + P],
                                     xbc[:, XS_T + SSD_G + g, lo:hi], start=True, stop=True)
                last.then_inc(sem("s2_done"), 1)

            def z_tile(pair):
                slab, m = SLAB0["z"] + pair // 2, pair % 2
                pe.wait_ge(sem("w_split"), slab + 1)
                if pair:
                    pe.wait_ge(sem("bank_free"), FREED["z"] + pair)
                for k in range(KT):
                    last = three(banks[0][:], weights(slab % 2, KT * m + k), (h_hi[:, k, :], h_lo[:, k, :]), k == 0, k == KT - 1)
                last.then_inc(sem("tile_done"), 1)

            group_scores(0)
            running_sums(0)
            for hd in range(SSD_H):
                pair = hd // 2
                if hd + 1 < SSD_H:
                    running_sums(hd + 1)
                if hd % 2:
                    z_tile(pair)
                    if hd % 8 == 7 and hd + 1 < SSD_H:
                        group_scores(hd // 8 + 1)
                pe.wait_ge(sem("p2_made"), hd + 1)
                if hd % 2 == 0 and pair >= 2:
                    pe.wait_ge(sem("ys_made"), pair - 1)
                out = banks[6 + pair % 2][64 * (hd % 2):64 * (hd % 2) + 64, :]
                for nth, (j, lo, hi, used) in enumerate(paired(0)):
                    last = pe.matmul(out[:, lo:hi], xdt[:, j, SSD_P * hd:SSD_P * hd + SSD_P], p2[:, hd % 2, used:used + hi - lo],
                                     start=nth == 0, stop=nth == TOK - 1)
                last.then_inc(sem("pv2_done"), 1)
            pe.wait_ge(sem("mean_set"), 3)
            for g in range(SSD_G):
                sum_squares(4, sq)
            pe.wait_ge(sem("bank_free"), FREED["gates"])
            product("gates", h_hi, h_lo)
            pe.wait_ge(sem("root_used"), 4 + SSD_G)
            product("ssd", ys_hi, ys_lo, 16)
            pe.wait_ge(sem("mean_set"), 4)
            sum_squares(2, sq_l)
            pe.wait_ge(sem("mean_set"), 5)
            sum_squares(1, sq_l)
            pe.wait_ge(sem("qn_made"), 3)
            pe.wait_ge(sem("bank_free"), FREED["gates"] + 16)

            def unit(n):
                keys, tok, slot = n // 8, slice(P * (n % 4), P * (n % 4) + P), n // 4 % 2
                pe.wait_ge(sem("w_split"), SLAB0["uq"] + n // 4 + 1)
                if n >= 2:
                    pe.wait_ge(sem("unit_squared"), n - 1)
                width = S if keys else 4 * QK
                for half in range(2):
                    for k in range(1 if keys else 2):
                        first = (0 if keys else 2 * width * k) + width * half
                        kk = 2 if keys else k
                        last = three(banks[2 * (n % 2) + half][:, 0:width], (qn_hi[:, kk, tok], qn_lo[:, kk, tok]),
                                     (w_hi[:, slot, first:first + width], w_lo[:, slot, first:first + width]),
                                     k == 0, bool(keys) or k == 1)
                last.then_inc(sem("tile_done" if n % 2 else "unit_done"), 1)

            def turn_heads(n):
                pe.wait_ge(sem("heads_scaled"), n + 1)
                if n >= 2:
                    pe.wait_ge(sem("heads_ready"), n - 1)
                for hh in range(HU):
                    last = pe.transpose(banks[4 + 2 * (n % 2) + hh // 4][0:QK, P * (hh % 4):P * (hh % 4) + P],
                                        tt[:, n % 2, hh, :], ident)
                last.then_inc(sem("heads_turned"), 1)

            for n in range(16):
                unit(n)
                if n:
                    turn_heads(n - 1)
            turn_heads(15)
            pe.wait_ge(sem("heads_ready"), 16)

            def scores(hd):
                for i, lo, hi, used in spans(1):
                    if hd:
                        pe.wait_ge(sem("p3_made"), TOK * (hd - 1) + i + 1)
                    pe.matmul(banks[i][:, 0:hi], q2[0:QK, hd, P * i:P * i + P], k2[0:QK, hd, 0:hi], start=True, stop=False)
                    pe.matmul(banks[i][:, P * i:hi], ident16, causal16, start=False, stop=True)\
                      .then_inc(sem("s3_done"), 1)

            def turn_probabilities(hd):
                if hd:
                    pe.wait_ge(sem("pt_made"), hd)
                for i, lo, hi, used in spans(1):
                    pe.wait_ge(sem("p3_scaled"), TOK * hd + i + 1)
                    for j in range(i + 1):
                        bank, first = ((4, 0), (5, 0), (6, 0), (5, 384))[j]
                        last = pe.transpose(banks[bank][:, first + P * (i - j):first + P * (i - j) + P],
                                            p3[hd % 2][:, used + P * j:used + P * j + P], ident)
                last.then_inc(sem("p3_turned"), 1)

            def weighted_values(hd):
                pair = hd // 2
                pe.wait_ge(sem("pt_made"), hd + 1)
                if hd % 2 == 0 and pair:
                    pe.wait_ge(sem("att_made"), pair)
                out = banks[7][64 * (hd % 2):64 * (hd % 2) + 64, :]
                for j, lo, hi, used in spans(0):
                    last = pe.matmul(out[:, lo:hi], v2[:, j, VD * hd:VD * hd + VD], pt[hd % 2][:, used:used + hi - lo],
                                     start=j == 0, stop=j == TOK - 1)
                last.then_inc(sem("pv3_done"), 1)

            pe.wait_ge(sem("mask_made"), 1)
            for step in range(QH + 2):
                if step < QH:
                    scores(step)
                if 1 <= step <= QH:
                    turn_probabilities(step - 1)
                if step >= 2:
                    weighted_values(step - 2)
            pe.wait_ge(sem("att_made"), 8)
            product("mla", att[:, 0:16:2, :], att[:, 1:16:2, :])
            pe.wait_ge(sem("mm_made"), 8)
            product("wo", mm_hi, mm_lo)
            pe.wait_ge(sem("mean_set"), 6)
            norm(4)
            product("upa", h_hi, h_lo)
            pe.wait_ge(sem("fa_made"), 16)
            product("downa", a_hi, a_lo, 16)
            product("upb", h_hi, h_lo)
            pe.wait_ge(sem("fa_made"), UP_T)
            product("downb", a_hi, a_lo, UP_T - 16)


def kernel(**inputs):
    import concourse.bacc as bacc
    from concourse.bass_utils import run_bass_kernel_spmd

    f = {name: np.asarray(a) for name, a in inputs.items()}
    one = {name: (a[0] if name not in ("x", "c", "g_final") else a) for name, a in f.items()}

    def pairs(w):
        n = w.shape[1] // 256
        kt = w.shape[0] // P
        out = np.zeros((n, P, 2, KT, P), w.dtype)
        out[:, :, :, :kt] = w.reshape(kt, P, n, 2, P).transpose(2, 1, 3, 0, 4)
        return out.reshape(n, P, SLAB)

    def wides(w):
        return w.reshape(16, P, KT, P).transpose(2, 1, 0, 3).reshape(KT, P, SLAB)

    def tiles(a):
        return a.reshape(-1, P).T

    w_in, w_in2 = one["w_in"], one["w_in_2"]
    dm = H1 * DH
    gate0 = 4 * dm
    u0 = gate0 + 16
    by_token = w_in[:, 2 * dm:3 * dm].reshape(KT, P, 2, 256).transpose(2, 1, 0, 3).reshape(2, P, SLAB)
    xbc0, dt0 = 2048, 5120
    qa0, kr0 = dt0 + 32, dt0 + 32 + 384
    misc = np.zeros((D, 4 * P), w_in2.dtype)
    misc[:, 0:384] = w_in2[:, qa0:qa0 + 384]
    misc[:, 384:416] = w_in2[:, dt0:dt0 + 32]
    misc[:, 448:480] = w_in2[:, kr0:kr0 + 32]
    up = one["w_up_2"].reshape(D, 2, UP_T, P).transpose(0, 2, 1, 3).reshape(D, 2 * UP_T * P)
    down, ff1, ff2 = one["w_down_2"], one["w_ff1"], one["w_ff2"]
    uq = np.zeros((2, P, SLAB), w_in.dtype)
    uq[:, :, 0:1536] = one["w_uq_2"].reshape(2, P, 2, 768).transpose(2, 1, 0, 3).reshape(2, P, 1536)
    ukv = np.zeros((2, P, SLAB), w_in.dtype)
    ukv[:, :, 0:1024] = one["w_ukv_2"].reshape(P, 2, 1024).transpose(1, 0, 2)
    parts = {"q": pairs(w_in[:, 0:dm]), "k": pairs(w_in[:, dm:2 * dm]), "v": by_token, "o": pairs(w_in[:, 3 * dm:4 * dm]),
             "u": pairs(w_in[:, u0:]), "out": pairs(one["w_out"]),
             "ff1a": pairs(ff1[:, 0:2048]), "ff1b": pairs(ff1[:, 2048:]), "ff2a": wides(ff2[0:2048]), "ff2b": wides(ff2[2048:]),
             "misc": pairs(misc), "xbc": pairs(w_in2[:, xbc0:dt0]), "z": pairs(w_in2[:, 0:2048]), "gates": pairs(w_in2[:, kr0 + 32:]),
             "ssd": wides(one["w_ssd_proj_2"]), "uq": uq, "ukv": ukv, "mla": pairs(one["w_mla_proj_2"]), "wo": pairs(one["w_o_2"]),
             "upa": pairs(up[:, 0:16 * 256]), "upb": pairs(up[:, 16 * 256:]), "downa": wides(down[0:2048]), "downb": pairs(down[2048:])}
    slabs = np.concatenate([parts[name] for name, _ in PHASES])
    gate_w = np.zeros((P, KT, P), w_in.dtype)
    gate_bias = np.zeros((P, 1), w_in.dtype)
    for d in range(2):
        for g, name in enumerate(("b_igate", "b_fgate")):
            first = 64 * g + 32 * d
            c0 = gate0 + 8 * d + 4 * g
            gate_w[:, :, first:first + H1] = w_in[:, c0:c0 + H1].reshape(KT, P, H1).transpose(1, 0, 2)
            gate_bias[first:first + H1, 0] = one[name][d]

    def rows32(a):
        out = np.zeros((P, 1), a.dtype)
        out[0:32, 0] = a
        return out

    convf_w = one["conv_ffn_w_2"].reshape(TAPS_F, 2, UP_T, P).transpose(3, 2, 1, 0).reshape(P, 2 * UP_T * TAPS_F)
    convf_b = one["conv_ffn_b_2"].reshape(2, UP_T, P).transpose(2, 1, 0).reshape(P, 2 * UP_T)
    by_name = {"c": tiles(f["c"][0]), "b_ada": tiles(one["b_ada"]), "g_mix": tiles(one["g_mix"]), "gate_bias": gate_bias,
               "g_head": tiles(one["g_head"]), "pool_scale": tiles(one["pool_scale"]), "g_ffn": tiles(one["g_ffn"]),
               "g_final": tiles(f["g_final"]), "g_mix2": tiles(one["norm_mix_g_2"]),
               "conv_w": one["conv_ssd_w_2"].reshape(TAPS, 24, P).transpose(2, 1, 0).reshape(P, 96),
               "conv_b": tiles(one["conv_ssd_b_2"]), "dt_bias": rows32(one["dt_bias_2"]), "a_log": rows32(one["a_log_2"]),
               "d_skip": tiles(np.repeat(one["d_skip_2"], SSD_P)), "ssd_g": tiles(one["ssd_norm_g_2"]),
               "qa_g": tiles(one["q_a_norm_g_2"]), "kva_g": tiles(one["kv_a_norm_g_2"]), "gate_b": tiles(one["gate_b_2"]),
               "g_ffn2": tiles(one["norm_ffn_g_2"]), "convf_w": convf_w, "convf_b": convf_b}
    cols = np.concatenate([by_name[name] for name in COLS], axis=1)
    ada = one["w_ada"].reshape(KT, P, 3, 2048).transpose(2, 0, 1, 3).reshape(3 * KT, P, 2048)
    x_t = f["x"][0].T.reshape(KT, P, S).transpose(1, 0, 2)
    at = np.arange(P)
    consts = np.stack([np.eye(P), at[None, :] >= at[:, None], at[None, :] <= at[:, None],
                       np.where(at[None, :] <= at[:, None], 0.0, -1e30)], 1).astype(np.float32)
    t = np.arange(S)
    sizes = [np.clip(t + n // 2, 0, S) - np.clip(t - n // 2, 0, S) for n in WINDOWS]
    inv = np.broadcast_to(1.0 / np.array(sizes, np.float32), (P, 4, S))
    freq = (1.0 / (10000.0 ** (np.arange(0, ROPE, 2, dtype=np.float32) / np.float32(ROPE)))).astype(np.float32)
    angle = t.astype(np.float32)[:, None] * freq[None, :]
    rope = np.stack([np.cos(angle), np.sin(angle)]).reshape(2, TOK, P, ROPE // 2).transpose(2, 0, 1, 3)
    qk_g = np.broadcast_to(np.stack([one["q_norm_g_2"], one["k_norm_g_2"]]), (P, 2, QK))
    pool_w = one["w_pool"].transpose(1, 0, 2)
    arrays = {"x_in": x_t, "slabs": slabs, "ada": ada, "cols": cols, "gate_w": gate_w, "pool_w": pool_w, "consts": consts,
              "inv": inv, "rope": rope, "qk_g": qk_g}
    arrays = {name: np.ascontiguousarray(a) for name, a in arrays.items()}
    nc = bacc.Bacc("TRN2", target_bir_lowering=False, num_devices=1)
    drams = [nc.dram_tensor(name, a.shape, mybir.dt.from_np(a.dtype), kind="ExternalInput").ap() for name, a in arrays.items()]
    out = nc.dram_tensor("out", (P, KT, S), mybir.dt.float32, kind="ExternalOutput").ap()
    build(nc, *drams, out)
    got = run_bass_kernel_spmd(nc, [arrays], core_ids=[0]).results[0]["out"]
    return np.ascontiguousarray(np.asarray(got).transpose(2, 1, 0).reshape(1, S, D))
```

```python
import numpy as np
import concourse.bass as bass
import concourse.mybir as mybir

P = 128
S = 512
D = 1024
KT = D // P
TOK = S // P
EPS = 1e-6
H1, DH = 4, 128
G1 = 36
WINDOWS = (2, 4, 8, 16)
SSD_H, SSD_P, SSD_G, XS_T, BC_T, TAPS = 32, 64, 4, 16, 8, 4
QH, QK, NOPE, ROPE, VD = 16, 96, 64, 32, 64
HU = 8
UP_T, TAPS_F = 22, 3
PAD = 8
SLAB = 16 * P

PHASES = [("u", 2), ("q", 2), ("k", 2), ("v", 2), ("o", 2), ("out", 4), ("ff1a", 8), ("ff2a", 8), ("ff1b", 8),
          ("ff2b", 8), ("misc", 2), ("xbc", 12), ("z", 8), ("gates", 8), ("ssd", 8), ("uq", 2), ("ukv", 2),
          ("mla", 4), ("wo", 4), ("upa", 16), ("downa", 8), ("upb", 6), ("downb", 4)]
WIDE = ("ff2a", "ff2b", "ssd", "downa")
OWN_BANKS = ("uq", "ukv")
SLAB0, SLABS, FREED, N_SLABS, _freed, _freed_wide = {}, {}, {}, 0, 0, 2
for _name, _n in PHASES:
    SLAB0[_name], SLABS[_name] = N_SLABS, _n
    N_SLABS += _n
    if _name in WIDE:
        FREED[_name], _freed_wide = _freed_wide, _freed_wide + _n
    elif _name not in OWN_BANKS:
        FREED[_name], _freed = _freed, _freed + 2 * _n

COLS, N_COLS = {}, 0
for _name, _n in [("c", 8), ("b_ada", 48), ("g_mix", 8), ("gate_bias", 1), ("g_head", 4), ("pool_scale", 4),
                  ("g_ffn", 8), ("g_final", 8), ("g_mix2", 8), ("conv_w", 96), ("conv_b", 24), ("dt_bias", 1),
                  ("a_log", 1), ("d_skip", 16), ("ssd_g", 16), ("qa_g", 2), ("kva_g", 1),
                  ("gate_b", 16), ("g_ffn2", 8), ("convf_w", 132), ("convf_b", 44)]:
    COLS[_name] = N_COLS
    N_COLS += _n
SH1, SC1, GT1, SH2, SC2, GT2 = (8 * n for n in range(6))


def build(nc, x_d, slabs_d, ada_d, cols_d, gate_w_d, pool_w_d, consts_d, inv_d, rope_d, qkg_d, out_d):
    f32, f32r, bf16 = mybir.dt.float32, mybir.dt.float32r, mybir.dt.bfloat16
    ALU, ACT, AX = mybir.AluOpType, mybir.ActivationFunctionType, mybir.AxisListType
    base = (nc.sbuf_base + 31) // 32 * 32
    K = 1024

    def at(name, shape, dt, offset):
        return nc.alloc_sbuf_tensor_at(name, [P] + shape, dt, offset=base + offset)

    x = at("x", [KT, S], f32, 0)
    raw = at("raw", [2, SLAB], f32, 16 * K)
    w_hi = at("w_hi", [2, SLAB], f32r, 32 * K)
    w_lo = at("w_lo", [2, SLAB], f32r, 48 * K)
    h = at("h", [2 * KT, S], f32r, 64 * K)
    h_hi, h_lo = h[:, 0:KT, :], h[:, KT:, :]
    A = 96 * K
    Z = A + 106 * K
    cols = at("cols", [N_COLS], f32, Z)
    consts = at("consts", [4, P], f32, Z + 1920)
    ident, keep_up, keep_low, causal = (consts[:, n, :] for n in range(4))
    mask16 = at("mask16", [2, P], bf16, Z + 1920 + 3 * 4 * P)
    mask16_made = at("mask16_made", [2, P], bf16, A + 103 * K)
    ident16, causal16 = mask16[:, 0, :], mask16[:, 1, :]
    mod = at("mod", [48], f32, Z + 3968)
    gain = at("gain", [16], f32, Z + 4160)
    small = at("small", [16], f32, Z + 4224)
    eps, c_act = small[:, 0:1], small[:, 8:16]
    mean = at("mean", [P], f32, Z + 4288)
    ones = at("ones", [P], f32, Z + 4800)
    kr_col = at("kr_col", [TOK, ROPE], f32, Z + 5312)
    sq = at("sq", [2, S], f32, A + 93 * K)
    rs = at("rs", [S], f32, A + 97 * K)
    t0 = at("t0", [S], f32, A + 99 * K)
    t1 = at("t1", [S], f32, A + 101 * K)
    ADA_AT = [0, 8, 16, 24, 32, 40, 53, 69] + [0, 8, 16, 24, 53, 16, 24, 53] + [0, 8, 16, 40] * 2
    ada_chunk = [at(f"ada_chunk_{n}", [2048], f32, A + k * K) for n, k in enumerate(ADA_AT)]
    ada_sum = [at(f"ada_sum_{n}", [2048], f32, A + k * K) for n, k in enumerate((61, 61, 32))]
    UW = S + 2 * PAD
    qk = at("qk", [8, S], f32, A)
    v1 = at("v1", [TOK, S], f32, A + 16 * K)
    og = at("og", [4, S], f32, A + 24 * K)
    u = at("u", [4, UW], f32, A + 32 * K)
    gw = at("gw", [KT, P], f32, A + 77 * K)
    gw_hi = at("gw_hi", [KT, P], f32r, A + 81 * K)
    gw_lo = at("gw_lo", [KT, P], f32r, A + 85 * K)
    win = at("win", [2, UW], f32, A + 41 * K)
    mixed1 = at("mixed1", [4, S], f32, A + 77 * K)
    p1 = at("p1", [2, 1280], f32, A + 41 * K)
    y_hi = at("y_hi", [8, S], f32r, A + 53 * K)
    y_lo = at("y_lo", [8, S], f32r, A + 69 * K)
    rows = at("rows", [4, S], f32, A + 85 * K)
    hm = at("hm", [H1, S], f32, A + 69 * K)
    den_col = at("den_col", [2, TOK], f32, A + 87 * K)
    num1 = at("num1", [S], f32, A + 24 * K)
    floor_col = at("floor_col", [TOK, G1], f32, A + 26 * K)
    rs_h = at("rs_h", [H1, S], f32, A + 85 * K)
    inv = at("inv", [4, S], f32, A + 69 * K)
    neg_max = at("neg_max", [S], f32, A + 103 * K)
    neg_m = at("neg_m", [S], f32, A + 99 * K)
    a_col = at("a_col", [TOK, G1], f32, A + 40 * K + 256)
    pool_w = at("pool_w", [4, P], f32, A + 51 * K)
    a_hi = at("a_hi", [16, S], f32r, A)
    a_lo = at("a_lo", [16, S], f32r, A + 32 * K)
    relu = at("relu", [2, S], f32, A + 64 * K)
    asq = at("asq", [S], f32, A + 68 * K)
    xbc = at("xbc", [XS_T + BC_T, S], f32, A)
    qa = at("qa", [3, S], f32, A + 48 * K)
    mz = at("mz", [S], f32, A + 54 * K)
    xdt = at("xdt", [TOK, SSD_H * SSD_P], f32, A + 56 * K)
    cpad = at("cpad", [2, S + 4], f32, A + 56 * K)
    cacc = at("cacc", [2, S], f32, A + 62 * K)
    sm = at("sm", [1280], f32, A + 88 * K)
    p2 = at("p2", [2, 1280], f32, A + 93 * K)
    drow = at("drow", [4, S], f32, A + 88 * K)
    acum = at("acum", [S], f32, A + 103 * K)
    nac_col = at("nac_col", [TOK, SSD_H], f32, A + 105 * K)
    dt_col = at("dt_col", [TOK, SSD_H], f32, A + 105 * K + 512)
    rope = at("rope", [2, TOK, ROPE // 2], f32, A + 87 * K)
    qk_g = at("qk_g", [2, QK], f32, A + 104 * K)
    zt = at("zt", [S], f32, A + 54 * K)
    rs_g = at("rs_g", [SSD_G, S], f32, A + 97 * K)
    sq_l = at("sq_l", [3, S], f32, A + 88 * K)
    rs_l = at("rs_l", [2, S], f32, A + 88 * K)
    ys_hi = at("ys_hi", [XS_T, S], f32r, A + 56 * K)
    ys_lo = at("ys_lo", [XS_T, S], f32r, A)
    mix = at("mix", [8, S], f32, A + 32 * K)
    gm = at("gm", [8, S], f32, A + 88 * K)
    q2 = at("q2", [QH, S], f32, 64 * K)
    k2 = at("k2", [QH, S], f32, A)
    v2 = at("v2", [TOK, QH * VD], f32, A + 56 * K)
    qn_hi = at("qn_hi", [3, S], f32r, A + 72 * K)
    qn_lo = at("qn_lo", [3, S], f32r, A + 78 * K)
    tt_at = [at(f"tt_{k}", [HU, QK], f32, A + k * K) for k in (48, 51, 56, 72)]
    tsq = at("tsq", [HU, QK], f32, A + 84 * K)
    trope = at("trope", [4, HU, ROPE // 2], f32, A + 54 * K)
    stat = at("stat", [2, 3, HU], f32, A + 87 * K + 512)
    p3 = [at(f"p3_{n}", [1280], f32, A + (72, 48)[n] * K) for n in range(2)]
    pt = [at(f"pt_{n}", [1280], f32, A + (77, 82)[n] * K) for n in range(2)]
    mx = at("mx", [2, 3, TOK], f32, A + 87 * K + 768)
    att = at("att", [QH, S], f32r, 64 * K)
    ao = at("ao", [S], f32, A + 53 * K)
    mt = at("mt", [S], f32, A + 84 * K)
    mm_hi = at("mm_hi", [8, S], f32r, A)
    mm_lo = at("mm_lo", [8, S], f32r, A + 16 * K)
    fpad = at("fpad", [2, S + 4], f32, A + 64 * K)
    facc = at("facc", [2, S], f32, A + 70 * K)
    fgate = at("fgate", [S], f32, A + 74 * K)
    fa = at("fa", [S], f32, A + 76 * K)

    banks = [nc.alloc_psum_tensor(f"bank{n}", [P, S], f32) for n in range(8)]
    sems = {}

    def sem(name):
        if name not in sems:
            sems[name] = nc.alloc_semaphore(name)
        return sems[name]

    def col(name, n=0, first=0, rows=P):
        return cols[first:first + rows, bass.ds(COLS[name] + n, 1)]

    class Steps:

        def __init__(self, eng, name):
            self.eng, self.sem, self.n, self.turn, self.per = eng, sem(name), 0, 0, 0

        def __call__(self, ins):
            self.n += 1
            ins.then_inc(self.sem, 1)
            self.eng.wait_ge(self.sem, self.per * self.turn + self.n)

        def tell(self, ins, name, value):
            ins.then_inc(sem(name), 1)
            self.eng.wait_ge(sem(name), value)

        def loop(self, turn, per):
            self.turn, self.per, self.start = turn, per, self.n

        def end(self, turns):
            assert self.n - self.start == self.per, (self.n - self.start, self.per)
            self.n, self.turn, self.per = self.start + self.per * turns, 0, 0

    def spans(back):
        out, used = [], 0
        for j in range(TOK):
            lo, hi = (0, P * (j + 1)) if back else (P * j, S)
            out.append((j, lo, hi, used))
            used += hi - lo
        return out

    def paired(back):
        out, used = [], 0
        for j in (1, 0, 2, 3) if back else (0, 1, 3, 2):
            lo, hi = (0, P * (j + 1)) if back else (P * j, S)
            out.append((j, lo, hi, used))
            used += hi - lo
        return out

    def diagonals(a, back):
        first, wide = (P, a[:, 2 * P:]) if back else (7 * P, a[:, 0:8 * P])
        wide = wide.rearrange("p (r c) -> p r c", r=2)
        near = a[:, first:first + 2 * P].rearrange("p (r c) -> p r c", r=2)
        far = wide[:, :, 3 * P:] if back else wide[:, :, 0:P]
        return far, near

    pool_banks, head_banks = [banks[n] for n in (5, 6, 7, 5)], [banks[n] for n in (4, 6, 2, 3)]

    def tt(n):
        return tt_at[3 if n % 3 == 2 and n >= 8 else n % 3]

    group_banks, latent_banks = [banks[n] for n in (2, 3, 4, 7)], [banks[n] for n in (5, 6)]

    def group_total(g):
        return xbc[:, XS_T + g, :]

    def group_square(pair):
        return xbc[:, XS_T + (SSD_G if pair % 4 else 0) + pair // 4, :]

    def score_place(j):
        return ((1, 0), (2, 0), (3, 0), (3, 256))[j]

    block = nc.Block()
    with block:
        @block.sync
        def _(sp):
            sp.dma_start(cols[:], cols_d).then_inc(sem("cols_in"), 16)
            for k in range(0, KT, 4):
                sp.dma_start(x[:, k:k + 4, :], x_d[:, k:k + 4, :]).then_inc(sem("x_in"), 16)
            sp.dma_start(consts[:], consts_d).then_inc(sem("consts_in"), 16)
            sp.dma_start(gw[:], gate_w_d).then_inc(sem("gate_w_in"), 16)
            sp.dma_start(pool_w[:], pool_w_d).then_inc(sem("pool_w_in"), 16)
            for slot in range(2):
                sp.dma_start(raw[:, slot, :], slabs_d[slot, :, :]).then_inc(sem(f"raw_in{slot}"), 16)
            with sp.Fori(1, N_SLABS // 2) as i:
                for slot in range(2):
                    sp.wait_ge(sem("w_split"), 2 * i + slot - 1)
                    sp.dma_start(raw[:, slot, :], slabs_d[2 * i + slot, :, :]).then_inc(sem(f"raw_in{slot}"), 16)
            for m in range(KT):
                sp.wait_ge(sem("x_final"), m + 1)
                sp.dma_start(out_d[:, m, :], x[:, m, :]).then_inc(sem("out_sent"), 16)
            sp.wait_ge(sem("out_sent"), 16 * KT)

        @block.gpsimd
        def _(pool):
            def split(slot, nth):
                pool.tensor_tensor(w_hi[:, slot, :], raw[:, slot, :], ones[:, 0:1].to_broadcast([P, SLAB]),
                                   ALU.mult).then_inc(sem("w_head"), 1)
                pool.wait_ge(sem("w_head"), nth)
                pool.tensor_tensor(w_lo[:, slot, :], raw[:, slot, :], w_hi[:, slot, :].bitcast(f32),
                                   ALU.subtract).then_inc(sem("w_split"), 1)

            pool.wait_ge(sem("set"), 1)
            for slot in range(2):
                pool.wait_ge(sem(f"raw_in{slot}"), 16)
                split(slot, slot + 1)
            with pool.Fori(1, N_SLABS // 2) as i:
                for slot in range(2):
                    pool.wait_ge(sem(f"raw_in{slot}"), 16 * i + 16)
                    pool.wait_ge(sem("tile_done"), 4 * i + 2 * slot - 2)
                    pool.wait_ge(sem("w_split"), 2 * i + slot - 1)
                    split(slot, 2 * i + slot + 1)

        @block.scalar
        def _(act):
            do = Steps(act, "act_step")
            n_sq, n_root = 0, 0

            def fn(out, in_, f, **kw):
                return act.activation(out, in_, f, **kw)

            def tile_ready(name, t):
                act.wait_ge(sem("tile_done"), 2 * SLAB0[name] + t + 1)

            def free(ins, name, t):
                do.tell(ins, "bank_free", FREED[name] + t + 1)

            def squares(tiles, buf):
                nonlocal n_sq
                for tile in tiles:
                    if n_sq >= 2:
                        act.wait_ge(sem("sq_used"), n_sq - 1)
                    n_sq += 1
                    do.tell(fn(buf[:, (n_sq - 1) % 2, :], tile, ACT.Square), "sq_ready", n_sq)

            def root(buf, totals=None):
                nonlocal n_root
                if totals is None:
                    act.wait_ge(sem("sq_used"), n_sq)
                else:
                    act.wait_ge(sem("total_used"), totals)
                if n_root:
                    act.wait_ge(sem("root_used"), n_root)
                n_root += 1
                do.tell(fn(buf[:], banks[7][:], ACT.Sqrt, bias=eps), "root_ready", n_root)

            def norm():
                squares([x[:, k, :] for k in range(KT)], sq)
                root(rs)

            def heads(stage, shift=None):
                for k in range(KT):
                    n = KT * (stage - 1) + k + 1
                    act.wait_ge(sem("h_scaled"), n)
                    src = (t0, t1)[k % 2]
                    if shift is None:
                        do.tell(fn(h_hi[:, k, :], src[:], ACT.Copy), "h_head", n)
                    else:
                        do.tell(fn(h_hi[:, k, :], src[:], ACT.Identity, bias=mod[:, shift + k:shift + k + 1]), "h_head", n)

            def ada_load(n):
                act.dma_start(ada_chunk[n][:], ada_d[n, :, :]).then_inc(sem(f"ada_in{n}"), 16)

            for n in range(KT):
                ada_load(n)
            act.wait_ge(sem("cols_in"), 16)
            act.wait_ge(sem("set"), 1)
            do.tell(fn(c_act, cols[:, COLS["c"]:COLS["c"] + KT], ACT.Silu), "c_ready", 1)
            act.wait_ge(sem("x_in"), 32)
            norm()
            for n in range(KT, KT + 5):
                act.wait_ge(sem("ada_used"), ADA_AT.index(ADA_AT[n]) + 1)
                ada_load(n)
            act.wait_ge(sem("ada_used"), KT)
            heads(1, SH1)
            act.dma_start(inv[:], inv_d).then_inc(sem("inv_in"), 16)
            act.wait_ge(sem("u_zeroed"), 1)
            for t in range(4):
                tile_ready("u", t)
                free(fn(u[:, t, PAD:PAD + S], banks[t % 2][:], ACT.Copy), "u", t)
            act.wait_ge(sem("gates_done"), 1)
            do(fn(rows[0:G1, 0, :], banks[4][0:G1, :], ACT.Identity, bias=col("gate_bias", 0, 0, G1)))
            do.tell(fn(rows[0:G1, 1, :], banks[4][64:64 + G1, :], ACT.Identity, bias=col("gate_bias", 0, 64, G1)),
                    "gates_biased", 1)
            act.wait_ge(sem("gate_negabs"), 1)
            do.tell(fn(rows[0:G1, 2, :], rows[0:G1, 2, :], ACT.Exp), "gate_exp", 1)
            act.wait_ge(sem("gate_onep"), 1)
            do.tell(fn(neg_m[0:G1, :], rows[0:G1, 3, :], ACT.Ln), "gate_ln", 1)
            for name, first, scale in (("q", 0, DH ** -0.5), ("k", 4, 1.0)):
                act.wait_ge(sem("ada_used"), KT + 1 + first // 4)
                for t in range(4):
                    tile_ready(name, t)
                    free(fn(qk[:, first + t, :], banks[t % 2][:], ACT.Copy, scale=scale), name, t)
                if name == "q":
                    for n in range(KT + 5, 2 * KT):
                        act.wait_ge(sem("ada_used"), n - 2)
                        ada_load(n)
                else:
                    act.wait_ge(sem("a_turned"), 1)
                    do.tell(fn(a_col[:], banks[4][:, 0:TOK * G1].rearrange("p (t g) -> p t g", t=TOK), ACT.Copy),
                            "a_col_ready", 1)
            act.wait_ge(sem("ada_used"), 2 * KT - 1)
            for c in range(2):
                for m in range(2):
                    tile_ready("v", 2 * c + m)
                    free(fn(v1[:, 2 * m:2 * m + 2, 256 * c:256 * c + 256],
                            banks[m][:].rearrange("p (t e) -> p t e", t=2), ACT.Copy), "v", 2 * c + m)
            do.tell(fn(floor_col[:], banks[2][:, 0:TOK * G1].rearrange("p (t g) -> p t g", t=TOK), ACT.Exp), "floor_made", 1)

            def take(n):
                act.wait_ge(sem("pv1_done"), n + 1)
                if n:
                    act.wait_ge(sem("h1_made"), n)
                do.tell(fn(num1[:], banks[5][:], ACT.Copy), "h1_taken", n + 1)

            for n in range(2 * H1):
                head, back = n // 2, n % 2
                r = 32 * back + head
                act.wait_ge(sem("bc1_done"), n + 1)
                if n >= 2:
                    act.wait_ge(sem("h1_made"), n - 1)
                for j, lo, hi, used in paired(back):
                    ins = fn(p1[:, back, used:used + hi - lo], banks[4][:, lo:hi], ACT.Exp, bias=a_col[:, j, r:r + 1])
                    if used + hi - lo < 1280:
                        do(ins)
                    else:
                        do.tell(ins, "e1_made", n + 1)
                if n:
                    take(n - 1)
            take(2 * H1 - 1)
            for head in range(H1):
                act.wait_ge(sem("hm_made"), head + 1)
                squares([hm[:, head, :]], sq)
            for n in range(2 * KT, 2 * KT + 4):
                ada_load(n)
            act.wait_ge(sem("sq_used"), n_sq)
            for head in range(H1):
                do.tell(fn(rs_h[:, head, :], head_banks[head][:], ACT.Sqrt, bias=eps), "head_root", head + 1)
            for t in range(4):
                tile_ready("o", t)
                free(fn(og[:, t, :], banks[t % 2][:], ACT.Sigmoid), "o", t)
            for n in range(2 * KT + 4, 3 * KT):
                act.wait_ge(sem("ada_used"), n - 3)
                ada_load(n)
            root(rs, totals=1)
            heads(2, SH2)
            for half, name in enumerate(("ff1a", "ff1b")):
                with act.Fori(0, SLABS[name] // 2) as i:
                    for t in range(4):
                        act.wait_ge(sem("tile_done"), 4 * i + 2 * SLAB0[name] + t + 1)
                        if half or t >= 2:
                            act.wait_ge(sem("relu_used"), 4 * i + 16 * half + t - 1)
                        else:
                            act.wait_ge(sem("relu_used"), 4 * i + t)
                        do.tell(fn(relu[:, t % 2, :], banks[t % 2][:], ACT.Relu), "bank_free", 4 * i + FREED[name] + t + 1)
            root(rs, totals=2)
            for k in range(KT):
                act.wait_ge(sem("x_scaled"), k + 1)
                squares([x[:, k, :]], sq)
            root(rs)
            heads(3)
            for t in range(4):
                tile_ready("misc", t)
                free(fn(qa[:, t, :] if t < 3 else mz[:], banks[t % 2][:], ACT.Copy), "misc", t)
            act.wait_ge(sem("dt_negabs"), 1)
            do.tell(fn(drow[0:32, 1, :], drow[0:32, 1, :], ACT.Exp), "dt_exp", 1)
            act.wait_ge(sem("dt_onep"), 1)
            do(fn(small[0:32, 1:2], col("a_log", 0, 0, 32), ACT.Exp))
            do.tell(fn(drow[0:32, 3, :], drow[0:32, 2, :], ACT.Ln), "dt_ln", 1)
            act.wait_ge(sem("cpad_zeroed"), 1)
            def conv_in(i, t):
                act.wait_ge(sem("tile_done"), 4 * i + 2 * SLAB0["xbc"] + t + 1)
                if not isinstance(i, int) or 4 * i + t > 1:
                    act.wait_ge(sem("conv_done"), 4 * i + t - 1)
                do.tell(fn(cpad[:, t % 2, TAPS - 1:TAPS - 1 + S], banks[t % 2][:], ACT.Copy), "bank_free",
                        4 * i + FREED["xbc"] + t + 1)

            def conv_out(i, t):
                act.wait_ge(sem("conv_done"), 4 * i + t + 1)
                do.tell(fn(xbc[:, 4 * i + t, :], cacc[:, t % 2, :], ACT.Silu), "xbc_ready", 4 * i + t + 1)

            turns = SLABS["xbc"] // 2
            conv_in(0, 0)
            with act.Fori(0, turns - 1) as i:
                for t in range(4):
                    conv_in(i, t + 1)
                    conv_out(i, t)
            for t in range(4):
                if t < 3:
                    conv_in(turns - 1, t + 1)
                conv_out(turns - 1, t)
            act.wait_ge(sem("dt_turned"), 1)
            for b, place in ((4, nac_col), (5, dt_col)):
                do(fn(place[:], banks[b][:, 0:P].rearrange("p (t g) -> p t g", t=TOK), ACT.Copy))
            do.tell(fn(kr_col[:], banks[6][:].rearrange("p (t g) -> p t g", t=TOK)[:, :, 64:64 + ROPE], ACT.Copy),
                    "dt_col_ready", 1)
            def half_tanh(pair):
                act.wait_ge(sem("tile_done"), 2 * SLAB0["z"] + pair + 1)
                if pair:
                    act.wait_ge(sem("z_used"), pair)
                do.tell(fn(zt[:], banks[0][:], ACT.Tanh, scale=0.5), "z_tanh", pair + 1)

            def pair_square(pair):
                act.wait_ge(sem("z_used"), pair + 1)
                if pair % 4 >= 2:
                    act.wait_ge(sem("square_added"), pair - pair // 4 - 1)
                do.tell(fn(group_square(pair), xbc[:, pair, :], ACT.Square), "pair_squared", pair + 1)

            for hd in range(SSD_H):
                if hd % 2 and hd > 1:
                    half_tanh(hd // 2 - 1)
                    if hd > 3:
                        pair_square(hd // 2 - 2)
                act.wait_ge(sem("diagonal_made"), hd + 1)
                e2 = p2[:, hd % 2, :]
                for j, lo, hi, used in paired(0):
                    if j < TOK - 1:
                        do(fn(e2[:, used + P:used + hi - lo], banks[4 + hd % 2][:, lo + P:hi], ACT.Exp, bias=nac_col[:, j, hd:hd + 1]))
                two, two_more = diagonals(e2, 0)
                do(fn(two, two, ACT.Exp))
                do.tell(fn(two_more, two_more, ACT.Exp), "e2_made", hd + 1)
            half_tanh(XS_T - 1)
            for pair in range(XS_T - 2, XS_T):
                pair_square(pair)
            for k in range(3):
                do.tell(fn(sq_l[:, k, :], qa[:, k, :], ACT.Square), "latent_squares", k + 1)
            for g in range(SSD_G):
                act.wait_ge(sem("group_mean"), g + 1)
                do.tell(fn(rs_g[:, g, :], group_banks[g][:], ACT.Sqrt, bias=eps), "group_root", g + 1)
            act.wait_ge(sem("latent_mean"), 2)
            for n, width in enumerate((2 * P, P)):
                do.tell(fn(rs_l[:, n, :], latent_banks[n][:], ACT.Sqrt, scale=4 * P / width, bias=eps), "latent_root", n + 1)
            for t in range(16):
                tile_ready("gates", t)
                if t == 8:
                    act.wait_ge(sem("latents_scaled"), 3)
                free(fn(mix[:, t, :] if t < 8 else gm[:, t - 8, :], banks[t % 2][:], ACT.Sigmoid, bias=col("gate_b", t)),
                     "gates", t)
            act.wait_ge(sem("mix_made"), 8)
            act.dma_start(rope[:], rope_d).then_inc(sem("rope_in"), 16)
            act.dma_start(qk_g[:], qkg_d).then_inc(sem("rope_in"), 16)
            def unit_in(n):
                keys, c, tok = n // 8, n // 4 % 2, n % 4
                if n % 2:
                    act.wait_ge(sem("tile_done"), 2 * (SLAB0["uq"] + n // 4) + n % 4 // 2 + 1)
                else:
                    act.wait_ge(sem("unit_done"), n // 2 + 1)
                if n >= 3:
                    act.wait_ge(sem("heads_turned"), n - 2)
                for half in range(2):
                    bank = banks[2 * (n % 2) + half]
                    part = slice(4 * half, 4 * half + 4)
                    if keys:
                        src = bank[:].rearrange("p (h e) -> p h e", h=4)
                        do(fn(tt(n)[:, part, 0:NOPE], src[:, :, 0:NOPE], ACT.Copy))
                        h0 = VD * (8 * c + 4 * half)
                        do(fn(v2[:, tok, h0:h0 + 4 * VD].rearrange("p (h e) -> p h e", h=4), src[:, :, NOPE:], ACT.Copy))
                        if half == 0:
                            do(fn(tt(n)[:, :, NOPE:QK], kr_col[:, tok, :].unsqueeze(1).to_broadcast([P, HU, ROPE]), ACT.Copy))
                    else:
                        do(fn(tt(n)[:, part, :], bank[:, 0:4 * QK].rearrange("p (h e) -> p h e", h=4), ACT.Copy))
                do.tell(fn(tsq[:], tt(n)[:], ACT.Square), "unit_squared", n + 1)

            def unit_out(n):
                keys, c, tok = n // 8, n // 4 % 2, n % 4
                act.wait_ge(sem("heads_turned"), n + 1)
                for half in range(2):
                    h0 = 8 * c + 4 * half
                    ins = fn((k2 if keys else q2)[0:QK, h0:h0 + 4, P * tok:P * tok + P],
                             banks[4 + 2 * (n % 2) + half][0:QK, :].rearrange("p (h t) -> p h t", h=4), ACT.Copy)
                    if half:
                        do.tell(ins, "heads_ready", n + 1)
                    else:
                        do(ins)

            act.wait_ge(sem("qn_made"), 3)
            def unit_root(n):
                act.wait_ge(sem("unit_summed"), n + 1)
                do.tell(fn(stat[:, n % 2, 1, :], stat[:, n % 2, 0, :], ACT.Sqrt, scale=1.0 / QK, bias=eps), "unit_root", n + 1)

            unit_in(0)
            unit_root(0)
            unit_in(1)
            for n in range(16):
                if n + 1 < 16:
                    unit_root(n + 1)
                if n + 2 < 16:
                    unit_in(n + 2)
                if n:
                    unit_out(n - 1)
            unit_out(15)
            for step in range(QH + 1):
                if step < QH:
                    hd = step
                    if hd >= 2:
                        act.wait_ge(sem("p3_turned"), hd - 1)
                    for i, lo, hi, used in spans(1):
                        act.wait_ge(sem("max_made"), TOK * hd + i + 1)
                        do.tell(fn(p3[hd % 2][:, used:used + hi], banks[i][:, 0:hi], ACT.Exp, scale=QK ** -0.5,
                                   bias=mx[:, hd % 2, 1, i:i + 1], accum_out=mx[:, hd % 2, 2, i:i + 1]),
                                "p3_made", TOK * hd + i + 1)
                if step:
                    hd = step - 1
                    place = pt[hd % 2]
                    act.wait_ge(sem("p3_turned"), hd + 1)
                    if hd >= 2:
                        act.wait_ge(sem("pv3_done"), hd - 1)
                    do(fn(place[:, 0:S], banks[4][:], ACT.Copy))
                    do(fn(place[:, S:S + 384], banks[5][:, 0:384], ACT.Copy))
                    do(fn(place[:, S + 384:S + 640], banks[6][:, 0:256], ACT.Copy))
                    do.tell(fn(place[:, S + 640:], banks[5][:, 384:S], ACT.Copy), "pt_made", hd + 1)
            root(rs, totals=3)
            heads(4)
            act.wait_ge(sem("fpad_zeroed"), 1)
            for name, done in (("upa", 0), ("upb", 16)):
                with act.Fori(0, SLABS[name] // 2) as i:
                    for slot in range(2):
                        for m in range(2):
                            t = 2 * slot + m
                            act.wait_ge(sem("tile_done"), 4 * i + 2 * SLAB0[name] + t + 1)
                            act.wait_ge(sem("fa_made"), 2 * i + done + slot)
                            do.tell(fn(fpad[:, m, TAPS_F - 1:TAPS_F - 1 + S], banks[m][:], ACT.Copy), "bank_free",
                                    4 * i + FREED[name] + t + 1)
                        act.wait_ge(sem("fconv_done"), 2 * i + done + slot + 1)
                        do.tell(fn(fgate[:], facc[:, 0, :], ACT.Silu), "fgate_made", 2 * i + done + slot + 1)

        @block.vector
        def _(dve):
            do = Steps(dve, "dve_step")
            n_root = 0

            def free(ins, name, t, which="bank_free"):
                do.tell(ins, which, FREED[name] + t + 1)

            def split(hi, lo, src):
                do(dve.tensor_copy(hi, src))
                return dve.tensor_tensor(lo, src, hi.bitcast(f32), ALU.subtract)

            def inverse_root(buf):
                nonlocal n_root
                n_root += 1
                dve.wait_ge(sem("root_ready"), n_root)
                do(dve.reciprocal(buf[:], buf[:]))

            def add_to_x(name, gate=None, wide=False, total=0, chunk=None):
                for m in range(KT):
                    if chunk is not None:
                        add_chunk(chunk + m)
                    s = SLAB0[name] + (m if wide else m // 2)
                    dve.wait_ge(sem("tile_done"), 2 * s + (2 if wide else m % 2 + 1))
                    bank = banks[(2 if wide else 0) + m % 2]
                    if gate is None:
                        ins = dve.tensor_tensor(x[:, m, :], bank[:], x[:, m, :], ALU.add)
                    else:
                        ins = dve.scalar_tensor_tensor(x[:, m, :], bank[:], mod[:, gate + m:gate + m + 1], x[:, m, :],
                                                       ALU.mult, ALU.add)
                    free(ins, name, m, "bank_free_wide" if wide else "bank_free")
                    if total:
                        square, acc = (sq[:, n, :] for n in range(2))
                        if m == 0:
                            do(dve.tensor_tensor(acc, x[:, m, :], x[:, m, :], ALU.mult))
                        else:
                            do(dve.tensor_tensor(square, x[:, m, :], x[:, m, :], ALU.mult))
                            ins = dve.tensor_tensor(acc, acc, square, ALU.add)
                            if m < KT - 1:
                                do(ins)
                            else:
                                do.tell(ins, "total_ready", total)

            def add_chunk(n):
                acc = ada_sum[n // KT][:]
                dve.wait_ge(sem(f"ada_in{n}"), 16)
                if n % KT == 0:
                    ins = dve.tensor_scalar(acc, ada_chunk[n][:], c_act[:, 0:1], None, ALU.mult)
                else:
                    ins = dve.scalar_tensor_tensor(acc, ada_chunk[n][:], c_act[:, n % KT:n % KT + 1], acc, ALU.mult, ALU.add)
                do.tell(ins, "ada_used", n + 1)

            def mod_third(third, mean_of):
                dve.wait_ge(sem("mod_done"), third + 1)
                part = slice(16 * third, 16 * third + 16)
                first = COLS["b_ada"] + 16 * third
                do(dve.scalar_tensor_tensor(mod[:, part], banks[4][:, 0:16], float(mean_of), cols[:, first:first + 16],
                                            ALU.mult, ALU.add))

            def mod_gain(first, scale, name):
                do(dve.scalar_tensor_tensor(gain[:, first:first + KT], mod[:, scale:scale + KT], 1.0,
                                            cols[:, COLS[name]:COLS[name] + KT], ALU.add, ALU.mult))

            def modulated(stage, scale, shift=None):
                inverse_root(rs)
                first = KT * (stage - 1)

                def scaled(k):
                    do.tell(dve.scalar_tensor_tensor((t0, t1)[k % 2][:], x[:, k, :], scale(k), rs[:], ALU.mult, ALU.mult),
                            "h_scaled", first + k + 1)

                scaled(0)
                for k in range(KT):
                    if k + 1 < KT:
                        scaled(k + 1)
                    dve.wait_ge(sem("h_head"), first + k + 1)
                    src, head = (t0, t1)[k % 2][:], h_hi[:, k, :].bitcast(f32)
                    if shift is None:
                        ins = dve.tensor_tensor(h_lo[:, k, :], src, head, ALU.subtract)
                    else:
                        ins = dve.scalar_tensor_tensor(h_lo[:, k, :], src, mod[:, shift + k:shift + k + 1], head,
                                                       ALU.add, ALU.subtract)
                    do.tell(ins, "h_ready", first + k + 1)
                do.tell(dve.tensor_copy(small[:, 2:3], small[:, 0:1]), "root_used", n_root)

            do(dve.memset(small[:], EPS))
            do(dve.memset(ones[:], 1.0))
            do.tell(dve.memset(mean[:], 1.0 / D), "set", 1)
            dve.wait_ge(sem("consts_in"), 16)
            do(dve.tensor_copy(mask16_made[:, 0, :], ident))
            do(dve.tensor_copy(mask16_made[:, 1, :], causal))
            do.tell(dve.tensor_copy(mask16[:], mask16_made[:]), "mask_made", 1)
            for n in range(2):
                do.tell(dve.memset(small[:, 3:4], 0.0), "bank_free_wide", n + 1)
            dve.wait_ge(sem("c_ready"), 1)
            for n in range(KT):
                add_chunk(n)
            mod_third(0, D)
            mod_gain(0, SC1, "g_mix")
            modulated(1, lambda k: gain[:, k:k + 1], SH1)
            dve.wait_ge(sem("gate_w_in"), 16)
            do.tell(split(gw_hi[:], gw_lo[:], gw[:]), "gate_w_split", 1)
            do.tell(dve.memset(u[:], 0.0), "u_zeroed", 1)
            for n in range(KT, KT + 5):
                add_chunk(n)
            dve.wait_ge(sem("gates_biased"), 1)
            li, lf, r2, r3 = (rows[0:G1, n, :] for n in range(4))
            ge, gs = neg_max[0:G1, :], neg_m[0:G1, :]
            do.tell(dve.scalar_tensor_tensor(r2, lf, -1.0, lf, ALU.mult, ALU.min), "gate_negabs", 1)
            dve.wait_ge(sem("gate_exp"), 1)
            do.tell(dve.tensor_scalar(r3, r2, 1.0, None, ALU.add), "gate_onep", 1)
            do(dve.scalar_tensor_tensor(r2, r3, -1.0, r2, ALU.add, ALU.subtract))
            dve.wait_ge(sem("gate_ln"), 1)
            do(dve.reciprocal(r3, r3))
            do(dve.tensor_tensor(r2, r2, r3, ALU.mult))
            do(dve.tensor_tensor(r2, gs, r2, ALU.subtract))
            do(dve.scalar_tensor_tensor(lf, lf, 0.0, r2, ALU.min, ALU.subtract))
            do(dve.memset(r3, 1.0))

            def scan(out, data0, data1, first, op0, op1, initial):
                rows_ = slice(first, first + H1)
                turn = slice(None, None, -1) if first else slice(None)
                do(dve.tensor_tensor_scan(out[rows_, turn], data0[rows_, turn], data1[rows_, turn], initial, op0, op1))

            total, a, top = r2, li, ge
            do(dve.memset(total, 0.0))
            do(dve.memset(top, 0.0))
            for first in (0, 32):
                scan(rows[:, 2, :], rows[:, 3, :], rows[:, 1, :], first, ALU.mult, ALU.add, 0.0)
            do(dve.tensor_tensor(a, li, total, ALU.subtract))
            for first in (0, 32):
                scan(neg_max[:], rows[:, 0, :], rows[:, 0, :], first, ALU.max, ALU.max, 0.0)
            do(dve.scalar_tensor_tensor(gs, total, -1.0, top, ALU.mult, ALU.subtract))
            do.tell(dve.tensor_scalar(ge, top, -1.0, None, ALU.mult), "gate_rows", 1)
            do.tell(dve.memset(mean[:], 1.0 / DH), "mean_set", 1)
            do(dve.memset(win[:], 0.0))
            dve.wait_ge(sem("inv_in"), 16)
            for g, size in enumerate(WINDOWS):
                dve.wait_ge(sem("bank_free"), FREED["u"] + g + 1)
                do(dve.tensor_tensor(win[:, 0, 1:UW], u[:, g, 0:UW - 1], u[:, g, 1:UW], ALU.add))
                w, reach, margin = 0, 1, 1
                while 2 * reach < size:
                    a0, a1 = margin + reach, UW - margin - reach
                    do(dve.tensor_tensor(win[:, 1 - w, a0:a1], win[:, w, a0 - reach:a1 - reach],
                                         win[:, w, a0 + reach:a1 + reach], ALU.add))
                    margin, w, reach = margin + reach, 1 - w, 2 * reach
                do(dve.tensor_tensor(mixed1[:, g, :], win[:, w, PAD:PAD + S], inv[:, g, :], ALU.mult))
                do.tell(dve.tensor_tensor(mixed1[:, g, :], mixed1[:, g, :], u[:, g, PAD:PAD + S], ALU.subtract), "pooled", g + 1)
            for n in range(KT + 5, 2 * KT):
                add_chunk(n)
            mod_third(1, DH)
            for g in range(4):
                dve.wait_ge(sem("pool_done"), g + 1)
                do(dve.tensor_scalar(t1[:], pool_banks[g][:], col("pool_scale", g), None, ALU.mult))
                do.tell(split(y_hi[:, 4 + g, :], y_lo[:, 4 + g, :], t1[:]), "y_ready", g + 1)
            def weighted(n):
                head, back = n // 2, n % 2
                place = p1[:, back, :]
                dve.wait_ge(sem("e1_made"), n + 1)
                dve.wait_ge(sem("s1_done"), head + 1)
                for j, lo, hi, used in paired(back):
                    part = place[:, used:used + hi - lo]
                    do(dve.scalar_tensor_tensor(part, part, 1.0, banks[j][:, lo:hi], ALU.min, ALU.mult))
                keep = (keep_low if back else keep_up).unsqueeze(1).to_broadcast([P, 2, P])
                two, two_more = diagonals(place, back)
                do(dve.tensor_tensor(two, two, keep, ALU.mult))
                do.tell(dve.tensor_tensor(two_more, two_more, keep, ALU.mult), "p1_made", n + 1)

            def inverted(n):
                head, back = n // 2, n % 2
                den, sums = den_col[:, back, :], banks[6][:, 0:TOK]
                dve.wait_ge(sem("den1_done"), n + 1)
                do(dve.scalar_tensor_tensor(den, sums, -1.0, floor_col[:, :, 32 * back + head], ALU.mult, ALU.max))
                do(dve.tensor_tensor(den, den, sums, ALU.max))
                do.tell(dve.reciprocal(den, den), "den1_inverted", n + 1)

            def normalised(n):
                head, back = n // 2, n % 2
                dve.wait_ge(sem("h1_taken"), n + 1)
                dve.wait_ge(sem("den1_spread"), n + 1)
                do.tell(dve.tensor_tensor(t1[:] if back else hm[:, head, :], num1[:], banks[7][:], ALU.mult), "h1_made", n + 1)
                if back:
                    do.tell(dve.tensor_tensor(hm[:, head, :], hm[:, head, :], t1[:], ALU.add), "hm_made", head + 1)

            for n in range(2 * H1):
                weighted(n)
                if n:
                    normalised(n - 1)
                inverted(n)
            normalised(2 * H1 - 1)
            for head in range(H1):
                dve.wait_ge(sem("head_root"), head + 1)
                do(dve.reciprocal(rs_h[:, head, :], rs_h[:, head, :]))
                do(dve.scalar_tensor_tensor(hm[:, head, :], hm[:, head, :], col("g_head", head), rs_h[:, head, :],
                                            ALU.mult, ALU.mult))
            do.tell(dve.memset(mean[:], 1.0 / D), "mean_set", 2)
            for head in range(H1):
                dve.wait_ge(sem("bank_free"), FREED["o"] + head + 1)
                do(dve.tensor_tensor(t1[:], hm[:, head, :], og[:, head, :], ALU.mult))
                do.tell(split(y_hi[:, head, :], y_lo[:, head, :], t1[:]), "y_ready", 4 + head + 1)
            add_to_x("out", GT1, total=1, chunk=2 * KT)
            mod_third(2, D)
            mod_gain(8, SC2, "g_ffn")
            modulated(2, lambda k: gain[:, 8 + k:9 + k], SH2)
            for half, (up, down) in enumerate((("ff1a", "ff2a"), ("ff1b", "ff2b"))):
                with dve.Fori(0, SLABS[up] // 2) as i:
                    do.loop(i, 4)
                    for t in range(4):
                        dve.wait_ge(sem("bank_free"), 4 * i + FREED[up] + t + 1)
                        do.tell(dve.tensor_tensor(asq[:], relu[:, t % 2, :], relu[:, t % 2, :], ALU.mult), "relu_used",
                                4 * i + 16 * half + t + 1)
                        place = 4 * i + t
                        do(dve.tensor_copy(a_hi[:, place, :], asq[:]))
                        do.tell(dve.tensor_tensor(a_lo[:, place, :], asq[:], a_hi[:, place, :].bitcast(f32), ALU.subtract),
                                "a_ready", 4 * i + 16 * half + t + 1)
                do.end(SLABS[up] // 2)
                add_to_x(down, GT2, wide=True, total=2 * half)
            inverse_root(rs)
            for k in range(KT):
                do.tell(dve.scalar_tensor_tensor(x[:, k, :], x[:, k, :], col("g_final", k), rs[:], ALU.mult, ALU.mult),
                        "x_scaled", k + 1)
            do.tell(dve.tensor_copy(small[:, 2:3], small[:, 0:1]), "root_used", n_root)
            modulated(3, lambda k: col("g_mix2", k))
            dve.wait_ge(sem("bank_free"), FREED["misc"] + 4)
            d0, d1, d2, d3 = (drow[0:32, n, :] for n in range(4))
            do(dve.tensor_scalar(d0, mz[0:32, :], col("dt_bias", 0, 0, 32), None, ALU.add))
            do.tell(dve.scalar_tensor_tensor(d1, d0, -1.0, d0, ALU.mult, ALU.min), "dt_negabs", 1)
            dve.wait_ge(sem("dt_exp"), 1)
            do.tell(dve.tensor_scalar(d2, d1, 1.0, None, ALU.add), "dt_onep", 1)
            do(dve.scalar_tensor_tensor(d1, d2, -1.0, d1, ALU.add, ALU.subtract))
            dve.wait_ge(sem("dt_ln"), 1)
            do(dve.reciprocal(d2, d2))
            do(dve.tensor_tensor(d1, d1, d2, ALU.mult))
            do(dve.tensor_tensor(d3, d3, d1, ALU.subtract))
            do(dve.scalar_tensor_tensor(d0, d0, 0.0, d3, ALU.max, ALU.add))
            do(dve.tensor_scalar(d1, d0, small[0:32, 1:2], -1.0, ALU.mult, ALU.mult))
            do(dve.memset(d2, 1.0))
            do(dve.tensor_tensor_scan(acum[0:32, :], d2, d1, 0.0, ALU.mult, ALU.add))
            do.tell(dve.tensor_scalar(d3, acum[0:32, :], -1.0, None, ALU.mult), "dt_rows", 1)
            do.tell(dve.memset(cpad[:], 0.0), "cpad_zeroed", 1)
            with dve.Fori(0, SLABS["xbc"] // 2) as i:
                do.loop(i, 4 * (TAPS - 1))
                for t in range(4):
                    n = 4 * i + t
                    dve.wait_ge(sem("bank_free"), 4 * i + FREED["xbc"] + t + 1)
                    if t >= 2:
                        dve.wait_ge(sem("xbc_ready"), 4 * i + t - 1)
                    else:
                        dve.wait_ge(sem("xbc_ready"), 4 * i)
                    acc, pad = cacc[:, t % 2, :], cpad[:, t % 2, :]
                    do(dve.tensor_scalar(acc, pad[:, 0:S], col("conv_w", TAPS * n), col("conv_b", n), ALU.mult, ALU.add))
                    for tap in range(1, TAPS):
                        ins = dve.scalar_tensor_tensor(acc, pad[:, tap:tap + S], col("conv_w", TAPS * n + tap), acc,
                                                       ALU.mult, ALU.add)
                        if tap < TAPS - 1:
                            do(ins)
                        else:
                            do.tell(ins, "conv_done", 4 * i + t + 1)
            do.end(SLABS["xbc"] // 2)
            dve.wait_ge(sem("dt_col_ready"), 1)
            for n in range(TOK * 4):
                tok, quad = n // 4, n % 4
                dve.wait_ge(sem("xs_turned"), n + 1)
                scale = dt_col[:, tok, 8 * quad:8 * quad + 8].unsqueeze(2).to_broadcast([P, 8, SSD_P])
                do.tell(dve.tensor_tensor(xdt[:, tok, S * quad:S * quad + S].rearrange("p (h e) -> p h e", h=8),
                                          banks[n % 4][:].rearrange("p (h e) -> p h e", h=8), scale, ALU.mult),
                        "xdt_made", n + 1)
            def gated_pair(pair):
                y = xbc[:, pair, :]
                dve.wait_ge(sem("pv2_done"), 2 * pair + 2)
                do.tell(dve.scalar_tensor_tensor(y, y, col("d_skip", pair), banks[6 + pair % 2][:], ALU.mult, ALU.add),
                        "ys_made", pair + 1)
                dve.wait_ge(sem("z_tanh"), pair + 1)
                free(dve.scalar_tensor_tensor(zt[:], zt[:], 1.0, banks[0][:], ALU.add, ALU.mult), "z", pair)
                do.tell(dve.scalar_tensor_tensor(y, zt[:], 0.5, y, ALU.mult, ALU.mult), "z_used", pair + 1)

            def add_square(pair):
                if pair % 4:
                    dve.wait_ge(sem("pair_squared"), pair + 1)
                    total = group_total(pair // 4)
                    do.tell(dve.tensor_tensor(total, total, group_square(pair), ALU.add), "square_added", pair - pair // 4)

            do.tell(dve.memset(mean[:], 1.0 / (4 * P)), "mean_set", 3)

            def diagonal_exponents(hd):
                dve.wait_ge(sem("bc2_done"), hd + 1)
                if hd >= 2:
                    dve.wait_ge(sem("pv2_done"), hd - 1)
                for nth, (j, lo, hi, used) in enumerate(paired(0)):
                    ins = dve.tensor_scalar(p2[:, hd % 2, used:used + P], banks[4 + hd % 2][:, lo:lo + P], nac_col[:, j, hd:hd + 1],
                                            0.0, ALU.add, ALU.min)
                    if nth < TOK - 1:
                        do(ins)
                    else:
                        do.tell(ins, "diagonal_made", hd + 1)

            def masked_scores(g):
                dve.wait_ge(sem("s2_done"), g + 1)
                for j, lo, hi, used in paired(0):
                    bank, first = score_place(j)
                    do(dve.tensor_copy(sm[:, used:used + hi - lo], banks[bank][:, first:first + hi - lo]))
                two, two_more = diagonals(sm, 0)
                keep = keep_up.unsqueeze(1).to_broadcast([P, 2, P])
                do(dve.tensor_tensor(two, two, keep, ALU.mult))
                do.tell(dve.tensor_tensor(two_more, two_more, keep, ALU.mult), "sm_made", g + 1)

            def weighted_scores(hd):
                if hd % 8 == 0:
                    masked_scores(hd // 8)
                dve.wait_ge(sem("e2_made"), hd + 1)
                do.tell(dve.tensor_tensor(p2[:, hd % 2, :], p2[:, hd % 2, :], sm[:], ALU.mult), "p2_made", hd + 1)

            diagonal_exponents(0)
            weighted_scores(0)
            for pair in range(XS_T):
                odd = 2 * pair + 1
                diagonal_exponents(odd)
                if pair:
                    gated_pair(pair - 1)
                if pair > 1:
                    add_square(pair - 2)
                if odd + 1 < SSD_H:
                    diagonal_exponents(odd + 1)
                weighted_scores(odd)
                if odd + 1 < SSD_H:
                    weighted_scores(odd + 1)
            gated_pair(XS_T - 1)
            for pair in range(XS_T - 2, XS_T):
                add_square(pair)
            for g in range(SSD_G):
                dve.wait_ge(sem("group_root"), g + 1)
                do(dve.reciprocal(rs_g[:, g, :], rs_g[:, g, :]))
                for k in range(4 * g, 4 * g + 4):
                    do(dve.scalar_tensor_tensor(zt[:], xbc[:, k, :], col("ssd_g", k), rs_g[:, g, :], ALU.mult, ALU.mult))
                    do.tell(split(ys_hi[:, k, :], ys_lo[:, k, :], zt[:]), "ys_split", k + 1)
            for n, first, last in ((0, 0, 2), (1, 2, 3)):
                dve.wait_ge(sem("latent_root"), n + 1)
                do(dve.reciprocal(rs_l[:, n, :], rs_l[:, n, :]))
                for k in range(first, last):
                    do.tell(dve.scalar_tensor_tensor(qa[:, k, :], qa[:, k, :], col("qa_g", k), rs_l[:, n, :], ALU.mult, ALU.mult),
                            "latents_scaled", k + 1)
            dve.wait_ge(sem("bank_free"), FREED["gates"] + 16)
            for m in range(8):
                dve.wait_ge(sem("tile_done"), 2 * (SLAB0["ssd"] + m) + 2)
                do.tell(dve.tensor_tensor(mix[:, m, :], mix[:, m, :], banks[2 + m % 2][:], ALU.mult), "bank_free_wide",
                        FREED["ssd"] + m + 1)
                do.tell(dve.tensor_copy(small[:, 2:3], small[:, 0:1]), "mix_made", m + 1)
            for k in range(3):
                do.tell(split(qn_hi[:, k, :], qn_lo[:, k, :], qa[:, k, :]), "qn_made", k + 1)
            dve.wait_ge(sem("rope_in"), 32)
            def unit_sums(n):
                dve.wait_ge(sem("unit_squared"), n + 1)
                do.tell(dve.tensor_reduce(stat[:, n % 2, 0, :], tsq[:], AX.X, ALU.add), "unit_summed", n + 1)

            unit_sums(0)
            for n in range(16):
                if n + 1 < 16:
                    unit_sums(n + 1)
                keys, tok = n // 8, n % 4
                tile, scale = tt(n)[:], stat[:, n % 2, 2, :]
                dve.wait_ge(sem("unit_root"), n + 1)
                do(dve.reciprocal(scale, stat[:, n % 2, 1, :]))
                do(dve.tensor_tensor(tile, tile, scale.unsqueeze(2).to_broadcast([P, HU, QK]), ALU.mult))
                do(dve.tensor_tensor(tile, tile, qk_g[:, keys, :].unsqueeze(1).to_broadcast([P, HU, QK]), ALU.mult))
                cos, sin = (rope[:, s, tok, :].unsqueeze(1).to_broadcast([P, HU, ROPE // 2]) for s in range(2))
                first, second = tile[:, :, NOPE:NOPE + ROPE // 2], tile[:, :, NOPE + ROPE // 2:QK]
                for part, src, f in ((0, first, cos), (1, second, sin), (2, first, sin), (3, second, cos)):
                    do(dve.tensor_tensor(trope[:, part, :, :], src, f, ALU.mult))
                do(dve.tensor_tensor(first, trope[:, 0, :, :], trope[:, 1, :, :], ALU.subtract))
                do.tell(dve.tensor_tensor(second, trope[:, 2, :, :], trope[:, 3, :, :], ALU.add), "heads_scaled", n + 1)

            def maxima(hd):
                for i, lo, hi, used in spans(1):
                    dve.wait_ge(sem("s3_done"), TOK * hd + i + 1)
                    top, bias = (mx[:, hd % 2, n, i:i + 1] for n in range(2))
                    do(dve.tensor_reduce(top, banks[i][:, 0:hi], AX.X, ALU.max))
                    do.tell(dve.tensor_scalar(bias, top, -QK ** -0.5, None, ALU.mult), "max_made", TOK * hd + i + 1)

            maxima(0)
            for step in range(QH + 2):
                if step < QH:
                    hd = step
                    for i, lo, hi, used in spans(1):
                        part, total = p3[hd % 2][:, used:used + hi], mx[:, hd % 2, 2, i:i + 1]
                        dve.wait_ge(sem("p3_made"), TOK * hd + i + 1)
                        do(dve.reciprocal(total, total))
                        do.tell(dve.tensor_scalar(part, part, total, None, ALU.mult), "p3_scaled", TOK * hd + i + 1)
                pair = step // 2 - 1 if step >= 2 and step % 2 else None
                if pair is not None:
                    dve.wait_ge(sem("pv3_done"), 2 * pair + 2)
                    do.tell(dve.tensor_copy(ao[:], banks[7][:]), "pair_taken", pair + 1)
                if step + 1 < QH:
                    maxima(step + 1)
                if pair is not None:
                    do.tell(split(att[:, 2 * pair, :], att[:, 2 * pair + 1, :], ao[:]), "att_made", pair + 1)
            for m in range(8):
                dve.wait_ge(sem("tile_done"), 2 * SLAB0["mla"] + m + 1)
                free(dve.tensor_tensor(mt[:], gm[:, m, :], banks[m % 2][:], ALU.mult), "mla", m)
                do(dve.tensor_tensor(mix[:, m, :], mix[:, m, :], mt[:], ALU.add))
                do.tell(split(mm_hi[:, m, :], mm_lo[:, m, :], mix[:, m, :]), "mm_made", m + 1)
            do.tell(dve.memset(mean[:], 1.0 / D), "mean_set", 4)
            add_to_x("wo", total=3)
            modulated(4, lambda k: col("g_ffn2", k))
            do.tell(dve.memset(fpad[:], 0.0), "fpad_zeroed", 1)
            for up, done in (("upa", 0), ("upb", 16)):
                with dve.Fori(0, SLABS[up] // 2) as i:
                    do.loop(i, 2 * (2 * TAPS_F - 1 + 2))
                    for slot in range(2):
                        for m in range(2):
                            dve.wait_ge(sem("bank_free"), 4 * i + FREED[up] + 2 * slot + m + 1)
                            tile = 2 * (2 * i + done + slot) + m
                            acc, pad = facc[:, m, :], fpad[:, m, :]
                            do(dve.tensor_scalar(acc, pad[:, 0:S], col("convf_w", TAPS_F * tile), col("convf_b", tile),
                                                 ALU.mult, ALU.add))
                            for tap in range(1, TAPS_F):
                                ins = dve.scalar_tensor_tensor(acc, pad[:, tap:tap + S], col("convf_w", TAPS_F * tile + tap),
                                                               acc, ALU.mult, ALU.add)
                                if m == 0 and tap == TAPS_F - 1:
                                    do.tell(ins, "fconv_done", 2 * i + done + slot + 1)
                                else:
                                    do(ins)
                        dve.wait_ge(sem("fgate_made"), 2 * i + done + slot + 1)
                        do(dve.tensor_tensor(fa[:], fgate[:], facc[:, 1, :], ALU.mult))
                        place = 2 * i + slot
                        do(dve.tensor_copy(a_hi[:, place, :], fa[:]))
                        do.tell(dve.tensor_tensor(a_lo[:, place, :], fa[:], a_hi[:, place, :].bitcast(f32), ALU.subtract),
                                "fa_made", 2 * i + done + slot + 1)
                do.end(SLABS[up] // 2)
                if up == "upa":
                    add_to_x("downa", wide=True)
            for m in range(KT):
                dve.wait_ge(sem("tile_done"), 2 * SLAB0["downb"] + m + 1)
                free(dve.tensor_tensor(x[:, m, :], banks[m % 2][:], x[:, m, :], ALU.add), "downb", m)
                do.tell(dve.tensor_copy(small[:, 2:3], small[:, 0:1]), "x_final", m + 1)

        @block.tensor
        def _(pe):
            n_sq = 0

            def three(out, w, a, start, stop):
                pe.matmul(out, w[0], a[0], start=start, stop=False)
                pe.matmul(out, w[0], a[1], start=False, stop=False)
                return pe.matmul(out, w[1], a[0], start=False, stop=stop)

            def weights(slot, tile, n=1):
                part = slice(P * tile, P * (tile + n))
                return w_hi[:, slot, part], w_lo[:, slot, part]

            def product(name, hi, lo, kt=KT, slots=(0, 1), stage=None, between=None):
                wide = name in WIDE
                bank0, which = (2, "bank_free_wide") if wide else (0, "bank_free")

                def turn(i, slots=slots):
                    for slot in slots:
                        pe.wait_ge(sem("w_split"), 2 * i + SLAB0[name] + slot + 1)
                        for m in range(1 if wide else 2):
                            t = slot if wide else 2 * slot + m
                            per = 2 if wide else 4
                            before = FREED[name] + t - 1
                            if not isinstance(i, int) or before > 0:
                                pe.wait_ge(sem(which), per * i + before)
                            for k in range(kt):
                                last = three(banks[bank0 + t % 2][:], weights(slot, (16 if wide else KT) * m + k),
                                             (hi[:, k, :], lo[:, k, :]), k == 0, k == kt - 1)
                            last.then_inc(sem("tile_done"), 2 if wide else 1)

                if stage is not None:
                    pe.wait_ge(sem("w_split"), SLAB0[name] + 1)
                    if FREED[name]:
                        pe.wait_ge(sem("bank_free"), FREED[name])
                    for k in range(KT):
                        pe.wait_ge(sem("h_ready"), KT * (stage - 1) + k + 1)
                        for m in range(2):
                            last = three(banks[m][:], weights(0, KT * m + k), (hi[:, k, :], lo[:, k, :]), k == 0, k == KT - 1)
                            if k == KT - 1:
                                last.then_inc(sem("tile_done"), 1)
                    turn(0, (1,))
                elif between is not None:
                    turn(0, (0,))
                    between()
                    turn(0, (1,))
                elif SLABS[name] == 2:
                    turn(0)
                if SLABS[name] > 2:
                    with pe.Fori(0 if stage is None and between is None else 1, SLABS[name] // 2) as i:
                        turn(i)

            def sum_squares(n, buf, bank=banks[7]):
                nonlocal n_sq
                for k in range(n):
                    pe.wait_ge(sem("sq_ready"), n_sq + 1)
                    pe.matmul(bank[:], mean[:], buf[:, n_sq % 2, :], start=k == 0, stop=k == n - 1)\
                      .then_inc(sem("sq_used"), 1)
                    n_sq += 1

            def total_square(n):
                pe.wait_ge(sem("total_ready"), n)
                pe.matmul(banks[7][:], mean[:], sq[:, 1, :], start=True, stop=True).then_inc(sem("total_used"), 1)

            def mod_sums(third):
                pe.wait_ge(sem("ada_used"), KT * (third + 1))
                for m in range(16):
                    last = pe.matmul(banks[4][:, m:m + 1], ada_sum[third][:, P * m:P * m + P], mean[:, 0:1], start=True, stop=True)
                last.then_inc(sem("mod_done"), 1)

            def row(n, count):
                return ident[0:count, n:n + 1].to_broadcast([count, P])

            pe.wait_ge(sem("set"), 1)
            sum_squares(KT, sq)
            mod_sums(0)
            product("u", h_hi, h_lo, stage=1)
            pe.wait_ge(sem("gate_w_split"), 1)
            for k in range(KT):
                last = three(banks[4][:], (gw_hi[:, k, :], gw_lo[:, k, :]), (h_hi[:, k, :], h_lo[:, k, :]), k == 0, k == KT - 1)
            last.then_inc(sem("gates_done"), 1)
            product("q", h_hi, h_lo)
            product("k", h_hi, h_lo)
            pe.wait_ge(sem("consts_in"), 16)
            pe.wait_ge(sem("gate_rows"), 1)
            for t in range(TOK):
                pe.transpose(banks[4][:, G1 * t:G1 * t + G1], rows[0:G1, 0, P * t:P * t + P], ident[0:G1, 0:G1])
            for t in range(TOK):
                last = pe.transpose(banks[2][:, G1 * t:G1 * t + G1], neg_m[0:G1, P * t:P * t + P], ident[0:G1, 0:G1])
            last.then_inc(sem("a_turned"), 1)
            for c in range(2):
                pe.wait_ge(sem("w_split"), SLAB0["v"] + c + 1)
                for m in range(2):
                    pe.wait_ge(sem("bank_free"), FREED["v"] + 2 * c + m - 1)
                    for half in range(2):
                        tok = slice(P * (2 * m + half), P * (2 * m + half + 1))
                        for k in range(KT):
                            last = three(banks[m][:, 256 * half:256 * half + 256], (h_hi[:, k, tok], h_lo[:, k, tok]),
                                         weights(c, 2 * k, 2), k == 0, k == KT - 1)
                    last.then_inc(sem("tile_done"), 1)
                if c == 0:
                    pe.wait_ge(sem("a_col_ready"), 1)
                    pe.wait_ge(sem("mean_set"), 1)
                    mod_sums(1)
                    pe.wait_ge(sem("pool_w_in"), 16)
                    for g in range(4):
                        pe.wait_ge(sem("pooled"), g + 1)
                        if g == 3:
                            pe.wait_ge(sem("y_ready"), 1)
                        pe.matmul(pool_banks[g][:], pool_w[:, g, :], mixed1[:, g, :], start=True, stop=True)\
                          .then_inc(sem("pool_done"), 1)
            def broadcast(n):
                r = 32 * (n % 2) + n // 2
                if n:
                    pe.wait_ge(sem("e1_made"), n)
                pe.matmul(banks[4][:], row(r, G1), neg_max[0:G1, :], start=True, stop=True).then_inc(sem("bc1_done"), 1)

            def head_scores(head):
                for j in range(TOK):
                    last = pe.matmul(banks[j][:], qk[:, 4 + head, P * j:P * j + P], qk[:, head, :], start=True, stop=True)
                last.then_inc(sem("s1_done"), 1)

            pe.wait_ge(sem("y_ready"), 4)
            broadcast(0)
            pe.wait_ge(sem("bank_free"), FREED["v"] + 4)
            pe.wait_ge(sem("floor_made"), 1)
            head_scores(0)
            for n in range(2 * H1):
                head, back = n // 2, n % 2
                if n + 1 < 2 * H1:
                    broadcast(n + 1)
                pe.wait_ge(sem("p1_made"), n + 1)
                if back and head + 1 < H1:
                    head_scores(head + 1)
                blocks = {j: (lo, used) for j, lo, hi, used in paired(back)}
                for t in range(TOK):
                    keys = range(t, TOK) if back else range(t + 1)
                    for j in keys:
                        first = blocks[j][1] + P * t - blocks[j][0]
                        last = pe.matmul(banks[6][:, t:t + 1], p1[:, back, first:first + P], ones[:, 0:1],
                                         start=j == keys[0], stop=j == keys[-1])
                last.then_inc(sem("den1_done"), 1)
                if n:
                    pe.wait_ge(sem("h1_taken"), n)
                order = sorted(paired(back), key=lambda block_row: block_row[1] - block_row[2])
                for nth, (j, lo, hi, used) in enumerate(order):
                    last = pe.matmul(banks[5][:, lo:hi], v1[:, j, DH * head:DH * head + DH], p1[:, back, used:used + hi - lo],
                                     start=nth == 0, stop=nth == TOK - 1)
                last.then_inc(sem("pv1_done"), 1)
                pe.wait_ge(sem("den1_inverted"), n + 1)
                if n:
                    pe.wait_ge(sem("h1_made"), n)
                for t in range(TOK):
                    last = pe.matmul(banks[7][:, P * t:P * t + P], den_col[:, back, t:t + 1].to_broadcast([P, P]), ident,
                                     start=True, stop=True)
                last.then_inc(sem("den1_spread"), 1)
            for head in range(H1 - 1):
                sum_squares(1, sq, head_banks[head])
            product("o", h_hi, h_lo, slots=(0,))
            sum_squares(1, sq, head_banks[H1 - 1])
            product("o", h_hi, h_lo, slots=(1,))
            pe.wait_ge(sem("y_ready"), 8)
            product("out", y_hi, y_lo)
            pe.wait_ge(sem("mean_set"), 2)
            mod_sums(2)
            total_square(1)
            for half in "ab":
                product("ff1" + half, h_hi, h_lo, stage=2 if half == "a" else None)
                pe.wait_ge(sem("a_ready"), 16 if half == "a" else 32)
                product("ff2" + half, a_hi, a_lo, 16)
            total_square(2)
            sum_squares(KT, sq)
            product("misc", h_hi, h_lo, stage=3)
            product("xbc", h_hi, h_lo)
            pe.wait_ge(sem("dt_rows"), 1)
            for t in range(TOK):
                tok = slice(P * t, P * t + P)
                pe.transpose(banks[4][:, 32 * t:32 * t + 32], drow[0:32, 3, tok], ident[0:32, 0:32])
                pe.transpose(banks[5][:, 32 * t:32 * t + 32], drow[0:32, 0, tok], ident[0:32, 0:32])
                last = pe.transpose(banks[6][:, P * t:P * t + P], mz[:, tok], ident)
            last.then_inc(sem("dt_turned"), 1)
            pe.wait_ge(sem("xbc_ready"), XS_T + BC_T)
            for n in range(TOK * 4):
                tok, quad = n // 4, n % 4
                if n >= 4:
                    pe.wait_ge(sem("xdt_made"), n - 3)
                for m in range(4):
                    last = pe.transpose(banks[n % 4][:, P * m:P * m + P], xbc[:, 4 * quad + m, P * tok:P * tok + P], ident)
                last.then_inc(sem("xs_turned"), 1)
            pe.wait_ge(sem("xdt_made"), TOK * 4)
            def running_sums(hd):
                bank = banks[4 + hd % 2]
                if hd >= 2:
                    pe.wait_ge(sem("e2_made"), hd - 1)
                pe.matmul(bank[:], row(hd, 32), acum[0:32, :], start=True, stop=True).then_inc(sem("bc2_done"), 1)

            def group_scores(g):
                if g:
                    pe.wait_ge(sem("sm_made"), g)
                for j, lo, hi, used in spans(0):
                    bank, first = score_place(j)
                    last = pe.matmul(banks[bank][:, first:first + hi - lo], xbc[:, XS_T + g, P * j:P * j + P],
                                     xbc[:, XS_T + SSD_G + g, lo:hi], start=True, stop=True)
                last.then_inc(sem("s2_done"), 1)

            def z_tile(pair):
                slab, m = SLAB0["z"] + pair // 2, pair % 2
                pe.wait_ge(sem("w_split"), slab + 1)
                if pair:
                    pe.wait_ge(sem("bank_free"), FREED["z"] + pair)
                for k in range(KT):
                    last = three(banks[0][:], weights(slab % 2, KT * m + k), (h_hi[:, k, :], h_lo[:, k, :]), k == 0, k == KT - 1)
                last.then_inc(sem("tile_done"), 1)

            group_scores(0)
            running_sums(0)
            for hd in range(SSD_H):
                pair = hd // 2
                if hd + 1 < SSD_H:
                    running_sums(hd + 1)
                if hd % 2:
                    z_tile(pair)
                    if hd % 8 == 7 and hd + 1 < SSD_H:
                        group_scores(hd // 8 + 1)
                pe.wait_ge(sem("p2_made"), hd + 1)
                if hd % 2 == 0 and pair >= 2:
                    pe.wait_ge(sem("ys_made"), pair - 1)
                out = banks[6 + pair % 2][64 * (hd % 2):64 * (hd % 2) + 64, :]
                for nth, (j, lo, hi, used) in enumerate(paired(0)):
                    last = pe.matmul(out[:, lo:hi], xdt[:, j, SSD_P * hd:SSD_P * hd + SSD_P], p2[:, hd % 2, used:used + hi - lo],
                                     start=nth == 0, stop=nth == TOK - 1)
                last.then_inc(sem("pv2_done"), 1)
            pe.wait_ge(sem("mean_set"), 3)

            def group_means(groups):
                for g in groups:
                    pe.wait_ge(sem("square_added"), 3 * (g + 1))
                    pe.matmul(group_banks[g][:], mean[:], group_total(g), start=True, stop=True).then_inc(sem("group_mean"), 1)

            def last_means():
                group_means([SSD_G - 1])
                pe.wait_ge(sem("latent_squares"), 3)
                for n, tiles in enumerate(((0, 1), (2,))):
                    for k in tiles:
                        last = pe.matmul(latent_banks[n][:], mean[:], sq_l[:, k, :], start=k == tiles[0], stop=k == tiles[-1])
                    last.then_inc(sem("latent_mean"), 1)

            group_means(range(SSD_G - 1))
            pe.wait_ge(sem("bank_free"), FREED["gates"])
            product("gates", h_hi, h_lo, between=last_means)
            pe.wait_ge(sem("ys_split"), XS_T)
            product("ssd", ys_hi, ys_lo, 16)
            pe.wait_ge(sem("qn_made"), 3)
            pe.wait_ge(sem("bank_free"), FREED["gates"] + 16)

            def unit(n):
                keys, tok, slot = n // 8, slice(P * (n % 4), P * (n % 4) + P), n // 4 % 2
                pe.wait_ge(sem("w_split"), SLAB0["uq"] + n // 4 + 1)
                if n >= 2:
                    pe.wait_ge(sem("unit_squared"), n - 1)
                width = S if keys else 4 * QK
                for half in range(2):
                    for k in range(1 if keys else 2):
                        first = (0 if keys else 2 * width * k) + width * half
                        kk = 2 if keys else k
                        last = three(banks[2 * (n % 2) + half][:, 0:width], (qn_hi[:, kk, tok], qn_lo[:, kk, tok]),
                                     (w_hi[:, slot, first:first + width], w_lo[:, slot, first:first + width]),
                                     k == 0, bool(keys) or k == 1)
                last.then_inc(sem("tile_done" if n % 2 else "unit_done"), 1)

            def turn_heads(n):
                pe.wait_ge(sem("heads_scaled"), n + 1)
                if n >= 2:
                    pe.wait_ge(sem("heads_ready"), n - 1)
                for hh in range(HU):
                    last = pe.transpose(banks[4 + 2 * (n % 2) + hh // 4][0:QK, P * (hh % 4):P * (hh % 4) + P],
                                        tt(n)[:, hh, :], ident)
                last.then_inc(sem("heads_turned"), 1)

            for n in range(3):
                unit(n)
            for n in range(16):
                if n + 3 < 16:
                    unit(n + 3)
                turn_heads(n)
            pe.wait_ge(sem("heads_ready"), 16)

            def scores(hd):
                for i, lo, hi, used in spans(1):
                    if hd:
                        pe.wait_ge(sem("p3_made"), TOK * (hd - 1) + i + 1)
                    pe.matmul(banks[i][:, 0:hi], q2[0:QK, hd, P * i:P * i + P], k2[0:QK, hd, 0:hi], start=True, stop=False)
                    pe.matmul(banks[i][:, P * i:hi], ident16, causal16, start=False, stop=True)\
                      .then_inc(sem("s3_done"), 1)

            def turn_probabilities(hd):
                if hd:
                    pe.wait_ge(sem("pt_made"), hd)
                for i, lo, hi, used in spans(1):
                    pe.wait_ge(sem("p3_scaled"), TOK * hd + i + 1)
                    for j in range(i + 1):
                        bank, first = ((4, 0), (5, 0), (6, 0), (5, 384))[j]
                        last = pe.transpose(banks[bank][:, first + P * (i - j):first + P * (i - j) + P],
                                            p3[hd % 2][:, used + P * j:used + P * j + P], ident)
                last.then_inc(sem("p3_turned"), 1)

            def weighted_values(hd):
                pair = hd // 2
                pe.wait_ge(sem("pt_made"), hd + 1)
                if hd % 2 == 0 and pair:
                    pe.wait_ge(sem("pair_taken"), pair)
                out = banks[7][64 * (hd % 2):64 * (hd % 2) + 64, :]
                for j, lo, hi, used in spans(0):
                    last = pe.matmul(out[:, lo:hi], v2[:, j, VD * hd:VD * hd + VD], pt[hd % 2][:, used:used + hi - lo],
                                     start=j == 0, stop=j == TOK - 1)
                last.then_inc(sem("pv3_done"), 1)

            pe.wait_ge(sem("mask_made"), 1)
            for step in range(QH + 2):
                if step < QH:
                    scores(step)
                if 1 <= step <= QH:
                    turn_probabilities(step - 1)
                if step >= 2:
                    weighted_values(step - 2)
            pe.wait_ge(sem("att_made"), 8)
            product("mla", att[:, 0:16:2, :], att[:, 1:16:2, :])
            pe.wait_ge(sem("mm_made"), 8)
            product("wo", mm_hi, mm_lo)
            pe.wait_ge(sem("mean_set"), 4)
            total_square(3)
            product("upa", h_hi, h_lo, stage=4)
            pe.wait_ge(sem("fa_made"), 16)
            product("downa", a_hi, a_lo, 16)
            product("upb", h_hi, h_lo)
            pe.wait_ge(sem("fa_made"), UP_T)
            product("downb", a_hi, a_lo, UP_T - 16)


def kernel(**inputs):
    import concourse.bacc as bacc
    from concourse.bass_utils import run_bass_kernel_spmd

    f = {name: np.asarray(a) for name, a in inputs.items()}
    one = {name: (a[0] if name not in ("x", "c", "g_final") else a) for name, a in f.items()}

    def pairs(w):
        n = w.shape[1] // 256
        kt = w.shape[0] // P
        out = np.zeros((n, P, 2, KT, P), w.dtype)
        out[:, :, :, :kt] = w.reshape(kt, P, n, 2, P).transpose(2, 1, 3, 0, 4)
        return out.reshape(n, P, SLAB)

    def wides(w):
        return w.reshape(16, P, KT, P).transpose(2, 1, 0, 3).reshape(KT, P, SLAB)

    def tiles(a):
        return a.reshape(-1, P).T

    w_in, w_in2 = one["w_in"], one["w_in_2"]
    dm = H1 * DH
    gate0 = 4 * dm
    u0 = gate0 + 16
    by_token = w_in[:, 2 * dm:3 * dm].reshape(KT, P, 2, 256).transpose(2, 1, 0, 3).reshape(2, P, SLAB)
    xbc0, dt0 = 2048, 5120
    qa0, kr0 = dt0 + 32, dt0 + 32 + 384
    misc = np.zeros((D, 4 * P), w_in2.dtype)
    misc[:, 0:384] = w_in2[:, qa0:qa0 + 384]
    misc[:, 384:416] = w_in2[:, dt0:dt0 + 32]
    misc[:, 448:480] = w_in2[:, kr0:kr0 + 32]
    up = one["w_up_2"].reshape(D, 2, UP_T, P).transpose(0, 2, 1, 3).reshape(D, 2 * UP_T * P)
    down, ff1, ff2 = one["w_down_2"], one["w_ff1"], one["w_ff2"]
    uq = np.zeros((2, P, SLAB), w_in.dtype)
    uq[:, :, 0:1536] = one["w_uq_2"].reshape(2, P, 2, 768).transpose(2, 1, 0, 3).reshape(2, P, 1536)
    ukv = np.zeros((2, P, SLAB), w_in.dtype)
    ukv[:, :, 0:1024] = one["w_ukv_2"].reshape(P, 2, 1024).transpose(1, 0, 2)
    parts = {"q": pairs(w_in[:, 0:dm]), "k": pairs(w_in[:, dm:2 * dm]), "v": by_token, "o": pairs(w_in[:, 3 * dm:4 * dm]),
             "u": pairs(w_in[:, u0:]), "out": pairs(one["w_out"]),
             "ff1a": pairs(ff1[:, 0:2048]), "ff1b": pairs(ff1[:, 2048:]), "ff2a": wides(ff2[0:2048]), "ff2b": wides(ff2[2048:]),
             "misc": pairs(misc), "xbc": pairs(w_in2[:, xbc0:dt0]), "z": pairs(w_in2[:, 0:2048]), "gates": pairs(w_in2[:, kr0 + 32:]),
             "ssd": wides(one["w_ssd_proj_2"]), "uq": uq, "ukv": ukv, "mla": pairs(one["w_mla_proj_2"]), "wo": pairs(one["w_o_2"]),
             "upa": pairs(up[:, 0:16 * 256]), "upb": pairs(up[:, 16 * 256:]), "downa": wides(down[0:2048]), "downb": pairs(down[2048:])}
    slabs = np.concatenate([parts[name] for name, _ in PHASES])
    gate_w = np.zeros((P, KT, P), w_in.dtype)
    gate_bias = np.zeros((P, 1), w_in.dtype)
    for d in range(2):
        for g, name in enumerate(("b_igate", "b_fgate")):
            first = 64 * g + 32 * d
            c0 = gate0 + 8 * d + 4 * g
            gate_w[:, :, first:first + H1] = w_in[:, c0:c0 + H1].reshape(KT, P, H1).transpose(1, 0, 2)
            gate_bias[first:first + H1, 0] = one[name][d]

    def rows32(a):
        out = np.zeros((P, 1), a.dtype)
        out[0:32, 0] = a
        return out

    convf_w = one["conv_ffn_w_2"].reshape(TAPS_F, 2, UP_T, P).transpose(3, 2, 1, 0).reshape(P, 2 * UP_T * TAPS_F)
    convf_b = one["conv_ffn_b_2"].reshape(2, UP_T, P).transpose(2, 1, 0).reshape(P, 2 * UP_T)
    by_name = {"c": tiles(f["c"][0]), "b_ada": tiles(one["b_ada"]), "g_mix": tiles(one["g_mix"]), "gate_bias": gate_bias,
               "g_head": tiles(one["g_head"]), "pool_scale": tiles(one["pool_scale"]), "g_ffn": tiles(one["g_ffn"]),
               "g_final": tiles(f["g_final"]), "g_mix2": tiles(one["norm_mix_g_2"]),
               "conv_w": one["conv_ssd_w_2"].reshape(TAPS, 24, P).transpose(2, 1, 0).reshape(P, 96),
               "conv_b": tiles(one["conv_ssd_b_2"]), "dt_bias": rows32(one["dt_bias_2"]), "a_log": rows32(one["a_log_2"]),
               "d_skip": tiles(np.repeat(one["d_skip_2"], SSD_P)), "ssd_g": tiles(one["ssd_norm_g_2"]),
               "qa_g": tiles(one["q_a_norm_g_2"]), "kva_g": tiles(one["kv_a_norm_g_2"]), "gate_b": tiles(one["gate_b_2"]),
               "g_ffn2": tiles(one["norm_ffn_g_2"]), "convf_w": convf_w, "convf_b": convf_b}
    cols = np.concatenate([by_name[name] for name in COLS], axis=1)
    ada = one["w_ada"].reshape(KT, P, 3, 2048).transpose(2, 0, 1, 3).reshape(3 * KT, P, 2048)
    x_t = f["x"][0].T.reshape(KT, P, S).transpose(1, 0, 2)
    at = np.arange(P)
    consts = np.stack([np.eye(P), at[None, :] >= at[:, None], at[None, :] <= at[:, None],
                       np.where(at[None, :] <= at[:, None], 0.0, -1e30)], 1).astype(np.float32)
    t = np.arange(S)
    sizes = [np.clip(t + n // 2, 0, S) - np.clip(t - n // 2, 0, S) for n in WINDOWS]
    inv = np.broadcast_to(1.0 / np.array(sizes, np.float32), (P, 4, S))
    freq = (1.0 / (10000.0 ** (np.arange(0, ROPE, 2, dtype=np.float32) / np.float32(ROPE)))).astype(np.float32)
    angle = t.astype(np.float32)[:, None] * freq[None, :]
    rope = np.stack([np.cos(angle), np.sin(angle)]).reshape(2, TOK, P, ROPE // 2).transpose(2, 0, 1, 3)
    qk_g = np.broadcast_to(np.stack([one["q_norm_g_2"], one["k_norm_g_2"]]), (P, 2, QK))
    pool_w = one["w_pool"].transpose(1, 0, 2)
    arrays = {"x_in": x_t, "slabs": slabs, "ada": ada, "cols": cols, "gate_w": gate_w, "pool_w": pool_w, "consts": consts,
              "inv": inv, "rope": rope, "qk_g": qk_g}
    arrays = {name: np.ascontiguousarray(a) for name, a in arrays.items()}
    nc = bacc.Bacc("TRN2", target_bir_lowering=False, num_devices=1)
    drams = [nc.dram_tensor(name, a.shape, mybir.dt.from_np(a.dtype), kind="ExternalInput").ap() for name, a in arrays.items()]
    out = nc.dram_tensor("out", (P, KT, S), mybir.dt.float32, kind="ExternalOutput").ap()
    build(nc, *drams, out)
    got = run_bass_kernel_spmd(nc, [arrays], core_ids=[0]).results[0]["out"]
    return np.ascontiguousarray(np.asarray(got).transpose(2, 1, 0).reshape(1, S, D))
```
